# Optimizing a Trainium2 kernel written in Bass

```python
import jax, jax.numpy as jnp
from jax import lax
import numpy as np

D_MODEL = 1024
BATCH = 1
SEQ = 512
DEPTH = 1

CHUNK = 64
HEAD_DIM = 64
SWA_Q_HEADS = 8
SWA_KV_HEADS = 2
SWA_WINDOW = 128
WINDOW_CHUNKS = SWA_WINDOW // CHUNK
SWA_BLOCK = 128
FOX_HEADS = 4
SB_HEADS = 4
ATTN_BLOCK = 128
MIX_HEADS = SWA_Q_HEADS + FOX_HEADS + SB_HEADS
MIX_WIDTH = MIX_HEADS * HEAD_DIM
A_Q = SWA_Q_HEADS * HEAD_DIM
A_KV = SWA_KV_HEADS * HEAD_DIM
B_W = FOX_HEADS * HEAD_DIM
C_W = SB_HEADS * HEAD_DIM
IN_SPLITS = (A_Q, A_KV, A_KV, B_W, B_W, B_W, FOX_HEADS, C_W, C_W, C_W)
IN_WIDTH = A_Q + 2 * A_KV + 3 * B_W + FOX_HEADS + 3 * C_W
N_EXPERTS = 32
TOP_K = 4
D_EXPERT = D_MODEL
SWIGLU_LIMIT = 7.0
SWIGLU_ALPHA = 1.702
EXPERT_BLOCK = 256
EPS = 1e-5

kernel_name = "hybrid_chunk_causal_swa_fox_stickbreak_moe"

def rmsnorm(x, gain):
    xf = x.astype(jnp.float32)
    y = xf * lax.rsqrt(jnp.mean(xf * xf, axis=-1, keepdims=True) + EPS)
    return (y * gain.astype(jnp.float32)).astype(x.dtype)

def modulate(h, shift, scale):
    return h * (1 + scale[:, None, :]) + shift[:, None, :]

def swa_sink_attention(q, k, v, sinks):
    b, s_len = q.shape[:2]
    nb = s_len // SWA_BLOCK
    grp = SWA_Q_HEADS // SWA_KV_HEADS
    qb = q.reshape(b, nb, SWA_BLOCK, SWA_KV_HEADS, grp, HEAD_DIM)

    def band(t):
        cur = t.reshape(b, nb, SWA_BLOCK, SWA_KV_HEADS, HEAD_DIM)
        prev = jnp.pad(cur, ((0, 0), (1, 0), (0, 0), (0, 0), (0, 0)))[:, :-1]
        return jnp.concatenate([prev, cur], axis=2)

    kband, vband = band(k), band(v)
    scores = jnp.einsum('bnqhgd,bnkhd->bnhgqk', qb, kband).astype(jnp.float32) * (HEAD_DIM ** -0.5)
    i = jnp.arange(SWA_BLOCK)[:, None]
    j = jnp.arange(2 * SWA_BLOCK)[None, :]
    rel_k = j - SWA_BLOCK
    q_chunk = i // CHUNK
    k_chunk = rel_k // CHUNK
    in_band = (k_chunk <= q_chunk) & (k_chunk > q_chunk - WINDOW_CHUNKS)
    blk_idx = jnp.arange(nb)[:, None, None]
    valid = in_band[None] & ((blk_idx > 0) | (j[None] >= SWA_BLOCK))
    dist = jnp.abs(i - rel_k).astype(jnp.float32)
    slopes = jnp.exp2(-8.0 * jnp.arange(1, SWA_Q_HEADS + 1, dtype=jnp.float32) / SWA_Q_HEADS)
    slopes = slopes.reshape(SWA_KV_HEADS, grp)[:, :, None, None]
    scores = scores - slopes * dist
    scores = jnp.where(valid[None, :, None, None], scores, -jnp.inf)
    sink = sinks.astype(jnp.float32).reshape(SWA_KV_HEADS, grp)[None, None, :, :, None, None]
    sink = jnp.broadcast_to(sink, scores.shape[:-1] + (1,))
    probs = jax.nn.softmax(jnp.concatenate([scores, sink], axis=-1), axis=-1)[..., :-1]
    out = jnp.einsum('bnhgqk,bnkhd->bnqhgd', probs.astype(v.dtype), vband)
    return out.reshape(b, s_len, A_Q)

def forgetting_attention(q, k, v, f_logit, f_bias):
    b, s_len, h, d = q.shape
    nb = s_len // ATTN_BLOCK
    log_f = jax.nn.log_sigmoid(f_logit.astype(jnp.float32) + f_bias.astype(jnp.float32))
    cum_f = jnp.cumsum(log_f, axis=1).transpose(0, 2, 1)
    q_blocks = q.reshape(b, nb, ATTN_BLOCK, h, d).transpose(1, 0, 2, 3, 4)
    f_blocks = cum_f.reshape(b, h, nb, ATTN_BLOCK).transpose(2, 0, 1, 3)
    kpos = jnp.arange(s_len)

    def one_block(args):
        qb, fq, n = args
        qpos = n * ATTN_BLOCK + jnp.arange(ATTN_BLOCK)
        sc = jnp.einsum('bqhd,bkhd->bhqk', qb, k).astype(jnp.float32) * (d ** -0.5)
        sc = sc + fq[..., :, None] - cum_f[:, :, None, :]
        sc = jnp.where(kpos[None, :] <= qpos[:, None], sc, -jnp.inf)
        p = jax.nn.softmax(sc, axis=-1)
        return jnp.einsum('bhqk,bkhd->bqhd', p.astype(v.dtype), v)

    out = lax.map(one_block, (q_blocks, f_blocks, jnp.arange(nb)))
    return out.transpose(1, 0, 2, 3, 4).reshape(b, s_len, h * d)

def stick_breaking_attention(q, k, v):
    b, s_len, h, d = q.shape
    nb = s_len // ATTN_BLOCK
    q_blocks = q.reshape(b, nb, ATTN_BLOCK, h, d).transpose(1, 0, 2, 3, 4)
    kpos = jnp.arange(s_len)

    def one_block(args):
        qb, n = args
        qpos = n * ATTN_BLOCK + jnp.arange(ATTN_BLOCK)
        z = jnp.einsum('bqhd,bkhd->bhqk', qb, k).astype(jnp.float32) * (d ** -0.5)
        strict = kpos[None, :] < qpos[:, None]
        log_beta = jax.nn.log_sigmoid(z)
        log_stay = jnp.where(strict, jax.nn.log_sigmoid(-z), 0.0)
        after = lax.cumsum(log_stay, axis=3, reverse=True) - log_stay
        a = jnp.where(strict, jnp.exp(log_beta + after), 0.0)
        return jnp.einsum('bhqk,bkhd->bqhd', a.astype(v.dtype), v)

    out = lax.map(one_block, (q_blocks, jnp.arange(nb)))
    return out.transpose(1, 0, 2, 3, 4).reshape(b, s_len, h * d)

def hybrid_mixer(h, w_in, sinks, f_bias, out_gain, w_out):
    b, s_len, _ = h.shape
    proj = h @ w_in
    offsets = [int(o) for o in np.cumsum(IN_SPLITS)[:-1]]
    qa, ka, va, qf, kf, vf, fl, qs, ks, vs = jnp.split(proj, offsets, axis=-1)
    heads = lambda t, n: t.reshape(b, s_len, n, HEAD_DIM)
    oa = swa_sink_attention(heads(qa, SWA_Q_HEADS), heads(ka, SWA_KV_HEADS), heads(va, SWA_KV_HEADS), sinks)
    ob = forgetting_attention(heads(qf, FOX_HEADS), heads(kf, FOX_HEADS), heads(vf, FOX_HEADS), fl, f_bias)
    oc = stick_breaking_attention(heads(qs, SB_HEADS), heads(ks, SB_HEADS), heads(vs, SB_HEADS))
    o = jnp.concatenate([oa, ob, oc], axis=-1).reshape(b, s_len, MIX_HEADS, HEAD_DIM)
    of = o.astype(jnp.float32)
    of = of * lax.rsqrt(jnp.mean(of * of, axis=-1, keepdims=True) + EPS)
    o = (of.reshape(b, s_len, MIX_WIDTH) * out_gain.astype(jnp.float32)).astype(h.dtype)
    return o @ w_out

def moe_ffn(h, router_w, router_b, w_gu, b_gu, w_dn, b_dn):
    b, s_len, dm = h.shape
    n_tok = b * s_len
    xt = h.reshape(n_tok, dm)
    logits = (xt @ router_w + router_b).astype(jnp.float32)
    top_val, top_idx = lax.top_k(logits, TOP_K)
    gates = jax.nn.softmax(top_val, axis=-1)
    n_assign = n_tok * TOP_K
    flat_e = top_idx.reshape(-1).astype(jnp.int32)
    flat_tok = jnp.repeat(jnp.arange(n_tok, dtype=jnp.int32), TOP_K)
    flat_g = gates.reshape(-1)
    order = jnp.argsort(flat_e)
    se, stok, sg = flat_e[order], flat_tok[order], flat_g[order]
    counts = jax.ops.segment_sum(jnp.ones_like(flat_e), flat_e, num_segments=N_EXPERTS)
    padded = ((counts + EXPERT_BLOCK - 1) // EXPERT_BLOCK) * EXPERT_BLOCK
    start = jnp.cumsum(counts) - counts
    pend = jnp.cumsum(padded)
    pstart = pend - padded
    dest = pstart[se] + (jnp.arange(n_assign, dtype=jnp.int32) - start[se])
    n_slots = ((n_assign + EXPERT_BLOCK - 1) // EXPERT_BLOCK + N_EXPERTS) * EXPERT_BLOCK
    n_blocks = n_slots // EXPERT_BLOCK
    slot_tok = jnp.zeros((n_slots,), jnp.int32).at[dest].set(stok)
    slot_g = jnp.zeros((n_slots,), flat_g.dtype).at[dest].set(sg)
    block_start = jnp.arange(n_blocks, dtype=jnp.int32) * EXPERT_BLOCK
    block_e = jnp.clip(jnp.searchsorted(pend, block_start, side='right'), 0, N_EXPERTS - 1)

    def expert_block(args):
        tok, g, e = args
        xb = xt[tok]
        gu = xb @ w_gu[e] + b_gu[e]
        x_glu = jnp.minimum(gu[:, 0::2], SWIGLU_LIMIT)
        x_lin = jnp.clip(gu[:, 1::2], -SWIGLU_LIMIT, SWIGLU_LIMIT)
        act = x_glu * jax.nn.sigmoid(SWIGLU_ALPHA * x_glu) * (x_lin + 1)
        y = act @ w_dn[e] + b_dn[e]
        return y * g[:, None].astype(y.dtype)

    ys = lax.map(expert_block, (slot_tok.reshape(n_blocks, EXPERT_BLOCK),
                                slot_g.reshape(n_blocks, EXPERT_BLOCK), block_e))
    out = jax.ops.segment_sum(ys.reshape(n_slots, dm), slot_tok, num_segments=n_tok)
    return out.reshape(b, s_len, dm).astype(h.dtype)

def setup_inputs(seed: int = 0) -> dict:
    key = jax.random.key(seed)
    ks = jax.random.split(key, 20)
    nrm = lambda k, shape, s: jax.random.normal(k, shape, jnp.float32) * s
    d = D_MODEL
    return {
        "x": nrm(ks[0], (BATCH, SEQ, d), 1.0),
        "c": nrm(ks[1], (BATCH, d), 1.0),
        "norm1_gain": 1.0 + nrm(ks[2], (DEPTH, d), 0.05),
        "norm2_gain": 1.0 + nrm(ks[3], (DEPTH, d), 0.05),
        "ada_w": nrm(ks[4], (DEPTH, d, 6 * d), 0.5 * d ** -0.5),
        "ada_b": nrm(ks[5], (DEPTH, 6 * d), 0.02),
        "w_in": nrm(ks[6], (DEPTH, d, IN_WIDTH), d ** -0.5),
        "attn_sinks": nrm(ks[7], (DEPTH, SWA_Q_HEADS), 1.0),
        "forget_bias": 1.0 + nrm(ks[8], (DEPTH, FOX_HEADS), 0.5),
        "mix_out_gain": 1.0 + nrm(ks[9], (DEPTH, MIX_WIDTH), 0.05),
        "w_out": nrm(ks[10], (DEPTH, MIX_WIDTH, d), MIX_WIDTH ** -0.5),
        "router_w": nrm(ks[11], (DEPTH, d, N_EXPERTS), d ** -0.5),
        "router_b": nrm(ks[12], (DEPTH, N_EXPERTS), 0.01),
        "expert_w_gate_up": nrm(ks[13], (DEPTH, N_EXPERTS, d, 2 * D_EXPERT), d ** -0.5),
        "expert_b_gate_up": nrm(ks[14], (DEPTH, N_EXPERTS, 2 * D_EXPERT), 0.02),
        "expert_w_down": nrm(ks[15], (DEPTH, N_EXPERTS, D_EXPERT, d), D_EXPERT ** -0.5),
        "expert_b_down": nrm(ks[16], (DEPTH, N_EXPERTS, d), 0.02),
        "final_gain": 1.0 + nrm(ks[17], (d,), 0.05),
    }

def reference(x, c, norm1_gain, norm2_gain, ada_w, ada_b, w_in, attn_sinks, forget_bias,
              mix_out_gain, w_out, router_w, router_b, expert_w_gate_up, expert_b_gate_up,
              expert_w_down, expert_b_down, final_gain):
    c_act = jax.nn.silu(c)
    for l in range(DEPTH):
        mod = c_act @ ada_w[l] + ada_b[l]
        shift1, scale1, gate1, shift2, scale2, gate2 = jnp.split(mod, 6, axis=-1)
        h = modulate(rmsnorm(x, norm1_gain[l]), shift1, scale1)
        x = x + gate1[:, None, :] * hybrid_mixer(h, w_in[l], attn_sinks[l], forget_bias[l],
                                                 mix_out_gain[l], w_out[l])
        h = modulate(rmsnorm(x, norm2_gain[l]), shift2, scale2)
        x = x + gate2[:, None, :] * moe_ffn(h, router_w[l], router_b[l], expert_w_gate_up[l],
                                            expert_b_gate_up[l], expert_w_down[l], expert_b_down[l])
    return rmsnorm(x, final_gain)


_drawn_inputs = setup_inputs


def setup_inputs(seed=0):
    import zlib

    import numpy as np

    out = dict(_drawn_inputs(seed))
    spreads = {}
    factors = {'attn_sinks': 64.0,
     'mix_out_gain': 2.738,
     'router_b': 12.698,
     'expert_b_gate_up': 8.0,
     'expert_b_down': 21.518}
    for name, (base, spread) in spreads.items():
        noise = np.random.default_rng([zlib.crc32(name.encode()), seed]).standard_normal(out[name].shape)
        drawn = base * np.exp(spread * noise) if base else spread * noise
        out[name] = __import__('jax').numpy.asarray(drawn.astype(out[name].dtype))
    for name, factor in factors.items():
        out[name] = (out[name] * factor).astype(out[name].dtype)
    return out
```

```python
from contextlib import ExitStack

import concourse.bass as bass
from concourse import mybir

F32 = mybir.dt.float32
F32R = mybir.dt.float32r
I32 = mybir.dt.int32
U32 = mybir.dt.uint32
ALU = mybir.AluOpType
ACT = mybir.ActivationFunctionType
AX = mybir.AxisListType

P = 128
SEQ, D = 512, 1024
NT, NK = SEQ // P, D // P
HD = 64
CW = 512
SWA_Q, SWA_KV, FOX, SB = 8, 2, 4, 4
HEADS = SWA_Q + FOX + SB
NE, TOPK = 32, 4
MAX_PASSES = NE + (SEQ * TOPK - NE) // P
NP_TAB = MAX_PASSES + 1
LIMIT, ALPHA, EPS = 7.0, 1.702, 1e-5
NEG = -1e30
QSCALE = HD ** -0.5
SLOTS = 6
KQ = 2
SPLITS = 4
GU_CHUNKS, DN_CHUNKS = 2 * D // CW, D // CW
CHUNKS = GU_CHUNKS + DN_CHUNKS
UPC = NK // KQ
UNITS = CHUNKS * UPC
USEMS = 6
UTURNS = UNITS // USEMS

C_QA, C_KA, C_VA = 0, 512, 640
C_QF, C_KF, C_VF, C_FL = 768, 1024, 1280, 1536
C_QS, C_KS, C_VS = 1540, 1796, 2052
KB = 1024


def build_program(nc, x, c, norm1_gain, norm2_gain, ada_w, ada_b, w_in, attn_sinks, forget_bias,
                  mix_out_gain, w_out, router_w, router_b, w_gu, b_gu, w_dn, b_dn, final_gain, out):
    ctx = ExitStack()
    with ctx:
        base = (nc.sbuf_base + 31) // 32 * 32

        def at(name, shape, dt, offset):
            return nc.alloc_sbuf_tensor_at(name, shape, dt, offset=base + offset)

        ring = at("ring", [P, SLOTS, NK, CW], F32, 0)
        cursor = [96 * KB]

        def small(name, shape, dt):
            size = 4
            for s in shape[1:]:
                size *= s
            t = at(name, shape, dt, cursor[0])
            cursor[0] += (size + 31) // 32 * 32
            return t

        ident = small("ident", [P, P], F32)
        ones = small("ones", [P, P], F32)
        slot_iota = small("slot_iota", [P, P], F32)
        expert_of_row = small("expert_of_row", [P, P], F32)
        dest = small("dest", [P, NT, NE], F32)
        etab = small("etab", [P, NP_TAB], F32)
        etab_i = small("etab_i", [P, NP_TAB], I32)
        iota_p = small("iota_p", [P, NP_TAB], F32)
        iota_e = small("iota_e", [P, NE], F32)
        ybase = small("ybase", [P, NP_TAB], F32)
        ybase_i = small("ybase_i", [P, NP_TAB], I32)
        passes_i = small("passes_i", [P, 1], I32)
        my_slot = small("my_slot", [P, NT, TOPK], F32)
        my_slot_i = small("my_slot_i", [P, NT, TOPK], I32)
        gate = small("gate", [P, NT, TOPK], F32)
        ssq = small("ssq", [P, 8], F32)
        rstd = small("rstd", [P, 8], F32)
        neg_sink = small("neg_sink", [P, 4], F32)
        assert cursor[0] <= 101 * KB, cursor[0]
        R0 = 101 * KB
        R1, R2, R3, R4 = R0 + 16 * KB, R0 + 32 * KB, R0 + 48 * KB, R0 + 86 * KB
        x_in = at("x_in", [P, NT, D], F32, R0)
        o = at("o", [P, NT, D], F32, R0)
        h2_hi = at("h2_hi", [P, NT, D], F32R, R0)
        mod1 = at("mod1", [P, 2 * D], F32, R1)
        cumf_row = at("cumf_row", [P, FOX, SEQ], F32, R1)
        stick = at("stick", [P, SEQ], F32, R1 + 8 * KB)
        alibi = at("alibi", [P, 4, P], F32, R1 + 10 * KB)
        c_rep = at("c_rep", [P, NK, P], F32, R1 + 12 * KB)
        h2_lo = at("h2_lo", [P, NT, D], F32R, R1)
        hT = at("hT", [P, NK, SEQ], F32, R2)
        oT = at("oT", [P, NK, SEQ], F32, R2)
        h2T = at("h2T", [P, NK, SEQ], F32, R2)
        qaT = at("qaT", [P, 4, SEQ], F32, R3)
        kaT = at("kaT", [P, SEQ], F32, R3 + 8 * KB)
        qfT = at("qfT", [P, 2, SEQ], F32, R3 + 10 * KB)
        kfT = at("kfT", [P, 2, SEQ], F32, R3 + 14 * KB)
        qsT = at("qsT", [P, 2, SEQ], F32, R3 + 18 * KB)
        ksT = at("ksT", [P, 2, SEQ], F32, R3 + 22 * KB)
        va = at("va", [P, NT, 2 * HD], F32, R3 + 26 * KB)
        va_mid = at("va_mid", [P, 3, 2 * HD], F32, R3 + 28 * KB)
        vf = at("vf", [P, NT, 4 * HD], F32, R3 + 29 * KB + 512)
        vs = at("vs", [P, NT, 4 * HD], F32, R3 + 33 * KB + 512)
        mod2 = at("mod2", [P, 4 * D], F32, R3)
        resid = at("resid", [P, NT, D], F32, R3 + 16 * KB)
        head_gain = at("head_gain", [P, NK], F32, R3 + 37 * KB + 512)
        gain = at("gain", [P, D], F32, R4)
        h_row = at("h_row", [P, 2, D], F32, R4 + 4 * KB)
        c_col = at("c_col", [P, 4, NK], F32, R4 + 12 * KB)
        score = at("score", [P, 2, SEQ], F32, R4)
        soft = at("soft", [P, 2, SEQ], F32, R4 + 4 * KB)
        prob = at("prob", [P, 2, SEQ], F32, R4 + 8 * KB)
        probT = at("probT", [P, 2, SEQ], F32, R4 + 12 * KB)
        tri_incl = at("tri_incl", [P, SEQ], F32, R4 + 16 * KB)
        tri_strict = at("tri_strict", [P, P], F32, R4 + 18 * KB)
        low_strict = at("low_strict", [P, P], F32, R4 + 18 * KB + 512)
        causal_add = at("causal_add", [P, P], F32, R4 + 19 * KB)
        strict_add = at("strict_add", [P, P], F32, R4 + 19 * KB + 512)
        tail = R4 + 20 * KB
        flog = at("flog", [P, NT, FOX], F32, tail)
        fwork = at("fwork", [P, NT, FOX], F32, tail + 64)
        fbias = at("fbias", [P, FOX], F32, tail + 128)
        cumf_col = at("cumf_col", [P, NT, FOX], F32, tail + 160)
        mrow = at("mrow", [P, 40, 4], F32, tail + 224)
        tail2 = R3 + 37 * KB + 544
        sinkd = at("sinkd", [P, 8, 4], F32, tail2)
        lrow = at("lrow", [P, 8, 4], F32, tail2 + 128)
        lfox = at("lfox", [P, NT, FOX], F32, tail2 + 256)
        mtmp = at("mtmp", [P, 4], F32, tail2 + 320)
        assert base + tail + 224 + 640 <= nc.sbuf_usable_end
        osq = at("osq", [P, D], F32, R4)
        hss = at("hss", [P, NT, HEADS], F32, R4 + 4 * KB)
        h2_row = at("h2_row", [P, 2, D], F32, R4 + 4 * KB + 512)
        gain2 = at("gain2", [P, D], F32, R4 + 12 * KB + 512)
        lfb = at("lfb", [P, NT, FOX, P], F32, R4 + 4 * KB)
        rw = at("rw", [P, NK, NE], F32, R3 + 32 * KB)
        rb = at("rb", [P, NE], F32, R3 + 33 * KB)
        logit = at("logit", [P, NT, NE], F32, R3 + 33 * KB + 128)
        top = at("top", [P, NT, 8], F32, R3 + 33 * KB + 640)
        topi = at("topi", [P, NT, 8], U32, R3 + 33 * KB + 768)
        topf = at("topf", [P, NT, TOPK], F32, R3 + 33 * KB + 896)
        hot = at("hot", [P, NT, TOPK, NE], F32, R3 + 34 * KB + 128)
        mask = at("mask", [P, NT, NE], F32, R3 + 36 * KB + 128)
        gates_e = at("gates_e", [P, NT, NE], F32, R3 + 36 * KB + 640)
        gsum = at("gsum", [P, NT, 2], F32, R3 + 37 * KB + 128)
        rest = R4
        hot_w = at("hot_w", [P, NT, TOPK, NE], F32, rest)
        count = at("count", [P, NE], F32, rest + 2 * KB)
        nblk = at("nblk", [P, 2, NE], F32, rest + 2 * KB + 128)
        pend = at("pend", [P, NE], F32, rest + 2 * KB + 384)
        pstart = at("pstart", [P, NE], F32, rest + 2 * KB + 512)
        start = at("start", [P, NE], F32, rest + 2 * KB + 640)
        from_pass = at("from_pass", [P, NE], F32, rest + 2 * KB + 768)
        pcmp = at("pcmp", [P, NP_TAB, NE], F32, rest + 3 * KB + 256)
        gT = at("gT", [NE, NT, P], F32, rest + 9 * KB + 256)
        bdn = at("bdn", [NE, D], F32, rest + 12 * KB)
        mixt = at("mixt", [P, CW], F32, rest + 16 * KB)
        m = [R2]

        def moe(name, shape, dt):
            size = 4
            for s in shape[1:]:
                size *= s
            t = at(name, shape, dt, m[0])
            m[0] += size
            return t

        w_hi = moe("w_hi", [P, SPLITS, KQ, CW], F32R)
        w_lo = moe("w_lo", [P, SPLITS, KQ, CW], F32R)
        xT_hi = moe("xT_hi", [P, NK, P], F32R)
        xT_lo = moe("xT_lo", [P, NK, P], F32R)
        aT_hi = moe("aT_hi", [P, NK, P], F32R)
        aT_lo = moe("aT_lo", [P, NK, P], F32R)
        glu = moe("glu", [P, 2, CW // 2], F32)
        lin = moe("lin", [P, 2, CW // 2], F32)
        sig = moe("sig", [P, 2, CW // 2], F32)
        prod = moe("prod", [P, 2, CW // 2], F32)
        act_out = moe("act_out", [P, 2, CW // 2], F32)
        y_row = moe("y_row", [P, D], F32)
        bgu = moe("bgu", [P, CW], F32)
        bgu_hi = moe("bgu_hi", [P, CW], F32R)
        bgu_lo = moe("bgu_lo", [P, CW], F32R)
        pick = moe("pick", [P, NT, P], F32R)
        pass_slots = moe("pass_slots", [P, P], F32)
        pick_e = moe("pick_e", [P, P], F32R)
        assert base + m[0] <= nc.sbuf_usable_end, (base + m[0], nc.sbuf_usable_end)
        y_tok = ring
        res_f = at("res_f", [P, NT, D], F32, R2)
        gate2_f = at("gate2_f", [P, D], F32, R2 + 16 * KB)
        gain_f = at("gain_f", [P, D], F32, R2 + 20 * KB)
        acc = at("acc", [P, 2, D], F32, R2 + 24 * KB)
        junk_f = at("junk_f", [P, D], F32, R2 + 32 * KB)

        bank = [ctx.enter_context(nc.psum_tensor(f"bank{i}", [P, 512], F32)) for i in range(8)]

        y_dram = nc.dram_tensor("y_slots", [SEQ * TOPK + P, D], F32, kind="Internal").ap()
        res_dram = nc.dram_tensor("residual", [NT, P, D], F32, kind="Internal").ap()
        gate2_dram = nc.dram_tensor("gate2_row", [1, D], F32, kind="Internal").ap()

        def sem(name):
            return ctx.enter_context(nc.semaphore(name))

        ring_loaded = [sem(f"ring_loaded{i}") for i in range(SLOTS)]
        (consts, c_in, x_got, gain_got, mod1_bias, small_got, late_got, x_again, bdn_got, bgu_got) = (sem(n) for n in (
            "consts", "c_in", "x_got", "gain_got", "mod1_bias", "small_got", "late_got", "x_again", "bdn_got", "bgu_got"))
        dve_chain, act_chain = sem("dve_chain"), sem("act_chain")
        c_sig, c_ready = sem("c_sig"), sem("c_ready")
        ssq_ready, var_ready, std_ready = sem("ssq_ready"), sem("var_ready"), sem("std_ready")
        ada_done, ada_read = sem("ada_done"), sem("ada_read")
        h_ready, ht_done, ht_read = sem("h_ready"), sem("ht_done"), sem("ht_read")
        proj_done, proj_read = sem("proj_done"), sem("proj_read")
        fz_ready, fl_ready, lfb_ready, cumf_done, cumf_read = (sem(n) for n in (
            "fz_ready", "fl_ready", "lfb_ready", "cumf_done", "cumf_read"))
        score_done, score_read, max_ready, exp_ready, swa_ready, tri_ready, softplus_ready, expo_ready = (sem(n) for n in (
            "score_done", "score_read", "max_ready", "exp_ready", "swa_ready", "tri_ready", "softplus_ready", "expo_ready"))
        pt_done, pt_read, pv_done, o_read_a, o_read_v = (sem(n) for n in ("pt_done", "pt_read", "pv_done", "o_read_a", "o_read_v"))
        hss_ready, hstd_ready, o_norm, ot_done, ot_read = (sem(n) for n in ("hss_ready", "hstd_ready", "o_norm", "ot_done", "ot_read"))
        mix_done, mix_read, x2_ready = sem("mix_done"), sem("mix_read"), sem("x2_ready")
        h2_hi_ready, h2_lo_ready, h2_ready, h2t_done, h2t_read = (sem(n) for n in (
            "h2_hi_ready", "h2_lo_ready", "h2_ready", "h2t_done", "h2t_read"))
        router_done, gate_z, gate_e, gates_ready, mask_ready, rank_done, tables_ready = (sem(n) for n in (
            "router_done", "gate_z", "gate_e", "gates_ready", "mask_ready", "rank_done", "tables_ready"))
        gt_done, gt_read, gb_done, gb_read, resid_ready, res_stored, bgu_ready = (sem(n) for n in (
            "gt_done", "gt_read", "gb_done", "gb_read", "resid_ready", "res_stored", "bgu_ready"))
        split_hi = [sem(f"split_hi{i}") for i in range(USEMS)]
        split_lo = [sem(f"split_lo{i}") for i in range(USEMS)]
        unit_used = [sem(f"unit_used{i}") for i in range(USEMS)]
        pick_step, pick_ready, pick_e_ready = sem("pick_step"), sem("pick_ready"), sem("pick_e_ready")
        gath_hi, gath_lo, xt_hi_ready, xt_lo_ready = (sem(n) for n in ("gath_hi", "gath_lo", "xt_hi_ready", "xt_lo_ready"))
        glu_ready = [sem(f"glu_ready{i}") for i in range(GU_CHUNKS)]
        lin_ready = [sem(f"lin_ready{i}") for i in range(GU_CHUNKS)]
        sig_ready = [sem(f"sig_ready{i}") for i in range(GU_CHUNKS)]
        prod_ready = [sem(f"prod_ready{i}") for i in range(GU_CHUNKS)]
        act_ready = [sem(f"act_ready{i}") for i in range(GU_CHUNKS)]
        at_done = [sem(f"at_done{i}") for i in range(GU_CHUNKS)]
        at_hi_ready = [sem(f"at_hi_ready{i}") for i in range(GU_CHUNKS)]
        at_lo_ready = [sem(f"at_lo_ready{i}") for i in range(GU_CHUNKS)]
        y_ready = [sem(f"y_ready{i}") for i in range(DN_CHUNKS)]
        y_stored = sem("y_stored")
        experts_over = sem("experts_over")
        fin_got, acc_step, fin_ss, fin_var, fin_std, fin_ready = (sem(n) for n in (
            "fin_got", "acc_step", "fin_ss", "fin_var", "fin_std", "fin_ready"))
        y_got = [sem(f"y_got{i}") for i in range(NT)]
        out_stored = [sem(f"out_stored{i}") for i in range(NT)]

        ada_v = ada_w[0].rearrange("(k p) n -> p k n", p=P)
        win_v = w_in[0].rearrange("(k p) n -> p k n", p=P)
        wout_v = w_out[0].rearrange("(k p) n -> p k n", p=P)

        PROJ = [(0, "T", t * P, qaT[:, t, :], QSCALE) for t in range(4)]
        PROJ += [
            (1, "T", 0, kaT[:], 1.0),
            (1, "V", (P, 2 * P, [0, P, 2 * P, 3 * P]), va[:], 1.0),
            (1, "V", (P, 2 * P, [HD, HD + P, HD + 2 * P]), va_mid[:], 1.0),
            (1, "T", 256, qfT[:, 0, :], QSCALE),
            (1, "T", 384, qfT[:, 1, :], QSCALE),
        ]
        PROJ += [(2, "V", (0, 256 + FOX, [n * P]), (vs[:, n, :], flog[:, n, :]), 1.0) for n in range(NT)]
        PROJ += [
            (3, "T", 0, kfT[:, 0, :], 1.0),
            (3, "T", P, kfT[:, 1, :], 1.0),
            (3, "V", (256, 512, [0, P]), vf[:, 0:2, :], 1.0),
            (3, "V", (256, 512, [2 * P, 3 * P]), vf[:, 2:4, :], 1.0),
        ]
        PROJ += [(4, "T", j * P, t, s) for j, (t, s) in enumerate((
            (qsT[:, 0, :], QSCALE), (qsT[:, 1, :], QSCALE), (ksT[:, 0, :], 1.0), (ksT[:, 1, :], 1.0)))]

        def ada_chunk(i):
            return [(0, CW, ada_v[:, :, i * CW:(i + 1) * CW])]

        STREAM = [(ada_chunk(i), ada_done, i + 1) for i in range(4)]
        PROJ0 = len(STREAM)
        win_parts = [
            [((2 * t + h) * HD, (2 * t + h + 1) * HD, win_v[:, :, C_QA + (4 * h + t) * HD:C_QA + (4 * h + t + 1) * HD])
             for t in range(4) for h in range(2)],
            [(0, CW, win_v[:, :, C_KA:C_KA + CW])],
            [(0, 256, win_v[:, :, C_VS:C_VS + 256]), (256, 256 + FOX, win_v[:, :, C_FL:C_FL + FOX])],
            [(0, CW, win_v[:, :, C_KF:C_KF + CW])],
            [(0, CW, win_v[:, :, C_QS:C_QS + CW])],
        ]
        for i, parts in enumerate(win_parts):
            STREAM.append((parts, proj_done, sum(1 for g in PROJ if g[0] <= i)))
        ADA1 = len(STREAM)
        STREAM += [(ada_chunk(i), ada_done, i + 1) for i in range(4, 12)]
        OUT0 = len(STREAM)
        STREAM += [([(0, CW, wout_v[:, :, i * CW:(i + 1) * CW])], mix_done, 2 * NT) for i in range(2)]
        G0 = len(STREAM)
        loads = [0] * SLOTS
        ring_value = []
        for g, (parts, _, _) in enumerate(STREAM):
            loads[g % SLOTS] += len(parts)
            ring_value.append(16 * loads[g % SLOTS])

        def slot_of(ch):
            return (G0 + ch) % SLOTS

        load0 = [loads[slot_of(ch)] + 1 for ch in range(CHUNKS)]

        def expert_chunk(e, ch):
            src, n = (w_gu, ch) if ch < GU_CHUNKS else (w_dn, ch - GU_CHUNKS)
            return src[0, bass.ds(e, 1)].rearrange("a (k p) n -> p (a k) n", p=P)[:, :, n * CW:(n + 1) * CW]

        ATT = [("swa", ch, 0) for ch in range(SEQ // HD)]
        FOX0 = len(ATT)
        ATT += [("fox", n, h) for n in range(NT) for h in range(FOX)]
        SB0 = len(ATT)
        ATT += [("sb", n, h) for n in range(NT) for h in range(SB)]
        NU = len(ATT)
        N_CONST = 20

        def turns(eng, p):
            return [eng.snap(p * UTURNS + (i + 1)) for i in range(UTURNS + 1)]

        block = ctx.enter_context(nc.Block())

        @block.sync
        def _(sp):
            for g, (parts, _, _) in enumerate(STREAM):
                s = g % SLOTS
                if g >= SLOTS:
                    sp.wait_ge(STREAM[g - SLOTS][1], STREAM[g - SLOTS][2])
                for a, b, src in parts:
                    sp.dma_start(ring[:, s, :, a:b], src).then_inc(ring_loaded[s], 16)
            for ch in range(CHUNKS):
                g = G0 + ch - SLOTS
                sp.wait_ge(STREAM[g][1], STREAM[g][2])
                sp.dma_start(ring[:, slot_of(ch)], expert_chunk(0, ch)).then_inc(ring_loaded[slot_of(ch)], 16)
            sp.wait_ge(tables_ready, 1)
            n_passes = sp.value_load(passes_i[0:1, 0:1], min_val=NE, max_val=MAX_PASSES)
            with sp.Fori(1, n_passes + 1) as p:
                e_now = sp.value_load(etab_i[0:1, bass.ds(p, 1)], min_val=0, max_val=NE - 1)
                e_before = sp.value_load(etab_i[0:1, bass.ds(p - 1, 1)], min_val=0, max_val=NE - 1)
                done = [sp.snap(p * UTURNS + (i + 1 - UTURNS)) for i in range(UTURNS)]
                before = {v: sp.snap(p * 16 + (v - 1) * 16) for v in sorted(set(load0))}
                with sp.If(e_now != e_before):
                    for ch in range(CHUNKS):
                        src = expert_chunk(e_now, ch)
                        last = UPC * ch + UPC - 1
                        sp.wait_ge(split_lo[last % USEMS], done[last // USEMS])
                        sp.dma_start(ring[:, slot_of(ch)], src).then_inc(ring_loaded[slot_of(ch)], 16)
                with sp.Else():
                    for ch in range(CHUNKS):
                        sp.wait_ge(ring_loaded[slot_of(ch)], before[load0[ch]])
                        sp.sem_inc(ring_loaded[slot_of(ch)], 16)
                sp.nop()

        @block.gpsimd
        def _(pool):
            g = nc.gpsimd
            g.memset(ident[:], 0.0).then_inc(consts, 1)
            g.memset(ones[:], 1.0).then_inc(consts, 1)
            g.memset(tri_incl[:], 1.0).then_inc(consts, 1)
            g.memset(tri_strict[:], 1.0).then_inc(consts, 1)
            g.memset(low_strict[:], 1.0).then_inc(consts, 1)
            g.memset(causal_add[:], 0.0).then_inc(consts, 1)
            g.memset(strict_add[:], 0.0).then_inc(consts, 1)
            pool.wait_ge(consts, 7)
            for t, cols, base_v, cm, step, keep, fill in (
                    (ident, P, 0, 1, -1, ALU.not_equal, 1.0),
                    (tri_incl, SEQ, 0, -1, 1, ALU.is_ge, 0.0),
                    (tri_strict, P, -1, -1, 1, ALU.is_ge, 0.0),
                    (low_strict, P, -1, 1, -1, ALU.is_ge, 0.0),
                    (causal_add, P, 0, 1, -1, ALU.is_ge, NEG),
                    (strict_add, P, -1, 1, -1, ALU.is_ge, NEG)):
                g.affine_select(out=t[:, 0:cols], in_=t[:, 0:cols], pattern=[[step, cols]], compare_op=keep,
                                fill=fill, base=base_v, channel_multiplier=cm).then_inc(consts, 1)
            pool.wait_ge(consts, 13)
            for h in range(2):
                g.iota(alibi[64 * h:64 * h + 64, 3, :], [[-1, P]], base=HD, channel_multiplier=1,
                       allow_small_or_imprecise_dtypes=True).then_inc(consts, 1)
                pool.wait_ge(consts, 14 + h)
            g.iota(slot_iota[:], [[1, P]], base=0, channel_multiplier=0,
                   allow_small_or_imprecise_dtypes=True).then_inc(consts, 1)
            for h in range(4):
                pool.wait_ge(consts, 16 + h)
                g.iota(expert_of_row[32 * h:32 * h + 32, :], [[0, P]], base=0, channel_multiplier=1,
                       allow_small_or_imprecise_dtypes=True).then_inc(consts, 1)
            pool.wait_ge(consts, N_CONST)
            g.iota(iota_e[:], [[1, NE]], base=0, channel_multiplier=0,
                   allow_small_or_imprecise_dtypes=True).then_inc(consts, 1)
            g.iota(iota_p[:], [[1, NP_TAB]], base=0, channel_multiplier=0,
                   allow_small_or_imprecise_dtypes=True).then_inc(consts, 1)

            pool.wait_ge(tables_ready, 1)
            n_passes = pool.value_load(passes_i[0:1, 0:1], min_val=NE, max_val=MAX_PASSES)
            with pool.Fori(0, n_passes) as p:
                p1, p2 = pool.snap(p + 1), pool.snap(p + 2)
                for ch in range(GU_CHUNKS):
                    pool.wait_ge(lin_ready[ch], p2 if ch >= 2 else p1)
                    g.tensor_tensor(prod[:, ch % 2], glu[:, ch % 2], lin[:, ch % 2], ALU.mult).then_inc(prod_ready[ch], 1)
                    pool.wait_ge(prod_ready[ch], p1)
                    pool.wait_ge(sig_ready[ch], p1)
                    pool.wait_ge(at_done[(ch + 2) % 4], p1)
                    g.tensor_tensor(act_out[:, ch % 2], prod[:, ch % 2], sig[:, ch % 2], ALU.mult).then_inc(act_ready[ch], 1)
            pool.wait_ge(experts_over, 1)
            for n in range(NT):
                for k in range(TOPK):
                    g.indirect_dma_start(
                        out=ring[:, n].rearrange("p a b -> p (a b)")[:, k * D:(k + 1) * D], out_offset=None,
                        in_=y_dram[0:SEQ * TOPK, :], in_offset=bass.IndirectOffsetOnAxis(ap=my_slot_i[:, n, k:k + 1], axis=0),
                        bounds_check=SEQ * TOPK - 1, oob_is_err=True).then_inc(y_got[n], 16)

        @block.scalar
        def _(sc):
            a = nc.scalar
            chain = [0]

            def link(ins):
                chain[0] += 1
                ins.then_inc(act_chain, 1)
                sc.wait_ge(act_chain, chain[0])

            sc.dma_start(c_col[:, 0, :], c.rearrange("a (k p) -> p (a k)", p=P), allow_slow_non_contiguous=True).then_inc(c_in, 16)
            xv = x[0].rearrange("(n p) d -> p n d", p=P)
            sc.dma_start(x_in[:], xv).then_inc(x_got, 16)
            sc.dma_start(gain[:], norm1_gain.broadcast_to([P, D])).then_inc(gain_got, 16)
            sc.dma_start(mod1[:], ada_b[:, 0:2 * D].broadcast_to([P, 2 * D])).then_inc(mod1_bias, 16)
            sc.dma_start(neg_sink[0:64, :], attn_sinks[:, 0:4].broadcast_to([64, 4])).then_inc(small_got, 16)
            sc.dma_start(neg_sink[64:128, :], attn_sinks[:, 4:8].broadcast_to([64, 4])).then_inc(small_got, 16)
            sc.dma_start(fbias[:], forget_bias.broadcast_to([P, FOX])).then_inc(small_got, 16)
            sc.wait_ge(c_in, 16)
            a.activation(c_col[:, 1, :], c_col[:, 0, :], ACT.Sigmoid).then_inc(c_sig, 1)
            sc.wait_ge(x_got, 16)
            for n in range(NT):
                if n >= 1:
                    sc.wait_ge(ssq_ready, n)
                a.activation(h_row[:, 0], x_in[:, n], ACT.Square, accum_out=ssq[:, n:n + 1]).then_inc(ssq_ready, 1)
            sc.wait_ge(var_ready, 1)
            a.activation(rstd[:, 0:4], ssq[:, 4:8], ACT.Sqrt).then_inc(std_ready, 1)
            for n in range(NT):
                for half in range(2):
                    sc.wait_ge(ht_done, 2 * n + half + 1)
                    a.copy(hT[:, 4 * half:4 * half + 4, n * P:(n + 1) * P],
                           bank[2 + 2 * (n % 2) + half][:].rearrange("p (k t) -> p k t", k=4)).then_inc(ht_read, 1)
            sc.wait_ge(fz_ready, 1)
            link(a.activation(fwork[:], flog[:], ACT.Abs))
            link(a.activation(fwork[:], fwork[:], ACT.Exp, scale=-1.0))
            a.activation(fwork[:], fwork[:], ACT.Ln, bias=1.0).then_inc(fl_ready, 1)

            def transposed(u):
                kind, n, _ = ATT[u]
                rows = HD if (kind, n) == ("swa", 0) else P
                cols = SEQ if kind == "swa" else (n + 1) * P
                sc.wait_ge(pt_done, u + 1)
                if u >= 2:
                    sc.wait_ge(pv_done, u - 1)
                a.copy(probT[0:rows, u % 2, 0:cols], bank[2 + u % 2][0:rows, 0:cols]).then_inc(pt_read, 1)

            def outputs(u):
                kind, n, h = ATT[u]
                if kind == "swa" and n % 2 == 1:
                    sc.wait_ge(pv_done, u + 1)
                    a.copy(o[:, n // 2, 0:512], bank[4 + (n // 2) % 2][:]).then_inc(o_read_a, 1)
                if kind == "sb" and h == SB - 1:
                    sc.wait_ge(pv_done, u + 1)
                    a.copy(o[:, n, 768:1024], bank[6 + n % 2][:, 0:256]).then_inc(o_read_a, 1)

            def stick_weights(u):
                cols = (ATT[u][1] + 1) * P
                sc.wait_ge(expo_ready, u - SB0 + 1)
                sc.wait_ge(pt_done, u - 1)
                a.activation(prob[:, u % 2, 0:cols], score[:, u % 2, 0:cols], ACT.Exp).then_inc(tri_ready, 1)

            for u, (kind, n, h) in enumerate(ATT):
                b, cols = u % 2, (n + 1) * P
                if kind == "swa":
                    first = HD if n == 0 else 0
                    sc.wait_ge(max_ready, u + 1)
                    for t in range(4):
                        a.activation(soft[:, b, t * P + first:(t + 1) * P], score[:, b, t * P + first:(t + 1) * P],
                                     ACT.Exp, bias=mrow[:, u, t:t + 1], accum_out=lrow[:, n, t:t + 1]).then_inc(exp_ready, 1)
                    a.activation(sinkd[:, n, :], sinkd[:, n, :], ACT.Exp).then_inc(exp_ready, 1)
                elif kind == "fox":
                    sc.wait_ge(max_ready, u + 1)
                    sc.wait_ge(pt_done, u - 1)
                    a.activation(prob[:, b, 0:cols], score[:, b, 0:cols], ACT.Exp, bias=mrow[:, u, 0:1],
                                 accum_out=lfox[:, n, h:h + 1]).then_inc(tri_ready, 1)
                else:
                    i = u - SB0
                    sc.wait_ge(score_done, u + 1)
                    if i >= 2:
                        sc.wait_ge(expo_ready, i - 1)
                    link(a.activation(soft[:, b, 0:cols], bank[b][:, 0:cols], ACT.Abs))
                    link(a.activation(soft[:, b, 0:cols], soft[:, b, 0:cols], ACT.Exp, scale=-1.0))
                    a.activation(soft[:, b, 0:cols], soft[:, b, 0:cols], ACT.Ln, bias=1.0).then_inc(softplus_ready, 1)
                    if i >= 1:
                        stick_weights(u - 1)
                if u >= 2:
                    transposed(u - 2)
                if u >= 4:
                    outputs(u - 4)
            stick_weights(NU - 1)
            transposed(NU - 2)
            transposed(NU - 1)
            for u in range(NU - 4, NU):
                outputs(u)
            sc.wait_ge(pv_done, NU)
            sc.dma_start(mod2[:], ada_b[:, 2 * D:6 * D].broadcast_to([P, 4 * D])).then_inc(late_got, 16)
            sc.dma_start(rw[:], router_w[0].rearrange("(k p) e -> p k e", p=P)).then_inc(late_got, 16)
            sc.dma_start(rb[:], router_b.broadcast_to([P, NE])).then_inc(late_got, 16)
            sc.dma_start(head_gain[:], mix_out_gain.rearrange("a (k p) -> p (a k)", p=P), allow_slow_non_contiguous=True).then_inc(late_got, 16)
            sc.dma_start(gain2[:], norm2_gain.broadcast_to([P, D])).then_inc(late_got, 16)
            sc.dma_start(resid[:], xv).then_inc(x_again, 16)
            sc.wait_ge(hss_ready, NT)
            a.activation(hss[:], hss[:], ACT.Sqrt).then_inc(hstd_ready, 1)

            def h2_out(n):
                sc.wait_ge(h2_ready, n + 1)
                a.copy(h2_hi[:, n], h2_row[:, n % 2]).then_inc(h2_hi_ready, 1)
                for half in range(2):
                    sc.wait_ge(h2t_done, 2 * n + half + 1)
                    a.copy(h2T[:, 4 * half:4 * half + 4, n * P:(n + 1) * P],
                           bank[4 + 2 * (n % 2) + half][:].rearrange("p (k t) -> p k t", k=4)).then_inc(h2t_read, 1)

            for n in range(NT):
                sc.wait_ge(x2_ready, n + 1)
                if n >= 1:
                    sc.wait_ge(ssq_ready, NT + n)
                a.activation(osq[:], resid[:, n], ACT.Square, accum_out=ssq[:, n:n + 1]).then_inc(ssq_ready, 1)
                sc.wait_ge(var_ready, 2 + n)
                a.activation(rstd[:, n:n + 1], ssq[:, 4 + n:5 + n], ACT.Sqrt).then_inc(std_ready, 1)
                if n >= 1:
                    h2_out(n - 1)
            h2_out(NT - 1)
            sc.wait_ge(h2_lo_ready, NT)
            sc.dma_start(bdn[:], b_dn[0]).then_inc(bdn_got, 16)
            sc.wait_ge(gate_z, 1)
            a.activation(gate[:], gate[:], ACT.Exp).then_inc(gate_e, 1)
            sc.wait_ge(resid_ready, 2 * NT)
            sc.dma_start(res_dram.rearrange("n p d -> p n d"), resid[:]).then_inc(res_stored, 16)
            sc.dma_start(gate2_dram, mod2[0:1, 3 * D:4 * D]).then_inc(res_stored, 16)
            sc.wait_ge(res_stored, 32)
            for n in range(4):
                sc.dma_start(bgu[32 * n:32 * n + 32, :], b_gu[0, :, n * CW:(n + 1) * CW]).then_inc(bgu_got, 16)

            def split_high(j):
                ch, q = divmod(j, UPC)
                a.copy(w_hi[:, j % SPLITS], ring[:, slot_of(ch), KQ * q:KQ * q + KQ, :]).then_inc(split_hi[j % USEMS], 1)

            def gathered(dst, done, ready, value):
                sc.wait_ge(done, value)
                a.copy(dst[:, 0:4], bank[6][:].rearrange("p (k t) -> p k t", k=4))
                a.copy(dst[:, 4:8], bank[7][:].rearrange("p (k t) -> p k t", k=4)).then_inc(ready, 1)

            def act_high(ch, p1, p2):
                sc.wait_ge(at_done[ch], p2 if ch >= 2 else p1)
                half = bank[4 + ch % 2][:, 0:256].rearrange("p (k t) -> p k t", k=2)
                a.copy(aT_hi[:, 2 * ch:2 * ch + 2], half).then_inc(at_hi_ready[ch], 1)

            n_passes = sc.value_load(passes_i[0:1, 0:1], min_val=NE, max_val=MAX_PASSES)
            sc.sem_inc(y_stored, 16)
            for hf in range(DN_CHUNKS):
                sc.sem_inc(y_ready[hf], 1)
            sc.wait_ge(ring_loaded[slot_of(0)], 16 * load0[0])
            for q in range(UPC):
                split_high(q)
            gathered(xT_hi, gath_hi, xt_hi_ready, 1)
            gathered(xT_lo, gath_lo, xt_lo_ready, 1)
            with sc.Fori(0, n_passes) as p:
                p1, p2 = sc.snap(p + 1), sc.snap(p + 2)
                turn = turns(sc, p)
                stored = sc.snap(p * 16 + 16)
                loaded = {v: sc.snap(p * 16 + 16 * v) for v in sorted(set(load0[1:]) | {load0[0] + 1})}
                for ch in range(1, CHUNKS + 1):
                    cc = ch % CHUNKS
                    sc.wait_ge(ring_loaded[slot_of(cc)], loaded[load0[0] + 1 if cc == 0 else load0[cc]])
                    for q in range(UPC):
                        used = (ch - 1) * UPC + q
                        sc.wait_ge(unit_used[used % USEMS], turn[used // USEMS])
                        split_high(cc * UPC + q)
                    if ch <= GU_CHUNKS:
                        sc.wait_ge(glu_ready[ch - 1], p1)
                        a.activation(sig[:, (ch - 1) % 2], glu[:, (ch - 1) % 2], ACT.Sigmoid,
                                     scale=ALPHA).then_inc(sig_ready[ch - 1], 1)
                    if 2 <= ch <= GU_CHUNKS:
                        act_high(ch - 2, p1, p2)
                    if ch == GU_CHUNKS:
                        gathered(xT_hi, gath_hi, xt_hi_ready, p2)
                        act_high(3, p1, p2)
                        gathered(xT_lo, gath_lo, xt_lo_ready, p2)
                sc.wait_ge(y_stored, stored)
                for hf in range(DN_CHUNKS):
                    used = (GU_CHUNKS + hf + 1) * UPC - 1
                    sc.wait_ge(unit_used[used % USEMS], turn[used // USEMS])
                    a.copy(y_row[:, hf * CW:(hf + 1) * CW], bank[2 + hf][:]).then_inc(y_ready[hf], 1)
                first_slot = sc.value_load(ybase_i[0:1, bass.ds(p, 1)], min_val=0, max_val=SEQ * TOPK)
                y_at = y_dram[bass.ds(first_slot, P), :]
                for hf in range(DN_CHUNKS):
                    sc.wait_ge(y_ready[hf], p2)
                sc.dma_start(y_at, y_row[:]).then_inc(y_stored, 16)

            stored = sc.snap(n_passes * 16 + 16)
            split_end, split_past = sc.snap(n_passes * UTURNS), sc.snap(n_passes * UTURNS + 1)
            for j in range(USEMS):
                sc.wait_ge(split_lo[j], split_past if j < UPC else split_end)
            sc.wait_ge(y_stored, stored)
            sc.sem_inc(experts_over, 1)
            sc.dma_start(res_f[:], res_dram.rearrange("n p d -> p n d")).then_inc(fin_got, 16)
            sc.dma_start(gate2_f[:], gate2_dram.broadcast_to([P, D])).then_inc(fin_got, 16)
            sc.dma_start(gain_f[:], final_gain.rearrange("(a d) -> a d", a=1).broadcast_to([P, D])).then_inc(fin_got, 16)
            for n in range(NT):
                sc.wait_ge(acc_step, 6 * n + 6)
                if n >= 1:
                    sc.wait_ge(fin_ss, n)
                a.activation(junk_f[:], acc[:, n % 2], ACT.Square, accum_out=ssq[:, n:n + 1]).then_inc(fin_ss, 1)
                sc.wait_ge(fin_var, n + 1)
                a.activation(rstd[:, n:n + 1], ssq[:, 4 + n:5 + n], ACT.Sqrt).then_inc(fin_std, 1)
                sc.wait_ge(fin_ready, n + 1)
                sc.dma_start(out[0, n * P:(n + 1) * P, :], acc[:, n % 2]).then_inc(out_stored[n], 16)
            for n in range(NT):
                sc.wait_ge(out_stored[n], 16)

        @block.vector
        def _(ve):
            v = nc.vector
            chain = [0]

            def link(ins):
                chain[0] += 1
                ins.then_inc(dve_chain, 1)
                ve.wait_ge(dve_chain, chain[0])

            def wide(ap, n, m):
                return ap.unsqueeze(2).broadcast_to([P, n, m])

            ve.wait_ge(c_sig, 1)
            link(v.tensor_tensor(c_col[:, 2, :], c_col[:, 0, :], c_col[:, 1, :], ALU.mult))
            v.tensor_copy(c_rep[:], wide(c_col[:, 2, :], NK, P)).then_inc(c_ready, 1)
            ve.wait_ge(consts, N_CONST)
            link(v.scalar_tensor_tensor(alibi[:, 3, :], alibi[:, 3, :], -1.0, alibi[:, 3, :], ALU.mult, ALU.max))
            for t in range(4):
                for h in range(2):
                    slope = 2.0 ** (-8.0 * (t + 4 * h + 1) / SWA_Q)
                    link(v.tensor_scalar(alibi[64 * h:64 * h + 64, t, :], alibi[64 * h:64 * h + 64, 3, :], -slope, None, ALU.mult))
            ve.wait_ge(small_got, 48)
            link(v.tensor_scalar(neg_sink[:], neg_sink[:], -1.0, None, ALU.mult))
            ve.wait_ge(ssq_ready, NT)
            v.tensor_scalar(ssq[:, 4:8], ssq[:, 0:4], 1.0 / D, EPS, ALU.mult, ALU.add).then_inc(var_ready, 1)
            ve.wait_ge(std_ready, 1)
            link(v.reciprocal(rstd[:, 0:4], rstd[:, 0:4]))
            ve.wait_ge(mod1_bias, 16)
            for i in range(4):
                ve.wait_ge(ada_done, i + 1)
                m = mod1[:, i * CW:(i + 1) * CW]
                v.tensor_tensor(m, bank[i % 2][:], m, ALU.add).then_inc(ada_read, 1)
            ve.wait_ge(gain_got, 16)
            ve.wait_ge(ada_read, 4)
            link(v.scalar_tensor_tensor(mod1[:, D:2 * D], mod1[:, D:2 * D], 1.0, gain[:], ALU.add, ALU.mult))
            for n in range(NT):
                if n >= 2:
                    ve.wait_ge(ht_done, 2 * (n - 1))
                link(v.scalar_tensor_tensor(h_row[:, n % 2], x_in[:, n], rstd[:, n:n + 1], mod1[:, D:2 * D], ALU.mult, ALU.mult))
                v.tensor_tensor(h_row[:, n % 2], h_row[:, n % 2], mod1[:, 0:D], ALU.add).then_inc(h_ready, 1)
            for j, (i, kind, cols, dst, scale) in enumerate(PROJ):
                ve.wait_ge(proj_done, j + 1)
                src = bank[6 + j % 2]
                if kind != "V":
                    v.tensor_scalar(dst, src[:], scale, None, ALU.mult).then_inc(proj_read, 1)
                elif i == 2:
                    link(v.tensor_copy(dst[1], src[:, 256:256 + FOX]))
                    v.tensor_copy(dst[0], src[:, 0:256]).then_inc(proj_read, 1)
                else:
                    w = cols[1] - cols[0]
                    m = len(cols[2])
                    v.tensor_copy(dst, src[:, 0:m * w].rearrange("p (m w) -> p m w", m=m)).then_inc(proj_read, 1)
                if (i, kind) == (2, "V") and cols[2] == [3 * P]:
                    v.tensor_tensor(flog[:], flog[:], fbias[:].unsqueeze(1).broadcast_to([P, NT, FOX]), ALU.add).then_inc(fz_ready, 1)
            ve.wait_ge(fl_ready, 1)
            link(v.scalar_tensor_tensor(flog[:], flog[:], 0.0, fwork[:], ALU.min, ALU.subtract))
            v.tensor_copy(lfb[:].rearrange("p n h m -> p (n h) m"),
                          wide(flog[:].rearrange("p n h -> p (n h)"), NT * FOX, P)).then_inc(lfb_ready, 1)
            ve.wait_ge(cumf_done, 1)
            v.tensor_copy(cumf_col[:].rearrange("p n h -> p (n h)"), bank[4][:, 0:NT * FOX]).then_inc(cumf_read, 1)
            for h in range(FOX):
                ve.wait_ge(cumf_done, h + 2)
                v.tensor_copy(cumf_row[:, h, :], bank[(5, 0, 1, 2)[h]][:]).then_inc(cumf_read, 1)
            ve.wait_ge(cumf_read, 1 + FOX)

            def swa_normalize(u):
                n, b = ATT[u][1], u % 2
                first = HD if n == 0 else 0
                ve.wait_ge(exp_ready, 5 * (u + 1))
                link(v.tensor_tensor(lrow[:, n, :], lrow[:, n, :], sinkd[:, n, :], ALU.add))
                link(v.reciprocal(lrow[:, n, :], lrow[:, n, :]))
                if u >= 2:
                    ve.wait_ge(pt_done, u - 1)
                v.tensor_tensor(prob[:, b].rearrange("p (t j) -> p t j", t=4)[:, :, first:],
                                soft[:, b].rearrange("p (t j) -> p t j", t=4)[:, :, first:],
                                wide(lrow[:, n, :], 4, P - first), ALU.mult).then_inc(swa_ready, 1)

            def fox_outputs(u):
                kind, n, h = ATT[u]
                if kind == "fox" and h == FOX - 1:
                    ve.wait_ge(pv_done, u + 1)
                    link(v.reciprocal(lfox[:, n, :], lfox[:, n, :]))
                    v.tensor_tensor(o[:, n, 512:768].rearrange("p (h d) -> p h d", h=FOX),
                                    bank[6 + n % 2][:, 0:256].rearrange("p (h d) -> p h d", h=FOX),
                                    wide(lfox[:, n, :], FOX, HD), ALU.mult).then_inc(o_read_v, 1)

            for u, (kind, n, h) in enumerate(ATT):
                b, cols = u % 2, (n + 1) * P
                diag = slice(n * P, (n + 1) * P)
                if kind == "swa":
                    first = HD if n == 0 else 0
                    s4 = score[:, b].rearrange("p (t j) -> p t j", t=4)[:, :, first:]
                    ve.wait_ge(score_done, u + 1)
                    v.tensor_tensor(s4, bank[b][:].rearrange("p (t j) -> p t j", t=4)[:, :, first:],
                                    alibi[:, :, first:], ALU.add).then_inc(score_read, 1)
                    ve.wait_ge(score_read, u + 1)
                    link(v.tensor_reduce(mtmp[:], s4, AX.X, ALU.max))
                    link(v.scalar_tensor_tensor(mrow[:, u, :], mtmp[:], -1.0, neg_sink[:], ALU.mult, ALU.min))
                    v.tensor_tensor(sinkd[:, n, :], mrow[:, u, :], neg_sink[:], ALU.subtract).then_inc(max_ready, 1)
                elif kind == "fox":
                    ve.wait_ge(score_done, u + 1)
                    if u >= FOX0 + 2:
                        ve.wait_ge(tri_ready, u - 1 - FOX0)
                    v.scalar_tensor_tensor(score[:, b, 0:cols], bank[b][:, 0:cols], cumf_col[:, n, h:h + 1],
                                           cumf_row[:, h, 0:cols], ALU.add, ALU.subtract).then_inc(score_read, 1)
                    ve.wait_ge(score_read, u + 1)
                    link(v.tensor_tensor(score[:, b, diag], score[:, b, diag], causal_add[:], ALU.add))
                    link(v.tensor_reduce(mtmp[:, 0:1], score[:, b, 0:cols], AX.X, ALU.max))
                    v.tensor_scalar(mrow[:, u, 0:1], mtmp[:, 0:1], -1.0, None, ALU.mult).then_inc(max_ready, 1)
                else:
                    ve.wait_ge(softplus_ready, u - SB0 + 1)
                    link(v.scalar_tensor_tensor(stick[:, 0:cols], bank[b][:, 0:cols], 0.0, soft[:, b, 0:cols], ALU.max, ALU.add))
                    link(v.tensor_tensor(stick[:, diag], stick[:, diag], low_strict[:], ALU.mult))
                    back = stick[:, cols - 1::-1] if cols == SEQ else stick[:, 0:cols][:, ::-1]
                    link(v.tensor_tensor_scan(back, ones[:, 0:1].broadcast_to([P, cols]), back, 0.0, ALU.mult, ALU.add))
                    ve.wait_ge(tri_ready, u - 1 - FOX0)
                    v.tensor_tensor(score[:, b, 0:cols], bank[b][:, 0:cols], stick[:, 0:cols], ALU.subtract).then_inc(score_read, 1)
                    ve.wait_ge(score_read, u + 1)
                    v.tensor_tensor(score[:, b, diag], score[:, b, diag], strict_add[:], ALU.add).then_inc(expo_ready, 1)
                if u >= 1 and ATT[u - 1][0] == "swa":
                    swa_normalize(u - 1)
                if u >= 4:
                    fox_outputs(u - 4)
            ve.wait_ge(pv_done, NU)
            for n in range(NT):
                ve.wait_ge(o_read_a, NT + n + 1)
                ve.wait_ge(o_read_v, NT)
                link(v.tensor_tensor(osq[:], o[:, n], o[:, n], ALU.mult))
                link(v.tensor_reduce(hss[:, n, :], osq[:].rearrange("p (h d) -> p h d", h=HEADS), AX.X, ALU.add))
                v.tensor_scalar(hss[:, n, :], hss[:, n, :], 1.0 / HD, EPS, ALU.mult, ALU.add).then_inc(hss_ready, 1)
            ve.wait_ge(hstd_ready, 1)
            link(v.reciprocal(hss[:].rearrange("p n h -> p (n h)"), hss[:].rearrange("p n h -> p (n h)")))
            for n in range(NT):
                on = o[:, n].rearrange("p (h d) -> p h d", h=HEADS)
                v.tensor_tensor(on, on, wide(hss[:, n, :], HEADS, HD), ALU.mult).then_inc(o_norm, 1)
            ve.wait_ge(late_got, 80)
            for i in range(4, 12):
                ve.wait_ge(ada_done, i + 1)
                m = mod2[:, (i - 4) * CW:(i - 3) * CW]
                v.tensor_tensor(m, bank[i % 4][:], m, ALU.add).then_inc(ada_read, 1)
            ve.wait_ge(ada_read, 12)
            gate1, shift2, scale2, gate2 = (mod2[:, i * D:(i + 1) * D] for i in range(4))
            link(v.scalar_tensor_tensor(scale2, scale2, 1.0, gain2[:], ALU.add, ALU.mult))
            for n in range(NT):
                for half in range(2):
                    ve.wait_ge(ot_done, 2 * n + half + 1)
                    v.tensor_tensor(oT[:, 4 * half:4 * half + 4, n * P:(n + 1) * P],
                                    bank[4 + 2 * (n % 2) + half][:].rearrange("p (k t) -> p k t", k=4),
                                    wide(head_gain[:, 4 * half:4 * half + 4], 4, P), ALU.mult).then_inc(ot_read, 1)

            def h2_low(n):
                ve.wait_ge(h2_hi_ready, n + 1)
                v.tensor_tensor(h2_lo[:, n], h2_row[:, n % 2], h2_hi[:, n].bitcast(F32), ALU.subtract).then_inc(h2_lo_ready, 1)

            ve.wait_ge(x_again, 16)
            for n in range(NT):
                for half in range(2):
                    cs = slice(half * CW, (half + 1) * CW)
                    ve.wait_ge(mix_done, 2 * n + half + 1)
                    v.tensor_tensor(mixt[:], bank[(2 * n + half) % 4][:], gate1[:, cs], ALU.mult).then_inc(mix_read, 1)
                    ve.wait_ge(mix_read, 2 * n + half + 1)
                    add = v.tensor_tensor(resid[:, n, cs], resid[:, n, cs], mixt[:], ALU.add)
                    if half:
                        add.then_inc(x2_ready, 1)
                    else:
                        link(add)
                ve.wait_ge(ssq_ready, NT + n + 1)
                v.tensor_scalar(ssq[:, 4 + n:5 + n], ssq[:, n:n + 1], 1.0 / D, EPS, ALU.mult, ALU.add).then_inc(var_ready, 1)
                if n >= 1:
                    h2_low(n - 1)
                ve.wait_ge(std_ready, 2 + n)
                link(v.reciprocal(rstd[:, n:n + 1], rstd[:, n:n + 1]))
                if n >= 2:
                    ve.wait_ge(h2t_done, 2 * (n - 1))
                    ve.wait_ge(h2_hi_ready, n - 1)
                    ve.wait_ge(h2_lo_ready, n - 1)
                link(v.scalar_tensor_tensor(h2_row[:, n % 2], resid[:, n], rstd[:, n:n + 1], scale2, ALU.mult, ALU.mult))
                v.tensor_tensor(h2_row[:, n % 2], h2_row[:, n % 2], shift2, ALU.add).then_inc(h2_ready, 1)
            h2_low(NT - 1)
            ve.wait_ge(router_done, 1)
            link(v.tensor_tensor(logit[:], bank[0][:, 0:NT * NE].rearrange("p (n e) -> p n e", n=NT),
                                 rb[:].unsqueeze(1).broadcast_to([P, NT, NE]), ALU.add))
            for n in range(NT):
                link(v.max(top[:, n, :], logit[:, n, :]))
                link(v.max_index(topi[:, n, :], top[:, n, :], logit[:, n, :]))
            link(v.tensor_copy(topf[:], topi[:, :, 0:TOPK]))
            v.tensor_tensor(gate[:], top[:, :, 0:TOPK], top[:, :, 0:1].broadcast_to([P, NT, TOPK]), ALU.subtract).then_inc(gate_z, 1)
            ve.wait_ge(consts, N_CONST + 2)
            for n in range(NT):
                link(v.tensor_tensor(hot[:, n], iota_e[:].unsqueeze(1).broadcast_to([P, TOPK, NE]), wide(topf[:, n, :], TOPK, NE), ALU.is_equal))
            v.tensor_reduce(mask[:], hot[:].rearrange("p n k e -> p n e k"), AX.X, ALU.add).then_inc(mask_ready, 1)
            ve.wait_ge(gate_e, 1)
            link(v.tensor_reduce(gsum[:, :, 0], gate[:], AX.X, ALU.add))
            link(v.reciprocal(gsum[:, :, 1], gsum[:, :, 0]))
            link(v.tensor_tensor(gate[:], gate[:], gsum[:, :, 1:2].broadcast_to([P, NT, TOPK]), ALU.mult))
            for n in range(NT):
                link(v.tensor_tensor(hot_w[:, n], hot[:, n], wide(gate[:, n, :], TOPK, NE), ALU.mult))
            v.tensor_reduce(gates_e[:], hot_w[:].rearrange("p n k e -> p n e k"), AX.X, ALU.add).then_inc(gates_ready, 1)
            ve.wait_ge(rank_done, 1)
            link(v.tensor_copy(count[:], bank[2][:, 0:NE]))
            link(v.tensor_scalar(nblk[:, 0, :], count[:], float(P), 1.0, ALU.is_gt, ALU.add))
            link(v.scalar_tensor_tensor(nblk[:, 1, :], count[:], 2.0 * P, nblk[:, 0, :], ALU.is_gt, ALU.add))
            link(v.scalar_tensor_tensor(nblk[:, 0, :], count[:], 3.0 * P, nblk[:, 1, :], ALU.is_gt, ALU.add))
            link(v.tensor_tensor_scan(pend[:], ones[:, 0:NE], nblk[:, 0, :], 0.0, ALU.mult, ALU.add))
            link(v.tensor_tensor(pstart[:], pend[:], nblk[:, 0, :], ALU.subtract))
            link(v.tensor_tensor_scan(start[:], ones[:, 0:NE], count[:], 0.0, ALU.mult, ALU.add))
            link(v.tensor_tensor(start[:], start[:], count[:], ALU.subtract))
            link(v.tensor_tensor(dest[:], start[:].unsqueeze(1).broadcast_to([P, NT, NE]),
                                 bank[1][:, 0:NT * NE].rearrange("p (n e) -> p n e", n=NT), ALU.add))
            link(v.scalar_tensor_tensor(dest[:], dest[:], 1.0, mask[:], ALU.add, ALU.mult))
            link(v.tensor_scalar(dest[:], dest[:], -1.0, None, ALU.add))
            for n in range(NT):
                link(v.tensor_tensor(hot_w[:, n], hot[:, n], dest[:, n, :].unsqueeze(1).broadcast_to([P, TOPK, NE]), ALU.mult))
            link(v.tensor_reduce(my_slot[:], hot_w[:], AX.X, ALU.add))
            link(v.tensor_copy(my_slot_i[:], my_slot[:]))
            link(v.tensor_tensor(pcmp[:], pend[:].unsqueeze(1).broadcast_to([P, NP_TAB, NE]), wide(iota_p[:], NP_TAB, NE), ALU.is_le))
            link(v.tensor_reduce(etab[:], pcmp[:], AX.X, ALU.add))
            link(v.tensor_scalar(etab[:], etab[:], float(NE - 1), None, ALU.min))
            link(v.tensor_copy(etab_i[:], etab[:]))
            link(v.scalar_tensor_tensor(from_pass[:], pstart[:], -float(P), start[:], ALU.mult, ALU.add))
            link(v.tensor_tensor(pcmp[:], iota_e[:].unsqueeze(1).broadcast_to([P, NP_TAB, NE]), wide(etab[:], NP_TAB, NE), ALU.is_equal))
            link(v.tensor_tensor(pcmp[:], pcmp[:], from_pass[:].unsqueeze(1).broadcast_to([P, NP_TAB, NE]), ALU.mult))
            link(v.tensor_reduce(ybase[:], pcmp[:], AX.X, ALU.add))
            link(v.scalar_tensor_tensor(ybase[:], iota_p[:], float(P), ybase[:], ALU.mult, ALU.add))
            link(v.tensor_copy(ybase_i[:], ybase[:]))
            v.tensor_copy(passes_i[:], pend[:, NE - 1:NE]).then_inc(tables_ready, 1)
            ve.wait_ge(gt_done, 1)
            v.tensor_copy(gT[:].rearrange("e n t -> e (n t)"), bank[3][0:NE, :]).then_inc(gt_read, 1)
            for n in range(NT):
                for half in range(2):
                    i = 2 * n + half
                    cs = slice(half * CW, (half + 1) * CW)
                    ve.wait_ge(gb_done, i + 1)
                    if i >= 1:
                        ve.wait_ge(resid_ready, i)
                    v.tensor_tensor(mixt[:], bank[4 + i % 4][:], gate2[:, cs], ALU.mult).then_inc(gb_read, 1)
                    ve.wait_ge(gb_read, i + 1)
                    v.tensor_tensor(resid[:, n, cs], resid[:, n, cs], mixt[:], ALU.add).then_inc(resid_ready, 1)

            def split_low(j):
                ch, q = divmod(j, UPC)
                v.tensor_tensor(w_lo[:, j % SPLITS], ring[:, slot_of(ch), KQ * q:KQ * q + KQ, :],
                                w_hi[:, j % SPLITS].bitcast(F32), ALU.subtract).then_inc(split_lo[j % USEMS], 1)

            def make_pick(dest_col):
                v.tensor_tensor(pick[:], pass_slots[:].unsqueeze(1).broadcast_to([P, NT, P]),
                                dest_col.broadcast_to([P, NT, P]), ALU.is_equal).then_inc(pick_ready, 1)

            def act_low(ch, p1):
                ve.wait_ge(at_hi_ready[ch], p1)
                half = bank[4 + ch % 2][:, 0:256].rearrange("p (k t) -> p k t", k=2)
                v.tensor_tensor(aT_lo[:, 2 * ch:2 * ch + 2], half, aT_hi[:, 2 * ch:2 * ch + 2].bitcast(F32),
                                ALU.subtract).then_inc(at_lo_ready[ch], 1)

            n_passes = ve.value_load(passes_i[0:1, 0:1], min_val=NE, max_val=MAX_PASSES)
            ve.sem_inc(lin_ready[2], 1)
            ve.sem_inc(lin_ready[3], 1)
            ve.sem_inc(act_ready[2], 1)
            ve.sem_inc(act_ready[3], 1)
            for ch in (2, 3):
                ve.sem_inc(at_lo_ready[ch], 1)
            ve.wait_ge(bgu_got, 64)
            odd = bgu[:].rearrange("p (f two) -> p f two", two=2)[:, :, 1]
            link(v.tensor_scalar(odd, odd, 1.0, None, ALU.add))
            link(v.tensor_copy(bgu_hi[:], bgu[:]))
            v.tensor_tensor(bgu_lo[:], bgu[:], bgu_hi[:].bitcast(F32), ALU.subtract).then_inc(bgu_ready, 1)
            link(v.tensor_copy(pass_slots[:], slot_iota[:]))
            make_pick(dest[:, :, 0:1])
            v.tensor_scalar(pick_e[:], expert_of_row[:], 0.0, None, ALU.is_equal).then_inc(pick_e_ready, 1)
            for q in range(UPC):
                ve.wait_ge(split_hi[q], 1)
                split_low(q)
            with ve.Fori(0, n_passes) as p:
                p1, p2 = ve.snap(p + 1), ve.snap(p + 2)
                turn = turns(ve, p)
                e_next = ve.value_load(etab_i[0:1, bass.ds(p1, 1)], min_val=0, max_val=NE - 1)
                for ch in range(1, CHUNKS + 1):
                    cc = ch % CHUNKS
                    for q in range(UPC):
                        j = ch * UPC + q
                        ve.wait_ge(split_hi[j % USEMS], turn[j // USEMS])
                        split_low(cc * UPC + q)
                    if ch <= GU_CHUNKS:
                        c0 = ch - 1
                        gu = bank[c0 % 2][:].rearrange("p (f two) -> p f two", two=2)
                        ve.wait_ge(unit_used[(ch * UPC - 1) % USEMS], turn[(ch * UPC - 1) // USEMS])
                        ve.wait_ge(act_ready[(c0 + 2) % 4], p1)
                        v.tensor_scalar(glu[:, c0 % 2], gu[:, :, 0], LIMIT, None, ALU.min).then_inc(glu_ready[c0], 1)
                        v.tensor_scalar(lin[:, c0 % 2], gu[:, :, 1], 1.0 - LIMIT, 1.0 + LIMIT, ALU.max, ALU.min).then_inc(lin_ready[c0], 1)
                    if ch == 1:
                        ve.wait_ge(gath_lo, p1)
                        v.tensor_scalar(pass_slots[:], slot_iota[:], ybase[:, bass.ds(p1, 1)], None, ALU.add).then_inc(pick_step, 1)
                        ve.wait_ge(pick_step, p1)
                        make_pick(dest[:, :, bass.ds(e_next, 1)])
                    if 2 <= ch <= GU_CHUNKS:
                        act_low(ch - 2, p1)
                    if ch == GU_CHUNKS:
                        act_low(3, p1)
                        v.tensor_scalar(pick_e[:], expert_of_row[:], etab[:, bass.ds(p1, 1)], None, ALU.is_equal).then_inc(pick_e_ready, 1)
            ve.wait_ge(fin_got, 48)
            for n in range(NT):
                rows = ring[:, n].rearrange("p a b -> p (a b)")
                cur = acc[:, n % 2]
                if n >= 2:
                    ve.wait_ge(out_stored[n - 2], 16)
                ve.wait_ge(y_got[n], 16 * TOPK)
                v.tensor_scalar(cur, rows[:, 0:D], gate[:, n, 0:1], None, ALU.mult).then_inc(acc_step, 1)
                for k in range(1, TOPK):
                    ve.wait_ge(acc_step, 6 * n + k)
                    v.scalar_tensor_tensor(cur, rows[:, k * D:(k + 1) * D], gate[:, n, k:k + 1], cur, ALU.mult, ALU.add).then_inc(acc_step, 1)
                ve.wait_ge(acc_step, 6 * n + 4)
                v.tensor_tensor(cur, cur, gate2_f[:], ALU.mult).then_inc(acc_step, 1)
                ve.wait_ge(acc_step, 6 * n + 5)
                v.tensor_tensor(cur, cur, res_f[:, n], ALU.add).then_inc(acc_step, 1)
                ve.wait_ge(fin_ss, n + 1)
                v.tensor_scalar(ssq[:, 4 + n:5 + n], ssq[:, n:n + 1], 1.0 / D, EPS, ALU.mult, ALU.add).then_inc(fin_var, 1)
                ve.wait_ge(fin_std, n + 1)
                link(v.reciprocal(rstd[:, n:n + 1], rstd[:, n:n + 1]))
                v.scalar_tensor_tensor(cur, cur, rstd[:, n:n + 1], gain_f[:], ALU.mult, ALU.mult).then_inc(fin_ready, 1)

        @block.tensor
        def _(pe):
            t = nc.tensor

            def ada(g, i):
                pe.wait_ge(ring_loaded[g % SLOTS], ring_value[g])
                out_bank = bank[i % 2] if i < 4 else bank[i % 4]
                for k in range(NK):
                    mm = t.matmul(out_bank[:], c_rep[:, k, :], ring[:, g % SLOTS, k, :], start=(k == 0), stop=(k == NK - 1))
                mm.then_inc(ada_done, 1)

            pe.wait_ge(consts, N_CONST)
            pe.wait_ge(c_ready, 1)
            for i in range(4):
                if i >= 2:
                    pe.wait_ge(ada_read, i - 1)
                ada(i, i)
            for n in range(NT):
                pe.wait_ge(h_ready, n + 1)
                for half in range(2):
                    if n >= 2:
                        pe.wait_ge(ht_read, 2 * (n - 2) + half + 1)
                    for k in range(4):
                        kk = 4 * half + k
                        mm = t.transpose(bank[2 + 2 * (n % 2) + half][:, k * P:(k + 1) * P], h_row[:, n % 2, kk * P:(kk + 1) * P], ident[:])
                    mm.then_inc(ht_done, 1)
            pe.wait_ge(ht_read, 2 * NT)
            for j, (i, kind, cols, dst, scale) in enumerate(PROJ):
                g = PROJ0 + i
                pe.wait_ge(ring_loaded[g % SLOTS], ring_value[g])
                if j >= 2:
                    pe.wait_ge(proj_read, j - 1)
                w, dstb = ring[:, g % SLOTS], bank[6 + j % 2]
                if kind == "V":
                    c0, c1, tokens = cols
                    for m, t0 in enumerate(tokens):
                        for k in range(NK):
                            mm = t.matmul(dstb[:, m * (c1 - c0):(m + 1) * (c1 - c0)], hT[:, k, t0:t0 + P], w[:, k, c0:c1],
                                          start=(k == 0), stop=(k == NK - 1))
                else:
                    for k in range(NK):
                        mm = t.matmul(dstb[:], w[:, k, cols:cols + P], hT[:, k, :], start=(k == 0), stop=(k == NK - 1))
                mm.then_inc(proj_done, 1)
            pe.wait_ge(lfb_ready, 1)
            for n in range(NT):
                for j in range(n + 1):
                    mm = t.matmul(bank[4][:, n * FOX:(n + 1) * FOX], ones[:] if j < n else tri_incl[:, 0:P], flog[:, j, :],
                                  start=(j == 0), stop=(j == n))
            mm.then_inc(cumf_done, 1)
            for h in range(FOX):
                for j in range(NT):
                    mm = t.matmul(bank[(5, 0, 1, 2)[h]][:, j * P:SEQ], lfb[:, j, h, :], tri_incl[:, 0:SEQ - j * P],
                                  start=(j == 0), stop=(j == NT - 1))
                mm.then_inc(cumf_done, 1)
            pe.wait_ge(cumf_read, 1 + FOX)
            pe.wait_ge(proj_read, len(PROJ))

            def scores(u):
                kind, n, h = ATT[u]
                if u >= 2:
                    pe.wait_ge(score_read, u - 1)
                dst = bank[u % 2]
                if kind == "swa":
                    k0 = 0 if n == 0 else (n - 1) * HD
                    for tt in range(4):
                        for a in range(2):
                            half = slice(HD * a, HD * a + HD)
                            first = HD if n == 0 else 0
                            mm = t.matmul(dst[half, tt * P + first:(tt + 1) * P], qaT[half, tt, n * HD:(n + 1) * HD],
                                          kaT[half, k0:(n + 1) * HD], start=True, stop=True)
                else:
                    q, kk = (qfT, kfT) if kind == "fox" else (qsT, ksT)
                    half = slice(HD * (h % 2), HD * (h % 2) + HD)
                    mm = t.matmul(dst[:, 0:(n + 1) * P], q[half, h // 2, n * P:(n + 1) * P], kk[half, h // 2, 0:(n + 1) * P],
                                  start=True, stop=True)
                mm.then_inc(score_done, 1)

            def transpose_probs(u):
                kind, n, h = ATT[u]
                if kind == "swa":
                    pe.wait_ge(swa_ready, u + 1)
                else:
                    pe.wait_ge(tri_ready, u - FOX0 + 1)
                if u >= 2:
                    pe.wait_ge(pt_read, u - 1)
                dst, b = bank[2 + u % 2], u % 2
                if kind == "swa" and n == 0:
                    for tt in range(4):
                        mm = t.transpose(dst[0:HD, tt * P:(tt + 1) * P], prob[:, b, tt * P + HD:(tt + 1) * P], ident[:])
                else:
                    for m in range(4 if kind == "swa" else n + 1):
                        mm = t.transpose(dst[:, m * P:(m + 1) * P], prob[:, b, m * P:(m + 1) * P], ident[:])
                mm.then_inc(pt_done, 1)

            def times_values(u):
                kind, n, h = ATT[u]
                b = u % 2
                pe.wait_ge(pt_read, u + 1)
                if kind == "swa":
                    dst = bank[4 + (n // 2) % 2]
                    if n % 2 == 0 and n >= 4:
                        pe.wait_ge(o_read_a, n // 2 - 1)
                    rows = HD if n == 0 else P
                    vals = va[:, n // 2] if n % 2 else (va[0:HD, 0] if n == 0 else va_mid[:, n // 2 - 1])
                    q0 = (n % 2) * HD
                    for tt in range(4):
                        for a in range(2):
                            head = tt + 4 * a
                            mm = t.matmul(dst[q0:q0 + HD, head * HD:(head + 1) * HD],
                                          probT[0:rows, b, tt * P + a * HD:tt * P + (a + 1) * HD],
                                          vals[0:rows, a * HD:(a + 1) * HD], start=True, stop=True)
                else:
                    dst = bank[6 + n % 2]
                    vals = vf if kind == "fox" else vs
                    if h == 0 and kind == "fox" and n >= 2:
                        pe.wait_ge(o_read_v, n - 1)
                    if h == 0 and kind == "sb":
                        if n < 2:
                            pe.wait_ge(o_read_v, n + 3)
                        else:
                            pe.wait_ge(o_read_a, NT + n - 1)
                    for m in range(n + 1):
                        mm = t.matmul(dst[:, h * HD:(h + 1) * HD], probT[:, b, m * P:(m + 1) * P], vals[:, m, h * HD:(h + 1) * HD],
                                      start=(m == 0), stop=(m == n))
                mm.then_inc(pv_done, 1)

            scores(0)
            for u in range(NU):
                if u + 1 < NU:
                    scores(u + 1)
                transpose_probs(u)
                if u >= 2:
                    times_values(u - 2)
            times_values(NU - 2)
            times_values(NU - 1)
            pe.wait_ge(score_read, NU)
            pe.wait_ge(pt_read, NU)
            for i in range(4, 12):
                if i >= 8:
                    pe.wait_ge(ada_read, i - 3)
                ada(ADA1 + i - 4, i)
            for n in range(NT):
                pe.wait_ge(o_norm, n + 1)
                for half in range(2):
                    if n >= 2:
                        pe.wait_ge(ot_read, 2 * (n - 2) + half + 1)
                    for k in range(4):
                        kk = 4 * half + k
                        mm = t.transpose(bank[4 + 2 * (n % 2) + half][:, k * P:(k + 1) * P], o[:, n, kk * P:(kk + 1) * P], ident[:])
                    mm.then_inc(ot_done, 1)
            pe.wait_ge(ada_read, 12)
            for n in range(NT):
                pe.wait_ge(ot_read, 2 * n + 2)
                for half in range(2):
                    g, i = OUT0 + half, 2 * n + half
                    pe.wait_ge(ring_loaded[g % SLOTS], ring_value[g])
                    if i >= 4:
                        pe.wait_ge(mix_read, i - 3)
                    for k in range(NK):
                        mm = t.matmul(bank[i % 4][:], oT[:, k, n * P:(n + 1) * P], ring[:, g % SLOTS, k, :],
                                      start=(k == 0), stop=(k == NK - 1))
                    mm.then_inc(mix_done, 1)
            pe.wait_ge(ot_read, 2 * NT)
            for n in range(NT):
                pe.wait_ge(h2_ready, n + 1)
                for half in range(2):
                    if n >= 2:
                        pe.wait_ge(h2t_read, 2 * (n - 2) + half + 1)
                    for k in range(4):
                        kk = 4 * half + k
                        mm = t.transpose(bank[4 + 2 * (n % 2) + half][:, k * P:(k + 1) * P], h2_row[:, n % 2, kk * P:(kk + 1) * P], ident[:])
                    mm.then_inc(h2t_done, 1)
            pe.wait_ge(mix_read, 2 * NT)
            pe.wait_ge(h2t_read, 2 * NT)
            for n in range(NT):
                for k in range(NK):
                    mm = t.matmul(bank[0][:, n * NE:(n + 1) * NE], h2T[:, k, n * P:(n + 1) * P], rw[:, k, :],
                                  start=(k == 0), stop=(k == NK - 1))
            mm.then_inc(router_done, 1)
            pe.wait_ge(mask_ready, 1)
            for n in range(NT):
                for j in range(n + 1):
                    t.matmul(bank[1][:, n * NE:(n + 1) * NE], ones[:] if j < n else tri_strict[:], mask[:, j, :],
                             start=(j == 0), stop=(j == n))
            for n in range(NT):
                mm = t.matmul(bank[2][:, 0:NE], ones[:], mask[:, n, :], start=(n == 0), stop=(n == NT - 1))
            mm.then_inc(rank_done, 1)
            pe.wait_ge(gates_ready, 1)
            for n in range(NT):
                mm = t.transpose(bank[3][0:NE, n * P:(n + 1) * P], gates_e[:, n, :], ident[:])
            mm.then_inc(gt_done, 1)
            pe.wait_ge(gt_read, 1)
            pe.wait_ge(bdn_got, 16)
            for n in range(NT):
                for half in range(2):
                    i = 2 * n + half
                    if i >= 4:
                        pe.wait_ge(gb_read, i - 3)
                    t.matmul(bank[4 + i % 4][:], gT[:, n, :], bdn[:, half * CW:(half + 1) * CW], start=True, stop=True).then_inc(gb_done, 1)
            pe.wait_ge(gb_read, 2 * NT)

            def gather(part, done):
                for k in range(NK):
                    for n in range(NT):
                        mm = t.matmul(bank[6 + k // 4][:, (k % 4) * P:(k % 4 + 1) * P], part[:, n, k * P:(k + 1) * P],
                                      pick[:, n, :], start=(n == 0), stop=(n == NT - 1))
                mm.then_inc(done, 1)

            def unit(dst, hi, lo, j, turn, first):
                pe.wait_ge(split_lo[j % USEMS], turn[j // USEMS])
                ch, q = divmod(j, UPC)
                for kk in range(KQ):
                    k = KQ * q + kk
                    w1, w2 = w_hi[:, j % SPLITS, kk, :], w_lo[:, j % SPLITS, kk, :]
                    t.matmul(dst[:], hi[:, k, :], w1, start=(first and k == 0), stop=False)
                    t.matmul(dst[:], hi[:, k, :], w2, start=False, stop=False)
                    mm = t.matmul(dst[:], lo[:, k, :], w1, start=False, stop=(k == NK - 1))
                mm.then_inc(unit_used[j % USEMS], 1)

            def act_transpose(ch, value):
                pe.wait_ge(act_ready[ch], value)
                pe.wait_ge(at_lo_ready[(ch + 2) % 4], pass_value[0])
                for m in range(2):
                    mm = t.transpose(bank[4 + ch % 2][:, m * P:(m + 1) * P],
                                     act_out[:, ch % 2, m * P:(m + 1) * P], ident[:])
                mm.then_inc(at_done[ch], 1)

            n_passes = pe.value_load(passes_i[0:1, 0:1], min_val=NE, max_val=MAX_PASSES)
            for ch in (2, 3):
                pe.sem_inc(at_done[ch], 1)
            pe.wait_ge(h2_lo_ready, NT)
            pe.wait_ge(h2_hi_ready, NT)
            pe.wait_ge(pick_ready, 1)
            gather(h2_hi, gath_hi)
            pe.wait_ge(xt_hi_ready, 1)
            gather(h2_lo, gath_lo)
            pe.wait_ge(bgu_ready, 1)
            pass_value = [None]
            with pe.Fori(0, n_passes) as p:
                p1, p2 = pe.snap(p + 1), pe.snap(p + 2)
                turn = turns(pe, p)
                pass_value[0] = p1
                pe.wait_ge(xt_lo_ready, p1)
                pe.wait_ge(pick_e_ready, p1)
                for ch in range(GU_CHUNKS):
                    dst = bank[ch % 2]
                    rows = slice(NE * ch, NE * ch + NE)
                    pe.wait_ge(lin_ready[(ch + 2) % 4], p1)
                    t.matmul(dst[:], pick_e[rows, :], bgu_hi[rows, :], start=True, stop=False)
                    t.matmul(dst[:], pick_e[rows, :], bgu_lo[rows, :], start=False, stop=False)
                    for q in range(UPC):
                        unit(dst, xT_hi, xT_lo, ch * UPC + q, turn, False)
                    if ch >= 1:
                        act_transpose(ch - 1, p2 if ch - 1 >= 2 else p1)
                pe.wait_ge(pick_ready, p2)
                gather(h2_hi, gath_hi)
                act_transpose(3, p2)
                pe.wait_ge(xt_hi_ready, p2)
                gather(h2_lo, gath_lo)
                for ch in range(GU_CHUNKS):
                    pe.wait_ge(at_lo_ready[ch], p2 if ch >= 2 else p1)
                for hf in range(DN_CHUNKS):
                    pe.wait_ge(y_ready[hf], p1)
                    for q in range(UPC):
                        unit(bank[2 + hf], aT_hi, aT_lo, (GU_CHUNKS + hf) * UPC + q, turn, True)


_INS = ['x', 'c', 'norm1_gain', 'norm2_gain', 'ada_w', 'ada_b', 'w_in', 'attn_sinks', 'forget_bias', 'mix_out_gain',
        'w_out', 'router_w', 'router_b', 'expert_w_gate_up', 'expert_b_gate_up', 'expert_w_down', 'expert_b_down',
        'final_gain']


def kernel(**inputs):
    import numpy as _np
    import concourse.bacc as _bacc
    from concourse import mybir as _mybir
    from concourse.bass_utils import run_bass_kernel_spmd as _run

    nc = _bacc.Bacc("TRN2", target_bir_lowering=False, num_devices=1)
    arrays, args = {}, []
    for name in _INS:
        a = _np.ascontiguousarray(inputs[name])
        arrays[f"in_{name}_dram"] = a
        args.append(nc.dram_tensor(f"in_{name}_dram", a.shape, _mybir.dt.from_np(a.dtype), kind="ExternalInput").ap())
    args.append(nc.dram_tensor("out_0_dram", (1, SEQ, D), _mybir.dt.float32, kind="ExternalOutput").ap())
    build_program(nc, *args)
    r = _run(nc, [arrays], core_ids=[0])
    return r.results[0]["out_0_dram"]
```

```python
from contextlib import ExitStack

import concourse.bass as bass
from concourse import mybir

F32 = mybir.dt.float32
F32R = mybir.dt.float32r
I32 = mybir.dt.int32
U32 = mybir.dt.uint32
ALU = mybir.AluOpType
ACT = mybir.ActivationFunctionType
AX = mybir.AxisListType

P = 128
SEQ, D = 512, 1024
NT, NK = SEQ // P, D // P
HD = 64
CW = 512
SWA_Q, SWA_KV, FOX, SB = 8, 2, 4, 4
HEADS = SWA_Q + FOX + SB
NE, TOPK = 32, 4
MAX_PASSES = NE + (SEQ * TOPK - NE) // P
NP_TAB = MAX_PASSES + 1
AB = 3
LIMIT, ALPHA, EPS = 7.0, 1.702, 1e-5
NEG = -1e30
QSCALE = HD ** -0.5
SLOTS = 6
KQ = 2
SPLITS = 8
GU_CHUNKS, DN_CHUNKS = 2 * D // CW, D // CW
CHUNKS = GU_CHUNKS + DN_CHUNKS
UPC = NK // KQ
UNITS = CHUNKS * UPC
POOL_Q = 1
USEMS = 8
UTURNS = UNITS // USEMS
LEAD = 2

C_QA, C_KA, C_VA = 0, 512, 640
C_QF, C_KF, C_VF, C_FL = 768, 1024, 1280, 1536
C_QS, C_KS, C_VS = 1540, 1796, 2052
KB = 1024


def build_program(nc, x, c, norm1_gain, norm2_gain, ada_w, ada_b, w_in, attn_sinks, forget_bias,
                  mix_out_gain, w_out, router_w, router_b, w_gu, b_gu, w_dn, b_dn, final_gain, out):
    ctx = ExitStack()
    with ctx:
        base = (nc.sbuf_base + 31) // 32 * 32

        def at(name, shape, dt, offset):
            return nc.alloc_sbuf_tensor_at(name, shape, dt, offset=base + offset)

        ring = at("ring", [P, SLOTS, NK, CW], F32, 0)
        cursor = [96 * KB]

        def small(name, shape, dt):
            size = 4
            for s in shape[1:]:
                size *= s
            t = at(name, shape, dt, cursor[0])
            cursor[0] += (size + 31) // 32 * 32
            return t

        ident = small("ident", [P, P], F32)
        ones = small("ones", [P, P], F32)
        tok_id = small("tok_id", [P, NT], F32)
        slot_iota = small("slot_iota", [P, P], F32)
        expert_of_row = small("expert_of_row", [P, P], F32)
        dest = small("dest", [P, NT, NE], F32)
        etab = small("etab", [P, NP_TAB], F32)
        etab_i = small("etab_i", [P, NP_TAB], I32)
        iota_p = small("iota_p", [P, NP_TAB], F32)
        iota_e = small("iota_e", [P, NE], F32)
        ybase = small("ybase", [P, NP_TAB], F32)
        ybase_i = small("ybase_i", [P, NP_TAB], I32)
        warm = small("warm", [P, 8], F32)
        passes_i = small("passes_i", [P, 1], I32)
        my_slot = small("my_slot", [P, NT, TOPK], F32)
        my_slot_i = small("my_slot_i", [P, NT, TOPK], I32)
        gate = small("gate", [P, NT, TOPK], F32)
        ssq = small("ssq", [P, 8], F32)
        rstd = small("rstd", [P, 8], F32)
        neg_sink = small("neg_sink", [P, 4], F32)
        assert cursor[0] <= 101 * KB, cursor[0]
        R0 = 101 * KB
        R1, R2, R3, R4 = R0 + 16 * KB, R0 + 32 * KB, R0 + 48 * KB, R0 + 86 * KB
        x_in = at("x_in", [P, NT, D], F32, R0)
        o = at("o", [P, NT, D], F32, R0)
        h2_row = at("h2_row", [P, NT, D], F32, R0)
        mod1 = at("mod1", [P, 2 * D], F32, R1)
        cumf_row = at("cumf_row", [P, FOX, SEQ], F32, R1)
        alibi = at("alibi", [P, 4, P], F32, R1 + 10 * KB)
        c_rep = at("c_rep", [P, NK, P], F32, R1 + 12 * KB)
        stay_from = at("stay_from", [P, SEQ + 8], F32, R1 + 12 * KB)
        hT = at("hT", [P, NK, SEQ], F32, R2)
        oT = at("oT", [P, NK, SEQ], F32, R2)
        h2T = at("h2T", [P, NK, SEQ], F32, R2)
        qaT = at("qaT", [P, 4, SEQ], F32, R3)
        kaT = at("kaT", [P, SEQ], F32, R3 + 8 * KB)
        qfT = at("qfT", [P, 2, SEQ], F32, R3 + 10 * KB)
        kfT = at("kfT", [P, 2, SEQ], F32, R3 + 14 * KB)
        qsT = at("qsT", [P, 2, SEQ], F32, R3 + 18 * KB)
        ksT = at("ksT", [P, 2, SEQ], F32, R3 + 22 * KB)
        va = at("va", [P, NT, 2 * HD], F32, R3 + 26 * KB)
        va_mid = at("va_mid", [P, 3, 2 * HD], F32, R3 + 28 * KB)
        vf = at("vf", [P, NT, 4 * HD], F32, R3 + 29 * KB + 512)
        vs = at("vs", [P, NT, 4 * HD], F32, R3 + 33 * KB + 512)
        mod2 = at("mod2", [P, 4 * D], F32, R3)
        resid = at("resid", [P, NT, D], F32, R3 + 16 * KB)
        head_gain = at("head_gain", [P, NK], F32, R3 + 37 * KB + 512)
        gain = at("gain", [P, D], F32, R4)
        h_row = at("h_row", [P, 2, D], F32, R4 + 4 * KB)
        ada_acc = at("ada_acc", [P, 2, CW], F32, R4)
        mod_row = at("mod_row", [1, 2, CW], F32, R4 + 12 * KB)
        score = at("score", [P, AB, SEQ], F32, R4)
        soft = at("soft", [P, AB, SEQ], F32, R4 + 6 * KB)
        prob = at("prob", [P, AB, SEQ], F32, R2)
        probT = at("probT", [P, AB, SEQ], F32, R2 + 6 * KB)
        tri_incl = at("tri_incl", [P, SEQ], F32, R4 + 16 * KB)
        tri_strict = at("tri_strict", [P, P], F32, R4 + 18 * KB)
        low_strict = at("low_strict", [P, P], F32, R4 + 18 * KB + 512)
        causal_add = at("causal_add", [P, P], F32, R4 + 19 * KB)
        tail = R4 + 20 * KB
        flog = at("flog", [P, NT, FOX], F32, tail)
        fwork = at("fwork", [P, NT, FOX], F32, tail + 64)
        fbias = at("fbias", [P, FOX], F32, tail + 128)
        cumf_col = at("cumf_col", [P, NT, FOX], F32, tail + 160)
        mrow = at("mrow", [P, 40, 4], F32, tail + 224)
        tail2 = R3 + 37 * KB + 544
        sinkd = at("sinkd", [P, 8, 4], F32, tail2)
        lrow = at("lrow", [P, 8, 4], F32, tail2 + 128)
        lfox = at("lfox", [P, NT, FOX], F32, tail2 + 256)
        mtmp = at("mtmp", [P, 4], F32, tail2 + 320)
        c_col = at("c_col", [P, 4, NK], F32, tail2 + 352)
        assert base + tail + 224 + 640 <= nc.sbuf_usable_end
        osq = at("osq", [P, D], F32, R4)
        hss = at("hss", [P, NT, HEADS], F32, R4 + 4 * KB)
        gain2 = at("gain2", [P, D], F32, R4 + 12 * KB + 512)
        lfb = at("lfb", [P, NT, FOX, P], F32, R4 + 4 * KB)
        rw = at("rw", [P, NK, NE], F32, R3 + 32 * KB)
        rb = at("rb", [P, NE], F32, R3 + 33 * KB)
        logit = at("logit", [P, NT, NE], F32, R3 + 33 * KB + 128)
        top = at("top", [P, NT, 8], F32, R3 + 33 * KB + 640)
        topi = at("topi", [P, NT, 8], U32, R3 + 33 * KB + 768)
        topf = at("topf", [P, NT, TOPK], F32, R3 + 33 * KB + 896)
        hot = at("hot", [P, NT, TOPK, NE], F32, R3 + 34 * KB + 128)
        mask = at("mask", [P, NT, NE], F32, R3 + 36 * KB + 128)
        gates_e = at("gates_e", [P, NT, NE], F32, R3 + 36 * KB + 640)
        gsum = at("gsum", [P, NT, 2], F32, R3 + 37 * KB + 128)
        rest = R2
        hot_w = at("hot_w", [P, NT, TOPK, NE], F32, rest)
        count = at("count", [P, NE], F32, rest + 2 * KB)
        nblk = at("nblk", [P, 2, NE], F32, rest + 2 * KB + 128)
        pend = at("pend", [P, NE], F32, rest + 2 * KB + 384)
        pstart = at("pstart", [P, NE], F32, rest + 2 * KB + 512)
        start = at("start", [P, NE], F32, rest + 2 * KB + 640)
        from_pass = at("from_pass", [P, NE], F32, rest + 2 * KB + 768)
        pcmp = at("pcmp", [P, NP_TAB, NE], F32, rest + 3 * KB + 256)
        gT = at("gT", [NE, NT, P], F32, rest + 9 * KB + 256)
        bdn = at("bdn", [NE, D], F32, R1 + 8 * KB)
        bgu = at("bgu", [P, CW], F32, R1 + 12 * KB)
        mixt = at("mixt", [P, CW], F32, R1 + 14 * KB)
        m = [R0]

        def moe(name, shape, dt):
            size = 4
            for s in shape[1:]:
                size *= s
            t = at(name, shape, dt, m[0])
            m[0] += size
            return t

        w_hi = moe("w_hi", [P, SPLITS, KQ, CW], F32R)
        w_lo = moe("w_lo", [P, SPLITS, KQ, CW], F32R)
        aT_hi = moe("aT_hi", [P, NK, P], F32R)
        aT_lo = moe("aT_lo", [P, NK, P], F32R)
        glu = moe("glu", [P, 2, CW // 2], F32)
        lin = moe("lin", [P, 2, CW // 2], F32)
        sig = moe("sig", [P, 2, CW // 2], F32)
        prod = moe("prod", [P, 2, CW // 2], F32)
        act_out = moe("act_out", [P, 2, CW // 2], F32)
        y_row = moe("y_row", [P, D], F32)
        assert m[0] == R4, (m[0], R4)
        x_rows = moe("x_rows", [P, D], F32)
        xT_hi = moe("xT_hi", [P, NK, P], F32R)
        xT_lo = moe("xT_lo", [P, NK, P], F32R)
        bgu_hi = moe("bgu_hi", [P, CW], F32R)
        bgu_lo = moe("bgu_lo", [P, CW], F32R)
        pick = moe("pick", [P, NT, P], F32)
        ids = moe("ids", [P, 8], I32)
        pass_slots = moe("pass_slots", [P, P], F32)
        pick_e = moe("pick_e", [P, P], F32R)
        assert base + m[0] <= nc.sbuf_usable_end, (base + m[0], nc.sbuf_usable_end)
        y_tok = ring
        res_f = at("res_f", [P, NT, D], F32, R2)
        gate2_f = at("gate2_f", [P, D], F32, R2 + 16 * KB)
        gain_f = at("gain_f", [P, D], F32, R2 + 20 * KB)
        acc = at("acc", [P, 2, D], F32, R2 + 24 * KB)
        junk_f = at("junk_f", [P, D], F32, R2 + 32 * KB)

        bank = [ctx.enter_context(nc.psum_tensor(f"bank{i}", [P, 512], F32)) for i in range(8)]

        y_dram = nc.dram_tensor("y_slots", [SEQ * TOPK + P, D], F32, kind="Internal").ap()
        h2_dram = nc.dram_tensor("h2_rows", [SEQ, D], F32, kind="Internal").ap()
        res_dram = nc.dram_tensor("residual", [NT, P, D], F32, kind="Internal").ap()
        mod_dram = nc.dram_tensor("mod_row_dram", [1, 4 * D], F32, kind="Internal").ap()

        def sem(name):
            return ctx.enter_context(nc.semaphore(name))

        ring_loaded = [sem(f"ring_loaded{i}") for i in range(SLOTS)]
        (consts, c_in, x_got, gain_got, mod1_bias, small_got, late_got, x_again, bdn_got, bgu_got) = (sem(n) for n in (
            "consts", "c_in", "x_got", "gain_got", "mod1_bias", "small_got", "late_got", "x_again", "bdn_got", "bgu_got"))
        dve_chain, act_chain = sem("dve_chain"), sem("act_chain")
        c_sig, c_ready = sem("c_sig"), sem("c_ready")
        ssq_ready, var_ready, std_ready = sem("ssq_ready"), sem("var_ready"), sem("std_ready")
        ada_done, ada_read = sem("ada_done"), sem("ada_read")
        h_ready, ht_done, ht_read = sem("h_ready"), sem("ht_done"), sem("ht_read")
        proj_done, proj_read = sem("proj_done"), sem("proj_read")
        fz_ready, fl_ready, lfb_ready, cumf_done, cumf_read = (sem(n) for n in (
            "fz_ready", "fl_ready", "lfb_ready", "cumf_done", "cumf_read"))
        score_done, score_read, max_ready, exp_ready, swa_ready, tri_ready, sb_read, stick_ready = (sem(n) for n in (
            "score_done", "score_read", "max_ready", "exp_ready", "swa_ready", "tri_ready", "sb_read", "stick_ready"))
        acc_ready, sum_done, row_ready, row_stored = (sem(n) for n in ("acc_ready", "sum_done", "row_ready", "row_stored"))
        bias_got = [sem(f"bias_got{i}") for i in range(2)]
        pt_done, pt_read, pv_done, o_read_a, o_read_v = (sem(n) for n in ("pt_done", "pt_read", "pv_done", "o_read_a", "o_read_v"))
        hss_ready, hstd_ready, o_norm, ot_done, ot_read = (sem(n) for n in ("hss_ready", "hstd_ready", "o_norm", "ot_done", "ot_read"))
        mix_done, mix_read, x2_ready = sem("mix_done"), sem("mix_read"), sem("x2_ready")
        h2_ready, h2t_done, h2t_read, h2_stored = (sem(n) for n in ("h2_ready", "h2t_done", "h2t_read", "h2_stored"))
        router_done, gate_z, gate_e, gates_ready, mask_ready, rank_done, tables_ready = (sem(n) for n in (
            "router_done", "gate_z", "gate_e", "gates_ready", "mask_ready", "rank_done", "tables_ready"))
        bdn_ready = sem("bdn_ready")
        gt_done, gt_read, gb_done, gb_read, resid_ready, res_stored, bgu_ready = (sem(n) for n in (
            "gt_done", "gt_read", "gb_done", "gb_read", "resid_ready", "res_stored", "bgu_ready"))
        split_hi = [sem(f"split_hi{i}") for i in range(USEMS)]
        split_lo = [sem(f"split_lo{i}") for i in range(USEMS)]
        unit_used = [sem(f"unit_used{i}") for i in range(USEMS)]
        pick_step, pick_ready, pick_e_ready = sem("pick_step"), sem("pick_ready"), sem("pick_e_ready")
        ids_done, ids_ready, x_rows_got, xt_done, xt_hi_ready, xt_lo_ready = (sem(n) for n in (
            "ids_done", "ids_ready", "x_rows_got", "xt_done", "xt_hi_ready", "xt_lo_ready"))
        glu_ready = sem("glu_ready")
        lin_ready = [sem(f"lin_ready{i}") for i in range(GU_CHUNKS)]
        sig_ready = sem("sig_ready")
        prod_ready = sem("prod_ready")
        act_ready = [sem(f"act_ready{i}") for i in range(GU_CHUNKS)]
        at_done = [sem(f"at_done{i}") for i in range(GU_CHUNKS)]
        at_hi_ready = [sem(f"at_hi_ready{i}") for i in range(GU_CHUNKS)]
        at_lo_ready = [sem(f"at_lo_ready{i}") for i in range(GU_CHUNKS)]
        y_ready = [sem(f"y_ready{i}") for i in range(DN_CHUNKS)]
        y_stored = sem("y_stored")
        experts_over = sem("experts_over")
        fin_got, acc_step, fin_ss, fin_var, fin_std, fin_ready = (sem(n) for n in (
            "fin_got", "acc_step", "fin_ss", "fin_var", "fin_std", "fin_ready"))
        y_got = [sem(f"y_got{i}") for i in range(NT)]
        out_stored = [sem(f"out_stored{i}") for i in range(2)]

        ada_v = ada_w[0].rearrange("(k p) n -> p k n", p=P)
        win_v = w_in[0].rearrange("(k p) n -> p k n", p=P)
        wout_v = w_out[0].rearrange("(k p) n -> p k n", p=P)

        PROJ = [(0, "T", t * P, qaT[:, t, :], QSCALE) for t in range(4)]
        PROJ += [
            (1, "T", 0, kaT[:], 1.0),
            (1, "V", (P, 2 * P, [0, P, 2 * P, 3 * P]), va[:], 1.0),
            (1, "V", (P, 2 * P, [HD, HD + P, HD + 2 * P]), va_mid[:], 1.0),
            (1, "T", 256, qfT[:, 0, :], QSCALE),
            (1, "T", 384, qfT[:, 1, :], QSCALE),
        ]
        PROJ += [(2, "V", (0, 256 + FOX, [n * P]), (vs[:, n, :], flog[:, n, :]), 1.0) for n in range(NT)]
        PROJ += [
            (3, "T", 0, kfT[:, 0, :], 1.0),
            (3, "T", P, kfT[:, 1, :], 1.0),
            (3, "V", (256, 512, [0, P]), vf[:, 0:2, :], 1.0),
            (3, "V", (256, 512, [2 * P, 3 * P]), vf[:, 2:4, :], 1.0),
        ]
        PROJ += [(4, "T", j * P, t, s) for j, (t, s) in enumerate((
            (qsT[:, 0, :], QSCALE), (qsT[:, 1, :], QSCALE), (ksT[:, 0, :], 1.0), (ksT[:, 1, :], 1.0)))]

        def ada_chunk(i):
            return [(0, CW, ada_v[:, :, i * CW:(i + 1) * CW])]

        STREAM = [(ada_chunk(i), ada_done, i + 1) for i in range(4)]
        proj_chunk, ada2_chunk = [], []
        win_parts = [
            [((2 * t + h) * HD, (2 * t + h + 1) * HD, win_v[:, :, C_QA + (4 * h + t) * HD:C_QA + (4 * h + t + 1) * HD])
             for t in range(4) for h in range(2)],
            [(0, CW, win_v[:, :, C_KA:C_KA + CW])],
            [(0, 256, win_v[:, :, C_VS:C_VS + 256]), (256, 256 + FOX, win_v[:, :, C_FL:C_FL + FOX])],
            [(0, CW, win_v[:, :, C_KF:C_KF + CW])],
            [(0, CW, win_v[:, :, C_QS:C_QS + CW])],
        ]
        for i, parts in enumerate(win_parts):
            proj_chunk.append(len(STREAM))
            STREAM.append((parts, proj_done, sum(1 for g in PROJ if g[0] <= i)))
            for _ in range(1 if i in (0, 4) else 2):
                m = len(ada2_chunk)
                ada2_chunk.append(len(STREAM))
                STREAM.append((ada_chunk(4 + m), acc_ready, m + 1))
        OUT0 = len(STREAM)
        STREAM += [([(0, CW, wout_v[:, :, i * CW:(i + 1) * CW])], mix_done, 2 * NT) for i in range(2)]
        G0 = len(STREAM)
        loads = [0] * SLOTS
        ring_value = []
        for g, (parts, _, _) in enumerate(STREAM):
            loads[g % SLOTS] += len(parts)
            ring_value.append(16 * loads[g % SLOTS])

        def slot_of(ch):
            return (G0 + ch) % SLOTS

        ADA_STEPS = [(m, k) for m in range(len(ada2_chunk)) for k in range(NK)]
        PER_JOB = -(-len(ADA_STEPS) // (len(PROJ) - 1))

        def ada_chunks_over(j):
            return min((j + 1) * PER_JOB, len(ADA_STEPS)) // NK

        load0 = [loads[slot_of(ch)] + 1 for ch in range(CHUNKS)]

        def expert_chunk(e, ch):
            src, n = (w_gu, ch) if ch < GU_CHUNKS else (w_dn, ch - GU_CHUNKS)
            return src[0, bass.ds(e, 1)].rearrange("a (k p) n -> p (a k) n", p=P)[:, :, n * CW:(n + 1) * CW]

        ATT = [("swa", ch, 0) for ch in range(SEQ // HD)]
        FOX0 = len(ATT)
        ATT += [("fox", n, h) for n in range(NT) for h in range(FOX)]
        SB0 = len(ATT)
        ATT += [("sb", n, h) for n in range(NT) for h in range(SB)]
        NU = len(ATT)
        N_CONST = 19

        def turns(eng, p):
            return [eng.snap(p * UTURNS + (i + 1)) for i in range(UTURNS + 1)]

        block = ctx.enter_context(nc.Block())

        @block.sync
        def _(sp):
            for g, (parts, _, _) in enumerate(STREAM):
                s = g % SLOTS
                if g >= SLOTS:
                    sp.wait_ge(STREAM[g - SLOTS][1], STREAM[g - SLOTS][2])
                for a, b, src in parts:
                    sp.dma_start(ring[:, s, :, a:b], src).then_inc(ring_loaded[s], 16)
            for ch in range(CHUNKS):
                g = G0 + ch - SLOTS
                sp.wait_ge(STREAM[g][1], STREAM[g][2])
                sp.dma_start(ring[:, slot_of(ch)], expert_chunk(0, ch)).then_inc(ring_loaded[slot_of(ch)], 16)
            sp.wait_ge(tables_ready, 1)
            n_passes = sp.value_load(passes_i[0:1, 0:1], min_val=NE, max_val=MAX_PASSES)
            with sp.Fori(1, n_passes + 1) as p:
                e_now = sp.value_load(etab_i[0:1, bass.ds(p, 1)], min_val=0, max_val=NE - 1)
                e_before = sp.value_load(etab_i[0:1, bass.ds(p - 1, 1)], min_val=0, max_val=NE - 1)
                done = [sp.snap(p * UTURNS + (i + 1 - UTURNS)) for i in range(UTURNS)]
                before = {v: sp.snap(p * 16 + (v - 1) * 16) for v in sorted(set(load0))}
                with sp.If(e_now != e_before):
                    for ch in range(CHUNKS):
                        src = expert_chunk(e_now, ch)
                        for last in (UPC * ch + POOL_Q, UPC * ch + UPC - 1):
                            sp.wait_ge(split_lo[last % USEMS], done[last // USEMS])
                        sp.dma_start(ring[:, slot_of(ch)], src).then_inc(ring_loaded[slot_of(ch)], 16)
                with sp.Else():
                    for ch in range(CHUNKS):
                        sp.wait_ge(ring_loaded[slot_of(ch)], before[load0[ch]])
                        sp.sem_inc(ring_loaded[slot_of(ch)], 16)
                sp.nop()

        @block.gpsimd
        def _(pool):
            g = nc.gpsimd
            g.memset(ident[:], 0.0).then_inc(consts, 1)
            g.memset(ones[:], 1.0).then_inc(consts, 1)
            g.memset(tri_incl[:], 1.0).then_inc(consts, 1)
            g.memset(tri_strict[:], 1.0).then_inc(consts, 1)
            g.memset(low_strict[:], 1.0).then_inc(consts, 1)
            g.memset(causal_add[:], 0.0).then_inc(consts, 1)
            pool.wait_ge(consts, 6)
            for t, cols, base_v, cm, step, keep, fill in (
                    (ident, P, 0, 1, -1, ALU.not_equal, 1.0),
                    (tri_incl, SEQ, 0, -1, 1, ALU.is_ge, 0.0),
                    (tri_strict, P, -1, -1, 1, ALU.is_ge, 0.0),
                    (low_strict, P, -1, 1, -1, ALU.is_ge, 0.0),
                    (causal_add, P, 0, 1, -1, ALU.is_ge, NEG)):
                g.affine_select(out=t[:, 0:cols], in_=t[:, 0:cols], pattern=[[step, cols]], compare_op=keep,
                                fill=fill, base=base_v, channel_multiplier=cm).then_inc(consts, 1)
            pool.wait_ge(consts, 11)
            for h in range(2):
                g.iota(alibi[64 * h:64 * h + 64, 3, :], [[-1, P]], base=HD, channel_multiplier=1,
                       allow_small_or_imprecise_dtypes=True).then_inc(consts, 1)
                pool.wait_ge(consts, 12 + h)
            g.iota(tok_id[:], [[P, NT]], base=0, channel_multiplier=1,
                   allow_small_or_imprecise_dtypes=True).then_inc(consts, 1)
            g.iota(slot_iota[:], [[1, P]], base=0, channel_multiplier=0,
                   allow_small_or_imprecise_dtypes=True).then_inc(consts, 1)
            for h in range(4):
                pool.wait_ge(consts, 15 + h)
                g.iota(expert_of_row[32 * h:32 * h + 32, :], [[0, P]], base=0, channel_multiplier=1,
                       allow_small_or_imprecise_dtypes=True).then_inc(consts, 1)
            pool.wait_ge(consts, N_CONST)
            g.iota(iota_e[:], [[1, NE]], base=0, channel_multiplier=0,
                   allow_small_or_imprecise_dtypes=True).then_inc(consts, 1)
            g.iota(iota_p[:], [[1, NP_TAB]], base=0, channel_multiplier=0,
                   allow_small_or_imprecise_dtypes=True).then_inc(consts, 1)


            def fetch_tokens():
                g.indirect_dma_start(
                    out=x_rows[:], out_offset=None, in_=h2_dram, in_offset=bass.IndirectOffsetOnAxis(ap=ids[:, 0:1], axis=0),
                    bounds_check=SEQ - 1, oob_is_err=True).then_inc(x_rows_got, 16)

            def split_low(j):
                ch, q = divmod(j, UPC)
                g.tensor_tensor(w_lo[:, j % SPLITS], ring[:, slot_of(ch), KQ * q:KQ * q + KQ, :],
                                w_hi[:, j % SPLITS].bitcast(F32), ALU.subtract).then_inc(split_lo[j % USEMS], 1)

            pool.wait_ge(h2_stored, 16 * NT)
            pool.wait_ge(ids_ready, 1)
            fetch_tokens()
            pool.wait_ge(tables_ready, 1)
            for ch in range(LEAD):
                pool.wait_ge(split_hi[ch * UPC + POOL_Q], 1)
                split_low(ch * UPC + POOL_Q)
            n_passes = pool.value_load(passes_i[0:1, 0:1], min_val=NE, max_val=MAX_PASSES)
            with pool.Fori(0, n_passes) as p:
                p1, p2 = pool.snap(p + 1), pool.snap(p + 2)
                nth = [pool.snap(p * GU_CHUNKS + (ch + 1)) for ch in range(GU_CHUNKS)]
                turn = turns(pool, p)
                for step in range(1, CHUNKS + 1):
                    ch = step - 1
                    if ch < GU_CHUNKS:
                        pool.wait_ge(lin_ready[ch], p2 if ch >= 2 else p1)
                        g.tensor_tensor(prod[:, ch % 2], glu[:, ch % 2], lin[:, ch % 2], ALU.mult).then_inc(prod_ready, 1)
                        pool.wait_ge(prod_ready, nth[ch])
                        pool.wait_ge(sig_ready, nth[ch])
                        pool.wait_ge(at_done[(ch + 2) % 4], p1)
                        if ch == 1:
                            pool.wait_ge(xt_done, p1)
                            pool.wait_ge(ids_ready, p2)
                        g.tensor_tensor(act_out[:, ch % 2], prod[:, ch % 2], sig[:, ch % 2], ALU.mult).then_inc(act_ready[ch], 1)
                        if ch == 1:
                            fetch_tokens()
                    j = (step + LEAD - 1) * UPC + POOL_Q
                    pool.wait_ge(split_hi[j % USEMS], turn[j // USEMS])
                    split_low(j % UNITS)
            pool.wait_ge(experts_over, 1)
            for n in range(NT):
                for k in range(TOPK):
                    g.indirect_dma_start(
                        out=ring[:, n].rearrange("p a b -> p (a b)")[:, k * D:(k + 1) * D], out_offset=None,
                        in_=y_dram[0:SEQ * TOPK, :], in_offset=bass.IndirectOffsetOnAxis(ap=my_slot_i[:, n, k:k + 1], axis=0),
                        bounds_check=SEQ * TOPK - 1, oob_is_err=True).then_inc(y_got[n], 16)

        @block.scalar
        def _(sc):
            a = nc.scalar
            chain = [0]

            def link(ins):
                chain[0] += 1
                ins.then_inc(act_chain, 1)
                sc.wait_ge(act_chain, chain[0])

            sc.dma_start(c_col[:, 0, :], c.rearrange("a (k p) -> p (a k)", p=P), allow_slow_non_contiguous=True).then_inc(c_in, 16)
            xv = x[0].rearrange("(n p) d -> p n d", p=P)
            sc.dma_start(x_in[:], xv).then_inc(x_got, 16)
            sc.dma_start(gain[:], norm1_gain.broadcast_to([P, D])).then_inc(gain_got, 16)
            sc.dma_start(mod1[:], ada_b[:, 0:2 * D].broadcast_to([P, 2 * D])).then_inc(mod1_bias, 16)
            sc.dma_start(neg_sink[0:64, :], attn_sinks[:, 0:4].broadcast_to([64, 4])).then_inc(small_got, 16)
            sc.dma_start(neg_sink[64:128, :], attn_sinks[:, 4:8].broadcast_to([64, 4])).then_inc(small_got, 16)
            sc.dma_start(fbias[:], forget_bias.broadcast_to([P, FOX])).then_inc(small_got, 16)
            sc.wait_ge(c_in, 16)
            a.activation(c_col[:, 1, :], c_col[:, 0, :], ACT.Sigmoid).then_inc(c_sig, 1)
            sc.wait_ge(x_got, 16)
            for n in range(NT):
                if n >= 1:
                    sc.wait_ge(ssq_ready, n)
                a.activation(h_row[:, 0], x_in[:, n], ACT.Square, accum_out=ssq[:, n:n + 1]).then_inc(ssq_ready, 1)
            sc.wait_ge(var_ready, 1)
            a.activation(rstd[:, 0:4], ssq[:, 4:8], ACT.Sqrt).then_inc(std_ready, 1)
            for n in range(NT):
                for half in range(2):
                    sc.wait_ge(ht_done, 2 * n + half + 1)
                    a.copy(hT[:, 4 * half:4 * half + 4, n * P:(n + 1) * P],
                           bank[2 + 2 * (n % 2) + half][:].rearrange("p (k t) -> p k t", k=4)).then_inc(ht_read, 1)
            for m in range(len(ada2_chunk)):
                if m >= 2:
                    sc.wait_ge(row_ready, m - 1)
                    sc.dma_start(mod_dram[:, (m - 2) * CW:(m - 1) * CW], mod_row[:, m % 2]).then_inc(row_stored, 16)
                    sc.wait_ge(row_stored, 16 * (m - 1))
                elif m == 0:
                    sc.wait_ge(ht_done, 2 * NT)
                sc.dma_start(mod_row[:, m % 2], ada_b[:, (4 + m) * CW:(5 + m) * CW]).then_inc(bias_got[m % 2], 16)
            for m in range(len(ada2_chunk) - 2, len(ada2_chunk)):
                sc.wait_ge(row_ready, m + 1)
                sc.dma_start(mod_dram[:, m * CW:(m + 1) * CW], mod_row[:, m % 2]).then_inc(row_stored, 16)
            sc.wait_ge(fz_ready, 1)
            link(a.activation(fwork[:], flog[:], ACT.Abs))
            link(a.activation(fwork[:], fwork[:], ACT.Exp, scale=-1.0))
            a.activation(fwork[:], fwork[:], ACT.Ln, bias=1.0).then_inc(fl_ready, 1)

            def transposed(u):
                kind, n, _ = ATT[u]
                rows = HD if (kind, n) == ("swa", 0) else P
                cols = SEQ if kind == "swa" else (n + 1) * P
                sc.wait_ge(pt_done, u + 1)
                if u >= AB:
                    sc.wait_ge(pv_done, u - AB + 1)
                a.copy(probT[0:rows, u % AB, 0:cols], bank[3 + u % 2][0:rows, 0:cols]).then_inc(pt_read, 1)

            def outputs(u):
                kind, n, h = ATT[u]
                if kind == "swa" and n % 2 == 1:
                    sc.wait_ge(pv_done, u + 1)
                    a.copy(o[:, n // 2, 0:512], bank[5 + (n // 2) % 2][:]).then_inc(o_read_a, 1)
                if kind == "sb" and h == SB - 1:
                    sc.wait_ge(pv_done, u + 1)
                    a.copy(o[:, n, 768:1024], bank[7 - n % 2][:, 0:256]).then_inc(o_read_a, 1)

            for u, (kind, n, h) in enumerate(ATT):
                b, cols = u % AB, (n + 1) * P
                if kind == "swa":
                    first = HD if n == 0 else 0
                    sc.wait_ge(max_ready, u + 1)
                    for t in range(4):
                        a.activation(soft[:, b, t * P + first:(t + 1) * P], score[:, b, t * P + first:(t + 1) * P],
                                     ACT.Exp, bias=mrow[:, u, t:t + 1], accum_out=lrow[:, n, t:t + 1]).then_inc(exp_ready, 1)
                    a.activation(sinkd[:, n, :], sinkd[:, n, :], ACT.Exp).then_inc(exp_ready, 1)
                elif kind == "fox":
                    sc.wait_ge(max_ready, u + 1)
                    sc.wait_ge(pt_done, u - AB + 1)
                    a.activation(prob[:, b, 0:cols], score[:, b, 0:cols], ACT.Exp, bias=mrow[:, u, 0:1],
                                 accum_out=lfox[:, n, h:h + 1]).then_inc(tri_ready, 1)
                else:
                    i = u - SB0
                    sc.wait_ge(score_done, u + 1)
                    if i < AB:
                        sc.wait_ge(tri_ready, SB0 - FOX0)
                    else:
                        sc.wait_ge(stick_ready, i - AB + 1)
                    a.activation(soft[:, b, 0:cols], bank[b][:, 0:cols], ACT.Sigmoid, scale=-1.0)
                    a.activation(score[:, b, 0:cols], bank[b][:, 0:cols], ACT.Sigmoid).then_inc(sb_read, 1)
                if u >= 1:
                    transposed(u - 1)
                if u >= 3:
                    outputs(u - 3)
            transposed(NU - 1)
            for u in range(NU - 3, NU):
                outputs(u)
            sc.wait_ge(pv_done, NU)
            sc.wait_ge(row_stored, 16 * len(ada2_chunk))
            sc.dma_start(mod2[:], mod_dram.broadcast_to([P, 4 * D])).then_inc(late_got, 16)
            sc.dma_start(rw[:], router_w[0].rearrange("(k p) e -> p k e", p=P)).then_inc(late_got, 16)
            sc.dma_start(rb[:], router_b.broadcast_to([P, NE])).then_inc(late_got, 16)
            sc.dma_start(head_gain[:], mix_out_gain.rearrange("a (k p) -> p (a k)", p=P), allow_slow_non_contiguous=True).then_inc(late_got, 16)
            sc.dma_start(gain2[:], norm2_gain.broadcast_to([P, D])).then_inc(late_got, 16)
            sc.dma_start(resid[:], xv).then_inc(x_again, 16)
            sc.dma_start(bdn[:], b_dn[0]).then_inc(bdn_got, 16)
            for n in range(4):
                sc.dma_start(bgu[32 * n:32 * n + 32, :], b_gu[0, :, n * CW:(n + 1) * CW]).then_inc(bgu_got, 16)
            sc.wait_ge(hss_ready, NT)
            a.activation(hss[:], hss[:], ACT.Sqrt).then_inc(hstd_ready, 1)

            def h2_out(n):
                sc.wait_ge(h2_ready, n + 1)
                sc.dma_start(h2_dram[n * P:(n + 1) * P, :], h2_row[:, n]).then_inc(h2_stored, 16)
                for half in range(2):
                    sc.wait_ge(h2t_done, 2 * n + half + 1)
                    a.copy(h2T[:, 4 * half:4 * half + 4, n * P:(n + 1) * P],
                           bank[4 + 2 * (n % 2) + half][:].rearrange("p (k t) -> p k t", k=4)).then_inc(h2t_read, 1)

            for n in range(NT):
                sc.wait_ge(x2_ready, n + 1)
                if n >= 1:
                    sc.wait_ge(ssq_ready, NT + n)
                a.activation(osq[:], resid[:, n], ACT.Square, accum_out=ssq[:, n:n + 1]).then_inc(ssq_ready, 1)
                sc.wait_ge(var_ready, 2 + n)
                a.activation(rstd[:, n:n + 1], ssq[:, 4 + n:5 + n], ACT.Sqrt).then_inc(std_ready, 1)
                if n >= 1:
                    h2_out(n - 1)
            h2_out(NT - 1)
            sc.wait_ge(gate_z, 1)
            a.activation(gate[:], gate[:], ACT.Exp).then_inc(gate_e, 1)
            a.activation(warm[:], ident[:, 0:8], ACT.Sigmoid)

            def split_high(j):
                ch, q = divmod(j, UPC)
                a.copy(w_hi[:, j % SPLITS], ring[:, slot_of(ch), KQ * q:KQ * q + KQ, :]).then_inc(split_hi[j % USEMS], 1)

            def tokens_high(value):
                sc.wait_ge(xt_done, value)
                a.copy(xT_hi[:, 0:4], bank[6][:].rearrange("p (k t) -> p k t", k=4))
                a.copy(xT_hi[:, 4:8], bank[7][:].rearrange("p (k t) -> p k t", k=4)).then_inc(xt_hi_ready, 1)

            def act_high(ch, p1, p2):
                sc.wait_ge(at_done[ch], p2 if ch >= 2 else p1)
                half = bank[4 + ch % 2][:, 0:256].rearrange("p (k t) -> p k t", k=2)
                a.copy(aT_hi[:, 2 * ch:2 * ch + 2], half).then_inc(at_hi_ready[ch], 1)

            sc.sem_inc(y_stored, 16)
            for hf in range(DN_CHUNKS):
                sc.sem_inc(y_ready[hf], 1)
            sc.wait_ge(h2_stored, 16 * NT)
            sc.wait_ge(router_done, 1)
            sc.wait_ge(ring_loaded[slot_of(0)], 16 * load0[0])
            for j in range(UPC):
                split_high(j)
            tokens_high(1)
            sc.wait_ge(resid_ready, 2 * NT)
            sc.wait_ge(bgu_ready, 1)
            sc.dma_start(res_dram.rearrange("n p d -> p n d"), resid[:]).then_inc(res_stored, 16)
            sc.wait_ge(ring_loaded[slot_of(1)], 16 * load0[1])
            for j in range(UPC, LEAD * UPC):
                split_high(j)
            n_passes = sc.value_load(passes_i[0:1, 0:1], min_val=NE, max_val=MAX_PASSES)
            with sc.Fori(0, n_passes) as p:
                p1, p2 = sc.snap(p + 1), sc.snap(p + 2)
                nth = [sc.snap(p * GU_CHUNKS + (ch + 1)) for ch in range(GU_CHUNKS)]
                turn = turns(sc, p)
                stored = sc.snap(p * 16 + 16)
                loaded = {v: sc.snap(p * 16 + 16 * v) for v in sorted(set(load0[LEAD:]) | {v + 1 for v in load0[:LEAD]})}
                for ch in range(1, CHUNKS + 1):
                    cc = (ch + LEAD - 1) % CHUNKS
                    if ch <= GU_CHUNKS:
                        sc.wait_ge(glu_ready, nth[ch - 1])
                        a.activation(sig[:, (ch - 1) % 2], glu[:, (ch - 1) % 2], ACT.Sigmoid,
                                     scale=ALPHA).then_inc(sig_ready, 1)
                    sc.wait_ge(ring_loaded[slot_of(cc)], loaded[load0[cc] + (ch + LEAD - 1) // CHUNKS])
                    for q in range(UPC):
                        j = (ch + LEAD - 1) * UPC + q
                        sc.wait_ge(unit_used[j % USEMS], turn[j // USEMS])
                        split_high(cc * UPC + q)
                        if ch <= GU_CHUNKS and q == 1:
                            act_high(ch - 1, p1, p2)
                        if ch == GU_CHUNKS + 1 and q == 1:
                            tokens_high(p2)
                    if ch == GU_CHUNKS + 1:
                        sc.wait_ge(y_stored, stored)
                    if ch > GU_CHUNKS:
                        hf = ch - GU_CHUNKS - 1
                        used = ch * UPC - 1
                        sc.wait_ge(unit_used[used % USEMS], turn[used // USEMS + 1])
                        a.copy(y_row[:, hf * CW:(hf + 1) * CW], bank[2 + hf][:]).then_inc(y_ready[hf], 1)
                first_slot = sc.value_load(ybase_i[0:1, bass.ds(p, 1)], min_val=0, max_val=SEQ * TOPK)
                y_at = y_dram[bass.ds(first_slot, P), :]
                for hf in range(DN_CHUNKS):
                    sc.wait_ge(y_ready[hf], p2)
                sc.dma_start(y_at, y_row[:]).then_inc(y_stored, 16)

            stored = sc.snap(n_passes * 16 + 16)
            split_past = sc.snap(n_passes * UTURNS + 1)
            for j in range(USEMS):
                sc.wait_ge(split_lo[j], split_past)
            sc.wait_ge(y_stored, stored)
            sc.sem_inc(experts_over, 1)
            sc.dma_start(res_f[:], res_dram.rearrange("n p d -> p n d")).then_inc(fin_got, 16)
            sc.dma_start(gate2_f[:], mod_dram[:, 3 * D:4 * D].broadcast_to([P, D])).then_inc(fin_got, 16)
            sc.dma_start(gain_f[:], final_gain.rearrange("(a d) -> a d", a=1).broadcast_to([P, D])).then_inc(fin_got, 16)
            for n in range(NT):
                sc.wait_ge(acc_step, 6 * n + 6)
                if n >= 1:
                    sc.wait_ge(fin_ss, n)
                a.activation(junk_f[:], acc[:, n % 2], ACT.Square, accum_out=ssq[:, n:n + 1]).then_inc(fin_ss, 1)
                sc.wait_ge(fin_var, n + 1)
                a.activation(rstd[:, n:n + 1], ssq[:, 4 + n:5 + n], ACT.Sqrt).then_inc(fin_std, 1)
                sc.wait_ge(fin_ready, n + 1)
                sc.dma_start(out[0, n * P:(n + 1) * P, :], acc[:, n % 2]).then_inc(out_stored[n % 2], 16)
            for i in range(2):
                sc.wait_ge(out_stored[i], 16 * NT // 2)

        @block.vector
        def _(ve):
            v = nc.vector
            chain = [0]

            def link(ins):
                chain[0] += 1
                ins.then_inc(dve_chain, 1)
                ve.wait_ge(dve_chain, chain[0])

            def wide(ap, n, m):
                return ap.unsqueeze(2).broadcast_to([P, n, m])

            ve.wait_ge(c_sig, 1)
            link(v.tensor_tensor(c_col[:, 2, :], c_col[:, 0, :], c_col[:, 1, :], ALU.mult))
            v.tensor_copy(c_rep[:], wide(c_col[:, 2, :], NK, P)).then_inc(c_ready, 1)
            ve.wait_ge(consts, N_CONST)
            link(v.scalar_tensor_tensor(alibi[:, 3, :], alibi[:, 3, :], -1.0, alibi[:, 3, :], ALU.mult, ALU.max))
            for t in range(4):
                for h in range(2):
                    slope = 2.0 ** (-8.0 * (t + 4 * h + 1) / SWA_Q)
                    link(v.tensor_scalar(alibi[64 * h:64 * h + 64, t, :], alibi[64 * h:64 * h + 64, 3, :], -slope, None, ALU.mult))
            ve.wait_ge(small_got, 48)
            link(v.tensor_scalar(neg_sink[:], neg_sink[:], -1.0, None, ALU.mult))
            ve.wait_ge(ssq_ready, NT)
            v.tensor_scalar(ssq[:, 4:8], ssq[:, 0:4], 1.0 / D, EPS, ALU.mult, ALU.add).then_inc(var_ready, 1)
            ve.wait_ge(std_ready, 1)
            link(v.reciprocal(rstd[:, 0:4], rstd[:, 0:4]))
            ve.wait_ge(mod1_bias, 16)
            for i in range(4):
                ve.wait_ge(ada_done, i + 1)
                m = mod1[:, i * CW:(i + 1) * CW]
                v.tensor_tensor(m, bank[i % 2][:], m, ALU.add).then_inc(ada_read, 1)
            ve.wait_ge(gain_got, 16)
            ve.wait_ge(ada_read, 4)
            link(v.scalar_tensor_tensor(mod1[:, D:2 * D], mod1[:, D:2 * D], 1.0, gain[:], ALU.add, ALU.mult))
            for n in range(NT):
                if n >= 2:
                    ve.wait_ge(ht_done, 2 * (n - 1))
                link(v.scalar_tensor_tensor(h_row[:, n % 2], x_in[:, n], rstd[:, n:n + 1], mod1[:, D:2 * D], ALU.mult, ALU.mult))
                v.tensor_tensor(h_row[:, n % 2], h_row[:, n % 2], mod1[:, 0:D], ALU.add).then_inc(h_ready, 1)
            link(v.memset(stay_from[:], 1.0))
            ve.wait_ge(ht_done, 2 * NT)

            def ada_step(m, k):
                g, acc_m = ada2_chunk[m], ada_acc[:, m % 2]
                w = ring[:, g % SLOTS, k, :]
                if k == 0:
                    ve.wait_ge(ring_loaded[g % SLOTS], ring_value[g])
                    if m >= 2:
                        ve.wait_ge(sum_done, m - 1)
                    link(v.tensor_scalar(acc_m, w, c_col[:, 2, 0:1], None, ALU.mult))
                else:
                    ins = v.scalar_tensor_tensor(acc_m, w, c_col[:, 2, k:k + 1], acc_m, ALU.mult, ALU.add)
                    if k == NK - 1:
                        ins.then_inc(acc_ready, 1)
                    else:
                        link(ins)

            def ada_row(m):
                ve.wait_ge(sum_done, m + 1)
                ve.wait_ge(bias_got[m % 2], 16 * (m // 2 + 1))
                v.tensor_tensor(mod_row[:, m % 2], bank[2 + m % 2][0:1, :], mod_row[:, m % 2], ALU.add).then_inc(row_ready, 1)

            for j, (i, kind, cols, dst, scale) in enumerate(PROJ):
                ve.wait_ge(proj_done, j + 1)
                src = bank[6 + j % 2]
                if kind != "V":
                    v.tensor_scalar(dst, src[:], scale, None, ALU.mult).then_inc(proj_read, 1)
                elif i == 2:
                    link(v.tensor_copy(dst[1], src[:, 256:256 + FOX]))
                    v.tensor_copy(dst[0], src[:, 0:256]).then_inc(proj_read, 1)
                else:
                    w = cols[1] - cols[0]
                    m = len(cols[2])
                    v.tensor_copy(dst, src[:, 0:m * w].rearrange("p (m w) -> p m w", m=m)).then_inc(proj_read, 1)
                if (i, kind) == (2, "V") and cols[2] == [3 * P]:
                    ve.wait_ge(proj_read, j + 1)
                    v.tensor_tensor(flog[:], flog[:], fbias[:].unsqueeze(1).broadcast_to([P, NT, FOX]), ALU.add).then_inc(fz_ready, 1)
                if j >= 2:
                    for m in range(ada_chunks_over(j - 3), ada_chunks_over(j - 2)):
                        ada_row(m)
                for m, k in ADA_STEPS[PER_JOB * j:PER_JOB * (j + 1)]:
                    ada_step(m, k)
            for m in range(ada_chunks_over(len(PROJ) - 3), len(ada2_chunk)):
                ada_row(m)
            ve.wait_ge(fl_ready, 1)
            link(v.scalar_tensor_tensor(flog[:], flog[:], 0.0, fwork[:], ALU.min, ALU.subtract))
            v.tensor_copy(lfb[:].rearrange("p n h m -> p (n h) m"),
                          wide(flog[:].rearrange("p n h -> p (n h)"), NT * FOX, P)).then_inc(lfb_ready, 1)
            ve.wait_ge(cumf_done, 1)
            v.tensor_copy(cumf_col[:].rearrange("p n h -> p (n h)"), bank[4][:, 0:NT * FOX]).then_inc(cumf_read, 1)
            for h in range(FOX):
                ve.wait_ge(cumf_done, h + 2)
                v.tensor_copy(cumf_row[:, h, :], bank[(5, 0, 1, 2)[h]][:]).then_inc(cumf_read, 1)
            ve.wait_ge(cumf_read, 1 + FOX)

            def swa_normalize(u):
                n, b = ATT[u][1], u % AB
                first = HD if n == 0 else 0
                ve.wait_ge(exp_ready, 5 * (u + 1))
                link(v.tensor_tensor(lrow[:, n, :], lrow[:, n, :], sinkd[:, n, :], ALU.add))
                link(v.reciprocal(lrow[:, n, :], lrow[:, n, :]))
                if u >= AB:
                    ve.wait_ge(pt_done, u - AB + 1)
                v.tensor_tensor(prob[:, b].rearrange("p (t j) -> p t j", t=4)[:, :, first:],
                                soft[:, b].rearrange("p (t j) -> p t j", t=4)[:, :, first:],
                                wide(lrow[:, n, :], 4, P - first), ALU.mult).then_inc(swa_ready, 1)

            def fox_outputs(u):
                kind, n, h = ATT[u]
                if kind == "fox" and h == FOX - 1:
                    ve.wait_ge(pv_done, u + 1)
                    link(v.reciprocal(lfox[:, n, :], lfox[:, n, :]))
                    v.tensor_tensor(o[:, n, 512:768].rearrange("p (h d) -> p h d", h=FOX),
                                    bank[7 - n % 2][:, 0:256].rearrange("p (h d) -> p h d", h=FOX),
                                    wide(lfox[:, n, :], FOX, HD), ALU.mult).then_inc(o_read_v, 1)

            for u, (kind, n, h) in enumerate(ATT):
                b, cols = u % AB, (n + 1) * P
                diag = slice(n * P, (n + 1) * P)
                if kind == "swa":
                    first = HD if n == 0 else 0
                    s4 = score[:, b].rearrange("p (t j) -> p t j", t=4)[:, :, first:]
                    ve.wait_ge(score_done, u + 1)
                    v.tensor_tensor(s4, bank[b][:].rearrange("p (t j) -> p t j", t=4)[:, :, first:],
                                    alibi[:, :, first:], ALU.add).then_inc(score_read, 1)
                    ve.wait_ge(score_read, u + 1)
                    link(v.tensor_reduce(mtmp[:], s4, AX.X, ALU.max))
                    link(v.scalar_tensor_tensor(mrow[:, u, :], mtmp[:], -1.0, neg_sink[:], ALU.mult, ALU.min))
                    v.tensor_tensor(sinkd[:, n, :], mrow[:, u, :], neg_sink[:], ALU.subtract).then_inc(max_ready, 1)
                elif kind == "fox":
                    ve.wait_ge(score_done, u + 1)
                    if u >= FOX0 + AB:
                        ve.wait_ge(tri_ready, u - AB + 1 - FOX0)
                    v.scalar_tensor_tensor(score[:, b, 0:cols], bank[b][:, 0:cols], cumf_col[:, n, h:h + 1],
                                           cumf_row[:, h, 0:cols], ALU.add, ALU.subtract).then_inc(score_read, 1)
                    ve.wait_ge(score_read, u + 1)
                    link(v.tensor_tensor(score[:, b, diag], score[:, b, diag], causal_add[:], ALU.add))
                    link(v.tensor_reduce(mtmp[:, 0:1], score[:, b, 0:cols], AX.X, ALU.max))
                    v.tensor_scalar(mrow[:, u, 0:1], mtmp[:, 0:1], -1.0, None, ALU.mult).then_inc(max_ready, 1)
                else:
                    ve.wait_ge(sb_read, u - SB0 + 1)
                    v.tensor_tensor(score[:, b, diag], score[:, b, diag], low_strict[:], ALU.mult).then_inc(score_read, 1)
                    link(v.tensor_tensor(soft[:, b, diag], soft[:, b, diag], tri_incl[:, 0:P], ALU.max))
                    link(v.tensor_tensor_scan(stay_from[:, 0:cols][:, ::-1], soft[:, b, 0:cols][:, ::-1],
                                              ones[:, 0:1].broadcast_to([P, cols]), 1.0, ALU.mult, ALU.mult))
                    ve.wait_ge(score_read, u + 1)
                    ve.wait_ge(pt_done, u - AB + 1)
                    v.tensor_tensor(prob[:, b, 0:cols], score[:, b, 0:cols], stay_from[:, 1:cols + 1], ALU.mult).then_inc(stick_ready, 1)
                if u >= 1 and ATT[u - 1][0] == "swa":
                    swa_normalize(u - 1)
                if u >= 3:
                    fox_outputs(u - 3)
            ve.wait_ge(pv_done, NU)
            for n in range(NT):
                ve.wait_ge(o_read_a, NT + n + 1)
                ve.wait_ge(o_read_v, NT)
                link(v.tensor_tensor(osq[:], o[:, n], o[:, n], ALU.mult))
                link(v.tensor_reduce(hss[:, n, :], osq[:].rearrange("p (h d) -> p h d", h=HEADS), AX.X, ALU.add))
                v.tensor_scalar(hss[:, n, :], hss[:, n, :], 1.0 / HD, EPS, ALU.mult, ALU.add).then_inc(hss_ready, 1)
            ve.wait_ge(hstd_ready, 1)
            link(v.reciprocal(hss[:].rearrange("p n h -> p (n h)"), hss[:].rearrange("p n h -> p (n h)")))
            for n in range(NT):
                on = o[:, n].rearrange("p (h d) -> p h d", h=HEADS)
                v.tensor_tensor(on, on, wide(hss[:, n, :], HEADS, HD), ALU.mult).then_inc(o_norm, 1)
            ve.wait_ge(late_got, 80)
            gate1, shift2, scale2, gate2 = (mod2[:, i * D:(i + 1) * D] for i in range(4))
            link(v.scalar_tensor_tensor(scale2, scale2, 1.0, gain2[:], ALU.add, ALU.mult))
            for n in range(NT):
                for half in range(2):
                    ve.wait_ge(ot_done, 2 * n + half + 1)
                    v.tensor_tensor(oT[:, 4 * half:4 * half + 4, n * P:(n + 1) * P],
                                    bank[4 + 2 * (n % 2) + half][:].rearrange("p (k t) -> p k t", k=4),
                                    wide(head_gain[:, 4 * half:4 * half + 4], 4, P), ALU.mult).then_inc(ot_read, 1)

            ve.wait_ge(x_again, 16)
            for n in range(NT):
                for half in range(2):
                    cs = slice(half * CW, (half + 1) * CW)
                    ve.wait_ge(mix_done, 2 * n + half + 1)
                    v.tensor_tensor(mixt[:], bank[(2 * n + half) % 4][:], gate1[:, cs], ALU.mult).then_inc(mix_read, 1)
                    ve.wait_ge(mix_read, 2 * n + half + 1)
                    add = v.tensor_tensor(resid[:, n, cs], resid[:, n, cs], mixt[:], ALU.add)
                    if half:
                        add.then_inc(x2_ready, 1)
                    else:
                        link(add)
                ve.wait_ge(ssq_ready, NT + n + 1)
                v.tensor_scalar(ssq[:, 4 + n:5 + n], ssq[:, n:n + 1], 1.0 / D, EPS, ALU.mult, ALU.add).then_inc(var_ready, 1)
                ve.wait_ge(std_ready, 2 + n)
                link(v.reciprocal(rstd[:, n:n + 1], rstd[:, n:n + 1]))
                link(v.scalar_tensor_tensor(h2_row[:, n], resid[:, n], rstd[:, n:n + 1], scale2, ALU.mult, ALU.mult))
                v.tensor_tensor(h2_row[:, n], h2_row[:, n], shift2, ALU.add).then_inc(h2_ready, 1)
            def make_pick(dest_col):
                v.tensor_tensor(pick[:], pass_slots[:].unsqueeze(1).broadcast_to([P, NT, P]),
                                dest_col.broadcast_to([P, NT, P]), ALU.is_equal).then_inc(pick_ready, 1)

            def token_ids(value):
                ve.wait_ge(ids_done, value)
                v.tensor_copy(ids[:, 0:1], bank[7][:, 0:1]).then_inc(ids_ready, 1)

            ve.wait_ge(bgu_got, 64)
            odd = bgu[:].rearrange("p (f two) -> p f two", two=2)[:, :, 1]
            link(v.tensor_scalar(odd, odd, 1.0, None, ALU.add))
            link(v.tensor_copy(bgu_hi[:], bgu[:]))
            v.tensor_tensor(bgu_lo[:], bgu[:], bgu_hi[:].bitcast(F32), ALU.subtract).then_inc(bgu_ready, 1)
            ve.wait_ge(bdn_got, 16)
            v.tensor_tensor(bdn[:], bdn[:], gate2[0:NE, :], ALU.mult).then_inc(bdn_ready, 1)
            ve.wait_ge(router_done, 1)
            link(v.tensor_tensor(logit[:], bank[0][:, 0:NT * NE].rearrange("p (n e) -> p n e", n=NT),
                                 rb[:].unsqueeze(1).broadcast_to([P, NT, NE]), ALU.add))
            for n in range(NT):
                link(v.max(top[:, n, :], logit[:, n, :]))
                link(v.max_index(topi[:, n, :], top[:, n, :], logit[:, n, :]))
            link(v.tensor_copy(topf[:], topi[:, :, 0:TOPK]))
            v.tensor_tensor(gate[:], top[:, :, 0:TOPK], top[:, :, 0:1].broadcast_to([P, NT, TOPK]), ALU.subtract).then_inc(gate_z, 1)
            ve.wait_ge(consts, N_CONST + 2)
            for n in range(NT):
                link(v.tensor_tensor(hot[:, n], iota_e[:].unsqueeze(1).broadcast_to([P, TOPK, NE]), wide(topf[:, n, :], TOPK, NE), ALU.is_equal))
            v.tensor_reduce(mask[:], hot[:].rearrange("p n k e -> p n e k"), AX.X, ALU.add).then_inc(mask_ready, 1)
            ve.wait_ge(gate_e, 1)
            link(v.tensor_reduce(gsum[:, :, 0], gate[:], AX.X, ALU.add))
            link(v.reciprocal(gsum[:, :, 1], gsum[:, :, 0]))
            link(v.tensor_tensor(gate[:], gate[:], gsum[:, :, 1:2].broadcast_to([P, NT, TOPK]), ALU.mult))
            for n in range(NT):
                link(v.tensor_tensor(hot_w[:, n], hot[:, n], wide(gate[:, n, :], TOPK, NE), ALU.mult))
            v.tensor_reduce(gates_e[:], hot_w[:].rearrange("p n k e -> p n e k"), AX.X, ALU.add).then_inc(gates_ready, 1)
            ve.wait_ge(rank_done, 1)
            link(v.tensor_copy(count[:], bank[2][:, 0:NE]))
            link(v.tensor_scalar(nblk[:, 0, :], count[:], float(P), 1.0, ALU.is_gt, ALU.add))
            link(v.scalar_tensor_tensor(nblk[:, 1, :], count[:], 2.0 * P, nblk[:, 0, :], ALU.is_gt, ALU.add))
            link(v.scalar_tensor_tensor(nblk[:, 0, :], count[:], 3.0 * P, nblk[:, 1, :], ALU.is_gt, ALU.add))
            link(v.tensor_tensor_scan(pend[:], ones[:, 0:NE], nblk[:, 0, :], 0.0, ALU.mult, ALU.add))
            link(v.tensor_tensor(pstart[:], pend[:], nblk[:, 0, :], ALU.subtract))
            link(v.tensor_tensor_scan(start[:], ones[:, 0:NE], count[:], 0.0, ALU.mult, ALU.add))
            link(v.tensor_tensor(start[:], start[:], count[:], ALU.subtract))
            link(v.tensor_tensor(dest[:], start[:].unsqueeze(1).broadcast_to([P, NT, NE]),
                                 bank[1][:, 0:NT * NE].rearrange("p (n e) -> p n e", n=NT), ALU.add))
            link(v.scalar_tensor_tensor(dest[:], dest[:], 1.0, mask[:], ALU.add, ALU.mult))
            link(v.tensor_scalar(dest[:], dest[:], -1.0, None, ALU.add))
            link(v.tensor_copy(pass_slots[:], slot_iota[:]))
            make_pick(dest[:, :, 0:1])
            ve.wait_ge(gt_done, 1)
            v.tensor_copy(gT[:].rearrange("e n t -> e (n t)"), bank[3][0:NE, :]).then_inc(gt_read, 1)
            for n in range(NT):
                link(v.tensor_tensor(hot_w[:, n], hot[:, n], dest[:, n, :].unsqueeze(1).broadcast_to([P, TOPK, NE]), ALU.mult))
            link(v.tensor_reduce(my_slot[:], hot_w[:], AX.X, ALU.add))
            token_ids(1)
            link(v.tensor_copy(my_slot_i[:], my_slot[:]))
            link(v.tensor_tensor(pcmp[:], pend[:].unsqueeze(1).broadcast_to([P, NP_TAB, NE]), wide(iota_p[:], NP_TAB, NE), ALU.is_le))
            link(v.tensor_reduce(etab[:], pcmp[:], AX.X, ALU.add))
            link(v.tensor_scalar(etab[:], etab[:], float(NE - 1), None, ALU.min))
            link(v.tensor_copy(etab_i[:], etab[:]))
            link(v.scalar_tensor_tensor(from_pass[:], pstart[:], -float(P), start[:], ALU.mult, ALU.add))
            link(v.tensor_tensor(pcmp[:], iota_e[:].unsqueeze(1).broadcast_to([P, NP_TAB, NE]), wide(etab[:], NP_TAB, NE), ALU.is_equal))
            link(v.tensor_tensor(pcmp[:], pcmp[:], from_pass[:].unsqueeze(1).broadcast_to([P, NP_TAB, NE]), ALU.mult))
            link(v.tensor_reduce(ybase[:], pcmp[:], AX.X, ALU.add))
            link(v.scalar_tensor_tensor(ybase[:], iota_p[:], float(P), ybase[:], ALU.mult, ALU.add))
            link(v.tensor_copy(ybase_i[:], ybase[:]))
            v.tensor_copy(passes_i[:], pend[:, NE - 1:NE]).then_inc(tables_ready, 1)
            for n in range(NT):
                for half in range(2):
                    i = 2 * n + half
                    cs = slice(half * CW, (half + 1) * CW)
                    ve.wait_ge(gb_done, i + 1)
                    v.tensor_tensor(resid[:, n, cs], resid[:, n, cs], bank[i % 6][:], ALU.add).then_inc(resid_ready, 1)

            def split_low(j):
                ch, q = divmod(j, UPC)
                v.tensor_tensor(w_lo[:, j % SPLITS], ring[:, slot_of(ch), KQ * q:KQ * q + KQ, :],
                                w_hi[:, j % SPLITS].bitcast(F32), ALU.subtract).then_inc(split_lo[j % USEMS], 1)

            def tokens_low(value):
                ve.wait_ge(xt_hi_ready, value)
                for half in range(2):
                    low = v.tensor_tensor(xT_lo[:, 4 * half:4 * half + 4], bank[6 + half][:].rearrange("p (k t) -> p k t", k=4),
                                          xT_hi[:, 4 * half:4 * half + 4].bitcast(F32), ALU.subtract)
                low.then_inc(xt_lo_ready, 1)

            def act_low(ch, p1):
                ve.wait_ge(at_hi_ready[ch], p1)
                half = bank[4 + ch % 2][:, 0:256].rearrange("p (k t) -> p k t", k=2)
                v.tensor_tensor(aT_lo[:, 2 * ch:2 * ch + 2], half, aT_hi[:, 2 * ch:2 * ch + 2].bitcast(F32),
                                ALU.subtract).then_inc(at_lo_ready[ch], 1)

            n_passes = ve.value_load(passes_i[0:1, 0:1], min_val=NE, max_val=MAX_PASSES)
            ve.sem_inc(lin_ready[2], 1)
            ve.sem_inc(lin_ready[3], 1)
            ve.sem_inc(act_ready[2], 1)
            ve.sem_inc(act_ready[3], 1)
            for i in range(USEMS):
                ve.sem_inc(unit_used[i], 1)
            for ch in (2, 3):
                ve.sem_inc(at_lo_ready[ch], 1)
            v.tensor_scalar(pick_e[:], expert_of_row[:], 0.0, None, ALU.is_equal).then_inc(pick_e_ready, 1)
            tokens_low(1)
            for j in range(LEAD * UPC):
                if j % UPC != POOL_Q:
                    ve.wait_ge(split_hi[j], 1)
                    split_low(j)
            ve.wait_ge(res_stored, 16)
            with ve.Fori(0, n_passes) as p:
                p1, p2 = ve.snap(p + 1), ve.snap(p + 2)
                turn = turns(ve, p)
                e_next = ve.value_load(etab_i[0:1, bass.ds(p1, 1)], min_val=0, max_val=NE - 1)
                ve.wait_ge(ids_done, p1)
                v.tensor_scalar(pass_slots[:], slot_iota[:], ybase[:, bass.ds(p1, 1)], None, ALU.add).then_inc(pick_step, 1)
                ve.wait_ge(pick_step, p1)
                make_pick(dest[:, :, bass.ds(e_next, 1)])
                for ch in range(1, CHUNKS + 1):
                    cc = (ch + LEAD - 1) % CHUNKS
                    if ch <= GU_CHUNKS:
                        c0, used = ch - 1, ch * UPC - 1
                        gu = bank[c0 % 2][:].rearrange("p (f two) -> p f two", two=2)
                        ve.wait_ge(unit_used[used % USEMS], turn[used // USEMS + 1])
                        ve.wait_ge(act_ready[(c0 + 2) % 4], p1)
                        v.tensor_scalar(glu[:, c0 % 2], gu[:, :, 0], LIMIT, None, ALU.min).then_inc(glu_ready, 1)
                        v.tensor_scalar(lin[:, c0 % 2], gu[:, :, 1], 1.0 - LIMIT, 1.0 + LIMIT, ALU.max, ALU.min).then_inc(lin_ready[c0], 1)
                    for q in range(UPC):
                        j = (ch + LEAD - 1) * UPC + q
                        if q != POOL_Q:
                            ve.wait_ge(split_hi[j % USEMS], turn[j // USEMS])
                            split_low(cc * UPC + q)
                        if ch <= GU_CHUNKS and q == 1:
                            act_low(ch - 1, p1)
                        if ch == GU_CHUNKS + 1 and q == 1:
                            tokens_low(p2)
                    if ch == 1:
                        token_ids(p2)
                    if ch == GU_CHUNKS:
                        v.tensor_scalar(pick_e[:], expert_of_row[:], etab[:, bass.ds(p1, 1)], None, ALU.is_equal).then_inc(pick_e_ready, 1)
            ve.wait_ge(fin_got, 48)
            for n in range(NT):
                rows = ring[:, n].rearrange("p a b -> p (a b)")
                cur = acc[:, n % 2]
                if n >= 2:
                    ve.wait_ge(out_stored[n % 2], 16 * (n // 2))
                ve.wait_ge(y_got[n], 16 * TOPK)
                v.tensor_scalar(cur, rows[:, 0:D], gate[:, n, 0:1], None, ALU.mult).then_inc(acc_step, 1)
                for k in range(1, TOPK):
                    ve.wait_ge(acc_step, 6 * n + k)
                    v.scalar_tensor_tensor(cur, rows[:, k * D:(k + 1) * D], gate[:, n, k:k + 1], cur, ALU.mult, ALU.add).then_inc(acc_step, 1)
                ve.wait_ge(acc_step, 6 * n + 4)
                v.tensor_tensor(cur, cur, gate2_f[:], ALU.mult).then_inc(acc_step, 1)
                ve.wait_ge(acc_step, 6 * n + 5)
                v.tensor_tensor(cur, cur, res_f[:, n], ALU.add).then_inc(acc_step, 1)
                ve.wait_ge(fin_ss, n + 1)
                v.tensor_scalar(ssq[:, 4 + n:5 + n], ssq[:, n:n + 1], 1.0 / D, EPS, ALU.mult, ALU.add).then_inc(fin_var, 1)
                ve.wait_ge(fin_std, n + 1)
                link(v.reciprocal(rstd[:, n:n + 1], rstd[:, n:n + 1]))
                v.scalar_tensor_tensor(cur, cur, rstd[:, n:n + 1], gain_f[:], ALU.mult, ALU.mult).then_inc(fin_ready, 1)

        @block.tensor
        def _(pe):
            t = nc.tensor

            def ada(g, i):
                pe.wait_ge(ring_loaded[g % SLOTS], ring_value[g])
                for k in range(NK):
                    mm = t.matmul(bank[i % 2][:], c_rep[:, k, :], ring[:, g % SLOTS, k, :], start=(k == 0), stop=(k == NK - 1))
                mm.then_inc(ada_done, 1)

            pe.wait_ge(consts, N_CONST)
            pe.wait_ge(c_ready, 1)
            for i in range(4):
                if i >= 2:
                    pe.wait_ge(ada_read, i - 1)
                ada(i, i)
            for n in range(NT):
                pe.wait_ge(h_ready, n + 1)
                for half in range(2):
                    if n >= 2:
                        pe.wait_ge(ht_read, 2 * (n - 2) + half + 1)
                    for k in range(4):
                        kk = 4 * half + k
                        mm = t.transpose(bank[2 + 2 * (n % 2) + half][:, k * P:(k + 1) * P], h_row[:, n % 2, kk * P:(kk + 1) * P], ident[:])
                    mm.then_inc(ht_done, 1)
            pe.wait_ge(ht_read, 2 * NT)

            def ada_sum(m):
                pe.wait_ge(acc_ready, m + 1)
                if m >= 2:
                    pe.wait_ge(row_ready, m - 1)
                t.matmul(bank[2 + m % 2][0:1, :], ones[:, 0:1], ada_acc[:, m % 2], start=True, stop=True).then_inc(sum_done, 1)

            for j, (i, kind, cols, dst, scale) in enumerate(PROJ):
                g = proj_chunk[i]
                pe.wait_ge(ring_loaded[g % SLOTS], ring_value[g])
                if j >= 2:
                    pe.wait_ge(proj_read, j - 1)
                w, dstb = ring[:, g % SLOTS], bank[6 + j % 2]
                if kind == "V":
                    c0, c1, tokens = cols
                    for m, t0 in enumerate(tokens):
                        for k in range(NK):
                            mm = t.matmul(dstb[:, m * (c1 - c0):(m + 1) * (c1 - c0)], hT[:, k, t0:t0 + P], w[:, k, c0:c1],
                                          start=(k == 0), stop=(k == NK - 1))
                else:
                    for k in range(NK):
                        mm = t.matmul(dstb[:], w[:, k, cols:cols + P], hT[:, k, :], start=(k == 0), stop=(k == NK - 1))
                mm.then_inc(proj_done, 1)
                if j >= 1:
                    for m in range(ada_chunks_over(j - 2), ada_chunks_over(j - 1)):
                        ada_sum(m)
            for m in range(ada_chunks_over(len(PROJ) - 2), len(ada2_chunk)):
                ada_sum(m)
            pe.wait_ge(lfb_ready, 1)
            for n in range(NT):
                for j in range(n + 1):
                    mm = t.matmul(bank[4][:, n * FOX:(n + 1) * FOX], ones[:] if j < n else tri_incl[:, 0:P], flog[:, j, :],
                                  start=(j == 0), stop=(j == n))
            mm.then_inc(cumf_done, 1)
            for h in range(FOX):
                for j in range(NT):
                    mm = t.matmul(bank[(5, 0, 1, 2)[h]][:, j * P:SEQ], lfb[:, j, h, :], tri_incl[:, 0:SEQ - j * P],
                                  start=(j == 0), stop=(j == NT - 1))
                mm.then_inc(cumf_done, 1)
            pe.wait_ge(cumf_read, 1 + FOX)
            pe.wait_ge(proj_read, len(PROJ))
            pe.wait_ge(row_ready, len(ada2_chunk))

            def scores(u):
                kind, n, h = ATT[u]
                if u >= AB:
                    if ATT[u - AB][0] == "sb":
                        pe.wait_ge(sb_read, u - AB - SB0 + 1)
                    else:
                        pe.wait_ge(score_read, u - AB + 1)
                dst = bank[u % AB]
                if kind == "swa":
                    k0 = 0 if n == 0 else (n - 1) * HD
                    for tt in range(4):
                        for a in range(2):
                            half = slice(HD * a, HD * a + HD)
                            first = HD if n == 0 else 0
                            mm = t.matmul(dst[half, tt * P + first:(tt + 1) * P], qaT[half, tt, n * HD:(n + 1) * HD],
                                          kaT[half, k0:(n + 1) * HD], start=True, stop=True)
                else:
                    q, kk = (qfT, kfT) if kind == "fox" else (qsT, ksT)
                    half = slice(HD * (h % 2), HD * (h % 2) + HD)
                    mm = t.matmul(dst[:, 0:(n + 1) * P], q[half, h // 2, n * P:(n + 1) * P], kk[half, h // 2, 0:(n + 1) * P],
                                  start=True, stop=True)
                mm.then_inc(score_done, 1)

            def transpose_probs(u):
                kind, n, h = ATT[u]
                if kind == "swa":
                    pe.wait_ge(swa_ready, u + 1)
                elif kind == "fox":
                    pe.wait_ge(tri_ready, u - FOX0 + 1)
                else:
                    pe.wait_ge(stick_ready, u - SB0 + 1)
                if u >= 2:
                    pe.wait_ge(pt_read, u - 1)
                dst, b = bank[3 + u % 2], u % AB
                if kind == "swa" and n == 0:
                    for tt in range(4):
                        mm = t.transpose(dst[0:HD, tt * P:(tt + 1) * P], prob[:, b, tt * P + HD:(tt + 1) * P], ident[:])
                else:
                    for m in range(4 if kind == "swa" else n + 1):
                        mm = t.transpose(dst[:, m * P:(m + 1) * P], prob[:, b, m * P:(m + 1) * P], ident[:])
                mm.then_inc(pt_done, 1)

            def times_values(u):
                kind, n, h = ATT[u]
                b = u % AB
                pe.wait_ge(pt_read, u + 1)
                if kind == "swa":
                    dst = bank[5 + (n // 2) % 2]
                    if n % 2 == 0 and n >= 4:
                        pe.wait_ge(o_read_a, n // 2 - 1)
                    rows = HD if n == 0 else P
                    vals = va[:, n // 2] if n % 2 else (va[0:HD, 0] if n == 0 else va_mid[:, n // 2 - 1])
                    q0 = (n % 2) * HD
                    for tt in range(4):
                        for a in range(2):
                            head = tt + 4 * a
                            mm = t.matmul(dst[q0:q0 + HD, head * HD:(head + 1) * HD],
                                          probT[0:rows, b, tt * P + a * HD:tt * P + (a + 1) * HD],
                                          vals[0:rows, a * HD:(a + 1) * HD], start=True, stop=True)
                else:
                    dst = bank[7 - n % 2]
                    vals = vf if kind == "fox" else vs
                    if h == 0 and kind == "fox" and n == 1:
                        pe.wait_ge(o_read_a, NT)
                    if h == 0 and kind == "fox" and n >= 2:
                        pe.wait_ge(o_read_v, n - 1)
                    if h == 0 and kind == "sb":
                        if n < 2:
                            pe.wait_ge(o_read_v, n + 3)
                        else:
                            pe.wait_ge(o_read_a, NT + n - 1)
                    for m in range(n + 1):
                        mm = t.matmul(dst[:, h * HD:(h + 1) * HD], probT[:, b, m * P:(m + 1) * P], vals[:, m, h * HD:(h + 1) * HD],
                                      start=(m == 0), stop=(m == n))
                mm.then_inc(pv_done, 1)

            scores(0)
            scores(1)
            for u in range(NU):
                if u + 2 < NU:
                    scores(u + 2)
                transpose_probs(u)
                if u >= 1:
                    times_values(u - 1)
            times_values(NU - 1)
            pe.wait_ge(sb_read, SB * NT)
            pe.wait_ge(pt_read, NU)
            for n in range(NT):
                pe.wait_ge(o_norm, n + 1)
                for half in range(2):
                    if n >= 2:
                        pe.wait_ge(ot_read, 2 * (n - 2) + half + 1)
                    for k in range(4):
                        kk = 4 * half + k
                        mm = t.transpose(bank[4 + 2 * (n % 2) + half][:, k * P:(k + 1) * P], o[:, n, kk * P:(kk + 1) * P], ident[:])
                    mm.then_inc(ot_done, 1)
            def h2_transposed(n):
                pe.wait_ge(h2_ready, n + 1)
                for half in range(2):
                    if n >= 2:
                        pe.wait_ge(h2t_read, 2 * (n - 2) + half + 1)
                    for k in range(4):
                        kk = 4 * half + k
                        mm = t.transpose(bank[4 + 2 * (n % 2) + half][:, k * P:(k + 1) * P], h2_row[:, n, kk * P:(kk + 1) * P], ident[:])
                    mm.then_inc(h2t_done, 1)

            def router(n):
                pe.wait_ge(h2t_read, 2 * n + 2)
                if n == 0:
                    pe.wait_ge(mix_read, 2 * NT - 3)
                for k in range(NK):
                    mm = t.matmul(bank[0][:, n * NE:(n + 1) * NE], h2T[:, k, n * P:(n + 1) * P], rw[:, k, :],
                                  start=(k == 0), stop=(k == NK - 1))
                if n == NT - 1:
                    mm.then_inc(router_done, 1)

            for n in range(NT):
                pe.wait_ge(ot_read, 2 * n + 2 if n < NT - 1 else 2 * NT)
                for half in range(2):
                    g, i = OUT0 + half, 2 * n + half
                    pe.wait_ge(ring_loaded[g % SLOTS], ring_value[g])
                    if i >= 4:
                        pe.wait_ge(mix_read, i - 3)
                    for k in range(NK):
                        mm = t.matmul(bank[i % 4][:], oT[:, k, n * P:(n + 1) * P], ring[:, g % SLOTS, k, :],
                                      start=(k == 0), stop=(k == NK - 1))
                    mm.then_inc(mix_done, 1)
            for n in range(NT):
                h2_transposed(n)
                if n >= 1:
                    router(n - 1)
            router(NT - 1)
            pe.wait_ge(mask_ready, 1)
            for n in range(NT):
                for j in range(n + 1):
                    if n == 0:
                        pe.wait_ge(mix_read, 2 * NT)
                    t.matmul(bank[1][:, n * NE:(n + 1) * NE], ones[:] if j < n else tri_strict[:], mask[:, j, :],
                             start=(j == 0), stop=(j == n))
            for n in range(NT):
                mm = t.matmul(bank[2][:, 0:NE], ones[:], mask[:, n, :], start=(n == 0), stop=(n == NT - 1))
            mm.then_inc(rank_done, 1)
            pe.wait_ge(gates_ready, 1)
            for n in range(NT):
                mm = t.transpose(bank[3][0:NE, n * P:(n + 1) * P], gates_e[:, n, :], ident[:])
            mm.then_inc(gt_done, 1)

            def token_numbers():
                for n in range(NT):
                    mm = t.matmul(bank[7][:, 0:1], pick[:, n, :], tok_id[:, n:n + 1], start=(n == 0), stop=(n == NT - 1))
                mm.then_inc(ids_done, 1)

            def transpose_tokens():
                for k in range(NK):
                    mm = t.transpose(bank[6 + k // 4][:, (k % 4) * P:(k % 4 + 1) * P], x_rows[:, k * P:(k + 1) * P], ident[:])
                mm.then_inc(xt_done, 1)

            def unit(dst, hi, lo, j, turn, first):
                pe.wait_ge(split_lo[j % USEMS], turn[j // USEMS])
                ch, q = divmod(j, UPC)
                for kk in range(KQ):
                    k = KQ * q + kk
                    w1, w2 = w_hi[:, j % SPLITS, kk, :], w_lo[:, j % SPLITS, kk, :]
                    t.matmul(dst[:], hi[:, k, :], w1, start=(first and k == 0), stop=False)
                    t.matmul(dst[:], hi[:, k, :], w2, start=False, stop=False)
                    mm = t.matmul(dst[:], lo[:, k, :], w1, start=False, stop=(k == NK - 1))
                mm.then_inc(unit_used[j % USEMS], 1)

            def act_transpose(ch, value):
                pe.wait_ge(act_ready[ch], value)
                pe.wait_ge(at_lo_ready[(ch + 2) % 4], pass_value[0])
                for m in range(2):
                    mm = t.transpose(bank[4 + ch % 2][:, m * P:(m + 1) * P],
                                     act_out[:, ch % 2, m * P:(m + 1) * P], ident[:])
                mm.then_inc(at_done[ch], 1)

            for ch in (2, 3):
                pe.sem_inc(at_done[ch], 1)
            pe.wait_ge(pick_ready, 1)
            token_numbers()
            def gated_bias(i):
                n, half = divmod(i, 2)
                if i >= 6:
                    pe.wait_ge(resid_ready, i - 5)
                t.matmul(bank[i % 6][:], gT[:, n, :], bdn[:, half * CW:(half + 1) * CW], start=True, stop=True).then_inc(gb_done, 1)

            pe.wait_ge(gt_read, 1)
            pe.wait_ge(bdn_ready, 1)
            for i in range(6):
                gated_bias(i)
            pe.wait_ge(ids_ready, 1)
            pe.wait_ge(x_rows_got, 16)
            transpose_tokens()
            pe.wait_ge(bgu_ready, 1)
            for i in range(6, 2 * NT):
                gated_bias(i)
            pe.wait_ge(resid_ready, 2 * NT)
            n_passes = pe.value_load(passes_i[0:1, 0:1], min_val=NE, max_val=MAX_PASSES)
            pass_value = [None]
            with pe.Fori(0, n_passes) as p:
                p1, p2 = pe.snap(p + 1), pe.snap(p + 2)
                turn = turns(pe, p)
                pass_value[0] = p1
                rows_got = pe.snap(p * 16 + 32)
                pe.wait_ge(xt_lo_ready, p1)
                pe.wait_ge(pick_e_ready, p1)
                for ch in range(GU_CHUNKS):
                    dst = bank[ch % 2]
                    rows = slice(NE * ch, NE * ch + NE)
                    pe.wait_ge(lin_ready[(ch + 2) % 4], p1)
                    t.matmul(dst[:], pick_e[rows, :], bgu_hi[rows, :], start=True, stop=False)
                    t.matmul(dst[:], pick_e[rows, :], bgu_lo[rows, :], start=False, stop=False)
                    for q in range(UPC):
                        unit(dst, xT_hi, xT_lo, ch * UPC + q, turn, False)
                        if ch >= 1 and q == 1:
                            act_transpose(ch - 1, p2 if ch - 1 >= 2 else p1)
                        if ch == 0 and q == 3:
                            pe.wait_ge(pick_ready, p2)
                            token_numbers()
                for hf in range(DN_CHUNKS):
                    pe.wait_ge(y_ready[hf], p1)
                    for q in range(UPC):
                        if hf == 0:
                            pe.wait_ge(at_lo_ready[q], p2 if q >= 2 else p1)
                        unit(bank[2 + hf], aT_hi, aT_lo, (GU_CHUNKS + hf) * UPC + q, turn, True)
                        if hf == 0 and q == 1:
                            act_transpose(3, p2)
                        if hf == 0 and q == 3:
                            pe.wait_ge(ids_ready, p2)
                            pe.wait_ge(x_rows_got, rows_got)
                            transpose_tokens()


_INS = ['x', 'c', 'norm1_gain', 'norm2_gain', 'ada_w', 'ada_b', 'w_in', 'attn_sinks', 'forget_bias', 'mix_out_gain',
        'w_out', 'router_w', 'router_b', 'expert_w_gate_up', 'expert_b_gate_up', 'expert_w_down', 'expert_b_down',
        'final_gain']


def kernel(**inputs):
    import numpy as _np
    import concourse.bacc as _bacc
    from concourse import mybir as _mybir
    from concourse.bass_utils import run_bass_kernel_spmd as _run

    nc = _bacc.Bacc("TRN2", target_bir_lowering=False, num_devices=1)
    arrays, args = {}, []
    for name in _INS:
        a = _np.ascontiguousarray(inputs[name])
        arrays[f"in_{name}_dram"] = a
        args.append(nc.dram_tensor(f"in_{name}_dram", a.shape, _mybir.dt.from_np(a.dtype), kind="ExternalInput").ap())
    args.append(nc.dram_tensor("out_0_dram", (1, SEQ, D), _mybir.dt.float32, kind="ExternalOutput").ap())
    build_program(nc, *args)
    r = _run(nc, [arrays], core_ids=[0])
    return r.results[0]["out_0_dram"]
```

```python
from contextlib import ExitStack

import concourse.bass as bass
from concourse import mybir

F32 = mybir.dt.float32
F32R = mybir.dt.float32r
I32 = mybir.dt.int32
U32 = mybir.dt.uint32
ALU = mybir.AluOpType
ACT = mybir.ActivationFunctionType
AX = mybir.AxisListType

P = 128
SEQ, D = 512, 1024
NT, NK = SEQ // P, D // P
HD = 64
CW = 512
SWA_Q, SWA_KV, FOX, SB = 8, 2, 4, 4
HEADS = SWA_Q + FOX + SB
NE, TOPK = 32, 4
MAX_PASSES = NE + (SEQ * TOPK - NE) // P
NP_TAB = MAX_PASSES + 1
AB = 3
LIMIT, ALPHA, EPS = 7.0, 1.702, 1e-5
NEG = -1e30
QSCALE = HD ** -0.5
SLOTS = 6
KQ = 2
SPLITS = 8
GU_CHUNKS, DN_CHUNKS = 2 * D // CW, D // CW
CHUNKS = GU_CHUNKS + DN_CHUNKS
UPC = NK // KQ
UNITS = CHUNKS * UPC
POOL_Q = 1
USEMS = 8
UTURNS = UNITS // USEMS
LEAD = 2

C_QA, C_KA, C_VA = 0, 512, 640
C_QF, C_KF, C_VF, C_FL = 768, 1024, 1280, 1536
C_QS, C_KS, C_VS = 1540, 1796, 2052
KB = 1024


def build_program(nc, x, c, norm1_gain, norm2_gain, ada_w, ada_b, w_in, attn_sinks, forget_bias,
                  mix_out_gain, w_out, router_w, router_b, w_gu, b_gu, w_dn, b_dn, final_gain, out):
    ctx = ExitStack()
    with ctx:
        base = (nc.sbuf_base + 31) // 32 * 32

        def at(name, shape, dt, offset):
            return nc.alloc_sbuf_tensor_at(name, shape, dt, offset=base + offset)

        ring = at("ring", [P, SLOTS, NK, CW], F32, 0)
        cursor = [96 * KB]

        def small(name, shape, dt):
            size = 4
            for s in shape[1:]:
                size *= s
            t = at(name, shape, dt, cursor[0])
            cursor[0] += (size + 31) // 32 * 32
            return t

        ident = small("ident", [P, P], F32)
        ones = small("ones", [P, P], F32)
        tok_id = small("tok_id", [P, NT], F32)
        slot_iota = small("slot_iota", [P, P], F32)
        expert_of_row = small("expert_of_row", [P, P], F32)
        dest = small("dest", [P, NT, NE], F32)
        etab = small("etab", [P, NP_TAB], F32)
        etab_i = small("etab_i", [P, NP_TAB], I32)
        iota_p = small("iota_p", [P, NP_TAB], F32)
        iota_e = small("iota_e", [P, NE], F32)
        ybase = small("ybase", [P, NP_TAB], F32)
        ybase_i = small("ybase_i", [P, NP_TAB], I32)
        warm = small("warm", [P, 8], F32)
        passes_i = small("passes_i", [P, 1], I32)
        my_slot = small("my_slot", [P, NT, TOPK], F32)
        my_slot_i = small("my_slot_i", [P, NT, TOPK], I32)
        gate = small("gate", [P, NT, TOPK], F32)
        ssq = small("ssq", [P, 8], F32)
        rstd = small("rstd", [P, 8], F32)
        neg_sink = small("neg_sink", [P, 4], F32)
        assert cursor[0] + 512 <= 101 * KB, cursor[0]
        R0 = 101 * KB
        R1, R2, R3, R4 = R0 + 16 * KB, R0 + 32 * KB, R0 + 48 * KB, R0 + 86 * KB
        x_in = at("x_in", [P, NT, D], F32, R0)
        o = at("o", [P, NT, D], F32, R0)
        h2_row = at("h2_row", [P, NT, D], F32, R0)
        cumf_row = at("cumf_row", [P, FOX, SEQ], F32, R1)
        alibi = at("alibi", [P, 4, P], F32, R1 + 10 * KB)
        ada_acc = at("ada_acc", [P, 2, CW], F32, R1)
        stay_from = at("stay_from", [P, SEQ + 8], F32, R1 + 12 * KB)
        mod1 = at("mod1", [P, 2 * NK], F32, R1 + 15 * KB)
        mod1_b = at("mod1_b", [P, 2 * NK], F32, R1 + 15 * KB + 64)
        gain1 = at("gain1", [P, NK], F32, R1 + 15 * KB + 128)
        hT = at("hT", [P, NK, SEQ], F32, R2)
        oT = at("oT", [P, NK, SEQ], F32, R2)
        h2T = at("h2T", [P, NK, SEQ], F32, R2)
        qaT = at("qaT", [P, 4, SEQ], F32, R3)
        kaT = at("kaT", [P, SEQ], F32, R3 + 8 * KB)
        qfT = at("qfT", [P, 2, SEQ], F32, R3 + 10 * KB)
        kfT = at("kfT", [P, 2, SEQ], F32, R3 + 14 * KB)
        qsT = at("qsT", [P, 2, SEQ], F32, R3 + 18 * KB)
        ksT = at("ksT", [P, 2, SEQ], F32, R3 + 22 * KB)
        va = at("va", [P, NT, 2 * HD], F32, R3 + 26 * KB)
        va_mid = at("va_mid", [P, 3, 2 * HD], F32, R3 + 28 * KB)
        vs = at("vs", [P, NT, 4 * HD], F32, R3 + 29 * KB + 512)
        vf = at("vf", [P, NT, 4 * HD], F32, R3 + 33 * KB + 512)
        mod2 = at("mod2", [P, 4 * D], F32, R3)
        resid = at("resid", [P, NT, D], F32, R3 + 16 * KB)
        head_gain = at("head_gain", [P, NK], F32, R3 + 37 * KB + 512)
        square = at("square", [P, D], F32, R4 + 4 * KB)
        mod_row = at("mod_row", [1, 2, CW], F32, R4 + 12 * KB)
        score = at("score", [P, AB, SEQ], F32, R4)
        soft = at("soft", [P, AB, SEQ], F32, R4 + 6 * KB)
        spare = (SLOTS - 1) * NK * CW * 4
        prob = at("prob", [P, AB, SEQ], F32, spare)
        probT = at("probT", [P, AB, SEQ], F32, spare + 6 * KB)
        lfb = at("lfb", [P, 2, NT, P], F32, spare + 12 * KB)
        tri_incl = at("tri_incl", [P, SEQ], F32, R4 + 16 * KB)
        tri_strict = at("tri_strict", [P, P], F32, R4 + 18 * KB)
        low_strict = at("low_strict", [P, P], F32, R4 + 18 * KB + 512)
        causal_add = at("causal_add", [P, P], F32, R4 + 19 * KB)
        tail = R4 + 20 * KB
        flog = at("flog", [P, NT, FOX], F32, tail)
        fwork = at("fwork", [P, NT, FOX], F32, tail + 64)
        fbias = at("fbias", [P, FOX], F32, tail + 128)
        cumf_col = at("cumf_col", [P, NT, FOX], F32, tail + 160)
        mrow = at("mrow", [P, 40, 4], F32, tail + 224)
        tail2 = R3 + 37 * KB + 544
        sinkd = at("sinkd", [P, 8, 4], F32, tail2)
        lrow = at("lrow", [P, 8, 4], F32, tail2 + 128)
        lfox = at("lfox", [P, NT, FOX], F32, tail2 + 256)
        mtmp = at("mtmp", [P, 4], F32, tail2 + 320)
        c_col = at("c_col", [P, 4, NK], F32, tail2 + 352)
        assert base + tail + 864 <= nc.sbuf_usable_end
        osq = at("osq", [P, D], F32, R4 + 12 * KB)
        hss = at("hss", [P, NT, HEADS], F32, R4 + 19 * KB + 512)
        gain2 = at("gain2", [P, D], F32, R4 + 8 * KB)
        rw = at("rw", [P, NK, NE], F32, R3 + 32 * KB)
        rb = at("rb", [P, NE], F32, R3 + 33 * KB)
        logit = at("logit", [P, NT, NE], F32, R3 + 33 * KB + 128)
        top = at("top", [P, NT, 8], F32, R3 + 33 * KB + 640)
        topi = at("topi", [P, NT, 8], U32, R3 + 33 * KB + 768)
        topf = at("topf", [P, NT, TOPK], F32, R3 + 33 * KB + 896)
        hot = at("hot", [P, NT, TOPK, NE], F32, R3 + 34 * KB + 128)
        mask = at("mask", [P, NT, NE], F32, R3 + 36 * KB + 128)
        gates_e = at("gates_e", [P, NT, NE], F32, R3 + 36 * KB + 640)
        gsum = at("gsum", [P, NT, 2], F32, R3 + 37 * KB + 128)
        rest = R2
        hot_w = at("hot_w", [P, NT, TOPK, NE], F32, rest)
        count = at("count", [P, NE], F32, rest + 2 * KB)
        nblk = at("nblk", [P, 2, NE], F32, rest + 2 * KB + 128)
        pend = at("pend", [P, NE], F32, rest + 2 * KB + 384)
        start = at("start", [P, NE], F32, rest + 2 * KB + 640)
        from_pass = at("from_pass", [P, NE], F32, rest + 2 * KB + 768)
        over = at("over", [P, 2, NE], F32, rest + 3 * KB + 256)
        pass_col = at("pass_col", [P, 2], F32, rest + 3 * KB + 512)
        pass_diag = at("pass_diag", [P, 2, NP_TAB], F32, rest + 4 * KB)
        gT = at("gT", [NE, NT, P], F32, R3 + 32 * KB)
        bdn = at("bdn", [NE, D], F32, R1 + 8 * KB)
        bgu = at("bgu", [P, CW], F32, R1 + 12 * KB)
        m = [R0]

        def moe(name, shape, dt):
            size = 4
            for s in shape[1:]:
                size *= s
            t = at(name, shape, dt, m[0])
            m[0] += size
            return t

        w_hi = moe("w_hi", [P, SPLITS, KQ, CW], F32R)
        w_lo = moe("w_lo", [P, SPLITS, KQ, CW], F32R)
        aT_hi = moe("aT_hi", [P, NK, P], F32R)
        aT_lo = moe("aT_lo", [P, NK, P], F32R)
        glu = moe("glu", [P, 2, CW // 2], F32)
        lin = moe("lin", [P, 2, CW // 2], F32)
        sig = moe("sig", [P, 2, CW // 2], F32)
        act_out = moe("act_out", [P, 2, CW // 2], F32)
        y_row = moe("y_row", [P, D], F32)
        gate2_row = moe("gate2_row", [P, D], F32)
        x_rows = moe("x_rows", [P, D], F32)
        xT_hi = moe("xT_hi", [P, NK, P], F32R)
        xT_lo = moe("xT_lo", [P, NK, P], F32R)
        bgu_hi = moe("bgu_hi", [P, CW], F32R)
        bgu_lo = moe("bgu_lo", [P, CW], F32R)
        pick = moe("pick", [P, NT, P], F32)
        ids = moe("ids", [P, 8], I32)
        pass_slots = at("pass_slots", [P, P], F32, R0 - 512)
        pick_e = moe("pick_e", [P, P], F32R)
        assert base + m[0] <= nc.sbuf_usable_end, (base + m[0], nc.sbuf_usable_end)
        res_f = at("res_f", [P, NT, D], F32, R2)
        gain_f = at("gain_f", [P, D], F32, R2 + 20 * KB)
        acc = at("acc", [P, NT, D], F32, R2 + 24 * KB)
        junk_f = at("junk_f", [P, D], F32, R2 + 40 * KB)

        bank = [ctx.enter_context(nc.psum_tensor(f"bank{i}", [P, 512], F32)) for i in range(8)]

        y_dram = nc.dram_tensor("y_slots", [SEQ * TOPK + P, D], F32, kind="Internal").ap()
        h2_dram = nc.dram_tensor("h2_rows", [SEQ, D], F32, kind="Internal").ap()
        res_dram = nc.dram_tensor("residual", [NT, P, D], F32, kind="Internal").ap()
        mod_dram = nc.dram_tensor("mod_row_dram", [1, 4 * D], F32, kind="Internal").ap()

        def sem(name):
            return ctx.enter_context(nc.semaphore(name))

        ring_loaded = [sem(f"ring_loaded{i}") for i in range(SLOTS)]
        heads_loaded = sem("heads_loaded")
        (consts, c_in, x_got, mod1_got, small_got, late_got, x_again, bdn_got, bgu_got) = (sem(n) for n in (
            "consts", "c_in", "x_got", "mod1_got", "small_got", "late_got", "x_again", "bdn_got", "bgu_got"))
        dve_chain, act_chain = sem("dve_chain"), sem("act_chain")
        c_sig, rstd_ready = sem("c_sig"), sem("rstd_ready")
        ssq_ready, var_ready, std_ready = sem("ssq_ready"), sem("var_ready"), sem("std_ready")
        ada_done, ada_summed = sem("ada_done"), sem("ada_summed")
        xn_ready, ht_done, ht_read, ht_mod = sem("xn_ready"), sem("ht_done"), sem("ht_read"), sem("ht_mod")
        proj_done, proj_read = sem("proj_done"), sem("proj_read")
        fz_ready, fl_ready, lfb_ready = sem("fz_ready"), sem("fl_ready"), sem("lfb_ready")
        score_done, score_read, max_ready, exp_ready, swa_ready, tri_ready, sb_read, stick_ready = (sem(n) for n in (
            "score_done", "score_read", "max_ready", "exp_ready", "swa_ready", "tri_ready", "sb_read", "stick_ready"))
        lf_ready, head_gain_got = sem("lf_ready"), sem("head_gain_got")
        acc_ready, sum_done, row_ready, row_stored = (sem(n) for n in ("acc_ready", "sum_done", "row_ready", "row_stored"))
        bias_got = [sem(f"bias_got{i}") for i in range(2)]
        pt_done, pt_read, pv_done, o_read_a, o_read_v = (sem(n) for n in ("pt_done", "pt_read", "pv_done", "o_read_a", "o_read_v"))
        hss_ready, hstd_ready, o_norm, ot_done, ot_read = (sem(n) for n in ("hss_ready", "hstd_ready", "o_norm", "ot_done", "ot_read"))
        mix_done, mix_read, x2_ready = sem("mix_done"), sem("mix_read"), sem("x2_ready")
        h2_ready, h2t_done, h2t_read, h2_stored = (sem(n) for n in ("h2_ready", "h2t_done", "h2t_read", "h2_stored"))
        router_done, gate_z, gate_e, gates_ready, mask_ready, rank_done, tables_ready = (sem(n) for n in (
            "router_done", "gate_z", "gate_e", "gates_ready", "mask_ready", "rank_done", "tables_ready"))
        tab_ready, tab_done, last_res_stored = sem("tab_ready"), sem("tab_done"), sem("last_res_stored")
        bdn_ready = sem("bdn_ready")
        gt_done, gt_read, gb_done, resid_ready, res_stored, bgu_ready = (sem(n) for n in (
            "gt_done", "gt_read", "gb_done", "resid_ready", "res_stored", "bgu_ready"))
        split_hi = [sem(f"split_hi{i}") for i in range(USEMS)]
        split_lo = [sem(f"split_lo{i}") for i in range(USEMS)]
        unit_used = [sem(f"unit_used{i}") for i in range(USEMS)]
        pick_step, pick_ready, pick_e_ready = sem("pick_step"), sem("pick_ready"), sem("pick_e_ready")
        ids_done, ids_ready, x_rows_got, xt_done, xt_hi_ready, xt_lo_ready = (sem(n) for n in (
            "ids_done", "ids_ready", "x_rows_got", "xt_done", "xt_hi_ready", "xt_lo_ready"))
        glu_ready = sem("glu_ready")
        lin_ready = [sem(f"lin_ready{i}") for i in range(GU_CHUNKS)]
        sig_ready = sem("sig_ready")
        prod_ready = sem("prod_ready")
        act_ready = [sem(f"act_ready{i}") for i in range(GU_CHUNKS)]
        at_done = [sem(f"at_done{i}") for i in range(GU_CHUNKS)]
        at_hi_ready = [sem(f"at_hi_ready{i}") for i in range(GU_CHUNKS)]
        at_lo_ready = [sem(f"at_lo_ready{i}") for i in range(GU_CHUNKS)]
        y_ready = [sem(f"y_ready{i}") for i in range(DN_CHUNKS)]
        y_stored, y_scaled = sem("y_stored"), sem("y_scaled")
        experts_over = sem("experts_over")
        fin_got, acc_step, fin_ss, fin_var, fin_std, fin_ready = (sem(n) for n in (
            "fin_got", "acc_step", "fin_ss", "fin_var", "fin_std", "fin_ready"))
        y_got = [sem(f"y_got{i}") for i in range(NT)]
        out_stored = [sem(f"out_stored{i}") for i in range(2)]

        ada_v = ada_w[0].rearrange("(k p) n -> p k n", p=P)
        win_v = w_in[0].rearrange("(k p) n -> p k n", p=P)
        wout_v = w_out[0].rearrange("(k p) n -> p k n", p=P)

        PROJ = [(0, "T", t * P, qaT[:, t, :], QSCALE) for t in range(4)]
        PROJ += [
            (1, "T", 0, kaT[:], 1.0),
        ]
        QK_JOBS = len(PROJ)
        PROJ += [
            (1, "V", (P, 2 * P, [0, P, 2 * P, 3 * P]), va[:], 1.0),
            (1, "V", (P, 2 * P, [HD, HD + P, HD + 2 * P]), va_mid[:], 1.0),
        ]
        SWA_JOBS = len(PROJ)
        PROJ += [(1, "V", (256, 512, [2 * n * P, (2 * n + 1) * P]), vs[:, 2 * n:2 * n + 2, :], 1.0) for n in range(NT // 2)]
        PROJ += [(2, "T", j * P, t, s) for j, (t, s) in enumerate((
            (qsT[:, 0, :], QSCALE), (qsT[:, 1, :], QSCALE), (ksT[:, 0, :], 1.0), (ksT[:, 1, :], 1.0)))]
        SB_JOBS = len(PROJ)
        PROJ += [(3, "V", (0, 256 + FOX, [n * P]), (vf[:, n, :], flog[:, n, :]), 1.0) for n in range(NT)]
        GATE_JOBS = len(PROJ)
        qk = [(4, "T", j * P, t, s) for j, (t, s) in enumerate((
            (qfT[:, 0, :], QSCALE), (qfT[:, 1, :], QSCALE), (kfT[:, 0, :], 1.0), (kfT[:, 1, :], 1.0)))]
        cum = [(None, "cum_col", None, cumf_col[:].rearrange("p n h -> p (n h)"), 1.0)]
        cum += [(None, "cum_row", h, cumf_row[:, h, :], 1.0) for h in range(FOX)]
        for k in range(4):
            PROJ += [qk[k], cum[k]]
        PROJ += cum[4:]
        JOBS_OF = {-1: list(range(QK_JOBS, SWA_JOBS))}
        for j in range(SWA_JOBS, len(PROJ)):
            JOBS_OF.setdefault(j - SWA_JOBS, []).append(j)

        def ada_chunk(i):
            return [(0, CW, ada_v[:, :, i * CW:(i + 1) * CW])]

        STREAM = [(ada_chunk(i), ada_done, i + 1) for i in range(4)]
        proj_chunk, ada2_chunk = [], []
        win_parts = [
            [((2 * t + h) * HD, (2 * t + h + 1) * HD, win_v[:, :, C_QA + (4 * h + t) * HD:C_QA + (4 * h + t + 1) * HD])
             for t in range(4) for h in range(2)],
            [(0, 256, win_v[:, :, C_KA:C_KA + 256]), (256, CW, win_v[:, :, C_VS:C_VS + 256])],
            [(0, CW, win_v[:, :, C_QS:C_QS + CW])],
            [(0, 256, win_v[:, :, C_VF:C_VF + 256]), (256, 256 + FOX, win_v[:, :, C_FL:C_FL + FOX])],
            [(0, CW, win_v[:, :, C_QF:C_QF + CW])],
        ]
        for i in ("W0", "W1", "A", "A", "A", "W2", "A", "W3", "A", "A", "W4", "A", "A"):
            if i == "A":
                m = len(ada2_chunk)
                ada2_chunk.append(len(STREAM))
                STREAM.append((ada_chunk(4 + m), acc_ready, m + 1))
            else:
                i = int(i[1])
                proj_chunk.append(len(STREAM))
                STREAM.append((win_parts[i], proj_done, max(j + 1 for j, job in enumerate(PROJ) if job[0] == i)))
        OUT0 = len(STREAM)
        STREAM += [([(0, CW, wout_v[:, :, i * CW:(i + 1) * CW])], mix_done, 2 * NT) for i in range(2)]
        RING0 = SLOTS - 1

        def slot_at(g):
            return g % RING0

        def load_done(g, part):
            return heads_loaded if g == proj_chunk[0] and part < 2 else ring_loaded[slot_at(g)]

        loads = [0] * SLOTS
        ring_value = []
        for g, (parts, _, _) in enumerate(STREAM):
            loads[slot_at(g)] += sum(load_done(g, part) is ring_loaded[slot_at(g)] for part in range(len(parts)))
            ring_value.append(16 * loads[slot_at(g)])
        G0 = len(STREAM)
        EXPERT_SLOTS = [slot_at(G0), slot_at(G0 + 1), slot_at(G0 + 2), SLOTS - 1, slot_at(G0 + 3), slot_at(G0 + 4)]
        EXPERT_FREE = [STREAM[G0 - RING0 + i][1:] for i in range(3)] + [None] + [STREAM[G0 - RING0 + i][1:] for i in (3, 4)]

        def slot_of(ch):
            return EXPERT_SLOTS[ch]

        ADA_STEPS = [(m, k) for m in range(len(ada2_chunk)) for k in range(NK)]
        STEPS_TO = [min(min(3 * (j + 1), 24) + 4 * max(0, j - 9), len(ADA_STEPS)) for j in range(len(PROJ))]

        def ada_chunks_over(j):
            return STEPS_TO[j] // NK if j >= 0 else 0

        load0 = [loads[slot_of(ch)] + 1 for ch in range(CHUNKS)]

        def expert_chunk(e, ch):
            src, n = (w_gu, ch) if ch < GU_CHUNKS else (w_dn, ch - GU_CHUNKS)
            return src[0, bass.ds(e, 1)].rearrange("a (k p) n -> p (a k) n", p=P)[:, :, n * CW:(n + 1) * CW]

        ATT = [("swa", ch, 0) for ch in range(SEQ // HD)]
        SB0 = len(ATT)
        ATT += [("sb", n, h) for n in range(NT) for h in range(SB)]
        FOX0 = len(ATT)
        ATT += [("fox", n, h) for n in range(NT) for h in range(FOX)]
        NU = len(ATT)
        def tile_at(u, later):
            n, r = divmod(u - later - FOX0, FOX)
            return n if r == FOX - 1 and 0 <= n < NT else None

        def heads_bank(n, half):
            return bank[half] if n == NT - 1 else bank[6 + half]

        def mix_bank(n, half):
            return bank[2 + half] if n == NT - 1 else bank[6 + half]

        GB_BANKS = (4, 5, 0, 2, 3, 1)
        GB_FIRST = 2 * (NT - 1)
        PT2 = SB0 + 10
        N_CONST = 19

        def turns(eng, p):
            return [eng.snap(p * UTURNS + (i + 1)) for i in range(UTURNS + 1)]

        def pt_bank(u):
            return bank[2] if u < PT2 else bank[2 + u % 2]

        block = ctx.enter_context(nc.Block())

        @block.sync
        def _(sp):
            for g, (parts, _, _) in enumerate(STREAM):
                s = slot_at(g)
                if g >= RING0:
                    sp.wait_ge(STREAM[g - RING0][1], STREAM[g - RING0][2])
                for part, (a, b, src) in enumerate(parts):
                    sp.dma_start(ring[:, s, :, a:b], src).then_inc(load_done(g, part), 16)
            for ch in range(CHUNKS):
                if EXPERT_FREE[ch] is None:
                    sp.wait_ge(pv_done, NU)
                else:
                    sp.wait_ge(EXPERT_FREE[ch][0], EXPERT_FREE[ch][1])
                sp.dma_start(ring[:, slot_of(ch)], expert_chunk(0, ch)).then_inc(ring_loaded[slot_of(ch)], 16)
            sp.wait_ge(tables_ready, 1)
            n_passes = sp.value_load(passes_i[0:1, 0:1], min_val=NE, max_val=MAX_PASSES)
            with sp.Fori(1, n_passes + 1) as p:
                e_now = sp.value_load(etab_i[0:1, bass.ds(p, 1)], min_val=0, max_val=NE - 1)
                e_before = sp.value_load(etab_i[0:1, bass.ds(p - 1, 1)], min_val=0, max_val=NE - 1)
                done = [sp.snap(p * UTURNS + (i + 1 - UTURNS)) for i in range(UTURNS)]
                before = {v: sp.snap(p * 16 + (v - 1) * 16) for v in sorted(set(load0))}
                with sp.If(e_now != e_before):
                    for ch in range(CHUNKS):
                        src = expert_chunk(e_now, ch)
                        for last in (UPC * ch + POOL_Q, UPC * ch + UPC - 1):
                            sp.wait_ge(split_lo[last % USEMS], done[last // USEMS])
                        sp.dma_start(ring[:, slot_of(ch)], src).then_inc(ring_loaded[slot_of(ch)], 16)
                with sp.Else():
                    for ch in range(CHUNKS):
                        sp.wait_ge(ring_loaded[slot_of(ch)], before[load0[ch]])
                        sp.sem_inc(ring_loaded[slot_of(ch)], 16)
                sp.nop()

        @block.gpsimd
        def _(pool):
            g = nc.gpsimd
            g.memset(ident[:], 0.0).then_inc(consts, 1)
            g.memset(ones[:], 1.0).then_inc(consts, 1)
            g.memset(tri_incl[:], 1.0).then_inc(consts, 1)
            g.memset(tri_strict[:], 1.0).then_inc(consts, 1)
            g.memset(low_strict[:], 1.0).then_inc(consts, 1)
            g.memset(causal_add[:], 0.0).then_inc(consts, 1)
            pool.wait_ge(consts, 6)
            for t, cols, base_v, cm, step, keep, fill in (
                    (ident, P, 0, 1, -1, ALU.not_equal, 1.0),
                    (tri_incl, SEQ, 0, -1, 1, ALU.is_ge, 0.0),
                    (tri_strict, P, -1, -1, 1, ALU.is_ge, 0.0),
                    (low_strict, P, -1, 1, -1, ALU.is_ge, 0.0),
                    (causal_add, P, 0, 1, -1, ALU.is_ge, NEG)):
                g.affine_select(out=t[:, 0:cols], in_=t[:, 0:cols], pattern=[[step, cols]], compare_op=keep,
                                fill=fill, base=base_v, channel_multiplier=cm).then_inc(consts, 1)
            pool.wait_ge(consts, 11)
            for h in range(2):
                g.iota(alibi[64 * h:64 * h + 64, 3, :], [[-1, P]], base=HD, channel_multiplier=1,
                       allow_small_or_imprecise_dtypes=True).then_inc(consts, 1)
                pool.wait_ge(consts, 12 + h)
            g.iota(tok_id[:], [[P, NT]], base=0, channel_multiplier=1,
                   allow_small_or_imprecise_dtypes=True).then_inc(consts, 1)
            g.iota(slot_iota[:], [[1, P]], base=0, channel_multiplier=0,
                   allow_small_or_imprecise_dtypes=True).then_inc(consts, 1)
            for h in range(4):
                pool.wait_ge(consts, 15 + h)
                g.iota(expert_of_row[32 * h:32 * h + 32, :], [[0, P]], base=0, channel_multiplier=1,
                       allow_small_or_imprecise_dtypes=True).then_inc(consts, 1)
            pool.wait_ge(consts, N_CONST)
            for m in range(len(ada2_chunk)):
                if m >= 2:
                    pool.wait_ge(row_ready, m - 1)
                    pool.dma_start(mod_dram[:, (m - 2) * CW:(m - 1) * CW], mod_row[:, m % 2]).then_inc(row_stored, 16)
                    pool.wait_ge(row_stored, 16 * (m - 1))
                pool.dma_start(mod_row[:, m % 2], ada_b[:, (4 + m) * CW:(5 + m) * CW]).then_inc(bias_got[m % 2], 16)
            for m in range(len(ada2_chunk) - 2, len(ada2_chunk)):
                pool.wait_ge(row_ready, m + 1)
                pool.dma_start(mod_dram[:, m * CW:(m + 1) * CW], mod_row[:, m % 2]).then_inc(row_stored, 16)
            g.iota(iota_e[:], [[1, NE]], base=0, channel_multiplier=0,
                   allow_small_or_imprecise_dtypes=True).then_inc(consts, 1)
            g.iota(iota_p[:], [[1, NP_TAB]], base=0, channel_multiplier=0,
                   allow_small_or_imprecise_dtypes=True).then_inc(consts, 1)

            def fetch_tokens():
                g.indirect_dma_start(
                    out=x_rows[:], out_offset=None, in_=h2_dram, in_offset=bass.IndirectOffsetOnAxis(ap=ids[:, 0:1], axis=0),
                    bounds_check=SEQ - 1, oob_is_err=True).then_inc(x_rows_got, 16)

            def split_low(j):
                ch, q = divmod(j, UPC)
                g.tensor_tensor(w_lo[:, j % SPLITS], ring[:, slot_of(ch), KQ * q:KQ * q + KQ, :],
                                w_hi[:, j % SPLITS].bitcast(F32), ALU.subtract).then_inc(split_lo[j % USEMS], 1)

            pool.wait_ge(h2_stored, 16 * NT)
            pool.wait_ge(ids_ready, 1)
            fetch_tokens()
            pool.wait_ge(tables_ready, 1)
            for ch in range(LEAD):
                pool.wait_ge(split_hi[ch * UPC + POOL_Q], 1)
                split_low(ch * UPC + POOL_Q)
            n_passes = pool.value_load(passes_i[0:1, 0:1], min_val=NE, max_val=MAX_PASSES)
            pool.wait_ge(resid_ready, 2 * NT)
            pool.dma_start(gate2_row[:], mod_dram[:, 3 * D:4 * D].broadcast_to([P, D])).then_inc(y_stored, 16)
            pool.wait_ge(y_stored, 16)
            with pool.Fori(0, n_passes) as p:
                p1, p2 = pool.snap(p + 1), pool.snap(p + 2)
                nth = [pool.snap(p * GU_CHUNKS + (ch + 1)) for ch in range(GU_CHUNKS)]
                turn = turns(pool, p)
                scaled = pool.snap(p * DN_CHUNKS + DN_CHUNKS)
                first_slot = pool.value_load(ybase_i[0:1, bass.ds(p, 1)], min_val=0, max_val=SEQ * TOPK)
                y_at = y_dram[bass.ds(first_slot, P), :]
                for step in range(1, CHUNKS + 1):
                    ch = step - 1
                    if ch < GU_CHUNKS:
                        pool.wait_ge(lin_ready[ch], p2 if ch >= 2 else p1)
                        g.tensor_tensor(lin[:, ch % 2], glu[:, ch % 2], lin[:, ch % 2], ALU.mult).then_inc(prod_ready, 1)
                        pool.wait_ge(prod_ready, nth[ch])
                        pool.wait_ge(sig_ready, nth[ch])
                        pool.wait_ge(at_done[(ch + 2) % 4], p1)
                        if ch == 1:
                            pool.wait_ge(xt_done, p1)
                            pool.wait_ge(ids_ready, p2)
                        g.tensor_tensor(act_out[:, ch % 2], lin[:, ch % 2], sig[:, ch % 2], ALU.mult).then_inc(act_ready[ch], 1)
                        if ch == 1:
                            fetch_tokens()
                    j = (step + LEAD - 1) * UPC + POOL_Q
                    pool.wait_ge(split_hi[j % USEMS], turn[j // USEMS])
                    split_low(j % UNITS)
                for hf in range(DN_CHUNKS):
                    pool.wait_ge(y_ready[hf], p2)
                    cs = slice(hf * CW, (hf + 1) * CW)
                    g.tensor_tensor(y_row[:, cs], y_row[:, cs], gate2_row[:, cs], ALU.mult).then_inc(y_scaled, 1)
                pool.wait_ge(y_scaled, scaled)
                pool.dma_start(y_at, y_row[:]).then_inc(y_stored, 16)
            pool.wait_ge(experts_over, 1)
            for n in range(NT):
                for k in range(TOPK):
                    g.indirect_dma_start(
                        out=ring[:, n].rearrange("p a b -> p (a b)")[:, k * D:(k + 1) * D], out_offset=None,
                        in_=y_dram[0:SEQ * TOPK, :], in_offset=bass.IndirectOffsetOnAxis(ap=my_slot_i[:, n, k:k + 1], axis=0),
                        bounds_check=SEQ * TOPK - 1, oob_is_err=True).then_inc(y_got[n], 16)

        @block.scalar
        def _(sc):
            a = nc.scalar
            chain = [0]

            def link(ins):
                chain[0] += 1
                ins.then_inc(act_chain, 1)
                sc.wait_ge(act_chain, chain[0])

            sc.dma_start(c_col[:, 0, :], c.rearrange("a (k p) -> p (a k)", p=P), allow_slow_non_contiguous=True).then_inc(c_in, 16)
            xv = x[0].rearrange("(n p) d -> p n d", p=P)
            sc.dma_start(x_in[:], xv).then_inc(x_got, 16)
            sc.dma_start(mod1_b[:], ada_b[:, 0:2 * D].rearrange("a (k p) -> p (a k)", p=P), allow_slow_non_contiguous=True).then_inc(mod1_got, 16)
            sc.dma_start(gain1[:], norm1_gain.rearrange("a (k p) -> p (a k)", p=P), allow_slow_non_contiguous=True).then_inc(mod1_got, 16)
            sc.dma_start(neg_sink[0:64, :], attn_sinks[:, 0:4].broadcast_to([64, 4])).then_inc(small_got, 16)
            sc.dma_start(neg_sink[64:128, :], attn_sinks[:, 4:8].broadcast_to([64, 4])).then_inc(small_got, 16)
            sc.dma_start(fbias[:], forget_bias.broadcast_to([P, FOX])).then_inc(small_got, 16)
            sc.dma_start(head_gain[:], mix_out_gain.rearrange("a (k p) -> p (a k)", p=P), allow_slow_non_contiguous=True).then_inc(head_gain_got, 16)
            sc.wait_ge(c_in, 16)
            a.activation(c_col[:, 1, :], c_col[:, 0, :], ACT.Sigmoid).then_inc(c_sig, 1)
            sc.wait_ge(consts, N_CONST)
            a.activation(warm[:], ident[:, 0:8], ACT.Sqrt)
            sc.wait_ge(x_got, 16)
            for n in range(NT):
                if n >= 1:
                    sc.wait_ge(ssq_ready, n)
                a.activation(square[:], x_in[:, n], ACT.Square, accum_out=ssq[:, n:n + 1]).then_inc(ssq_ready, 1)
            sc.wait_ge(var_ready, 1)
            a.activation(rstd[:, 0:4], ssq[:, 4:8], ACT.Sqrt).then_inc(std_ready, 1)
            sc.wait_ge(rstd_ready, 1)

            def x_transposed(n):
                for half in range(2):
                    sc.wait_ge(ht_done, 2 * n + half + 1)
                    a.copy(hT[:, 4 * half:4 * half + 4, n * P:(n + 1) * P],
                           bank[4 + 2 * (n % 2) + half][:].rearrange("p (k t) -> p k t", k=4)).then_inc(ht_read, 1)

            for n in range(NT):
                a.activation(x_in[:, n], x_in[:, n], ACT.Copy, scale=rstd[:, n:n + 1]).then_inc(xn_ready, 1)
                if n >= 1:
                    x_transposed(n - 1)
            x_transposed(NT - 1)

            def softplus():
                sc.wait_ge(fz_ready, 1)
                link(a.activation(fwork[:], flog[:], ACT.Abs))
                link(a.activation(fwork[:], fwork[:], ACT.Exp, scale=-1.0))
                a.activation(fwork[:], fwork[:], ACT.Ln, bias=1.0).then_inc(fl_ready, 1)

            def transposed(u):
                kind, n, _ = ATT[u]
                rows = HD if (kind, n) == ("swa", 0) else P
                cols = SEQ if kind == "swa" else (n + 1) * P
                sc.wait_ge(pt_done, u + 1)
                if u >= AB:
                    sc.wait_ge(pv_done, u - AB + 1)
                a.copy(probT[0:rows, u % AB, 0:cols], pt_bank(u)[0:rows, 0:cols]).then_inc(pt_read, 1)

            def outputs(u):
                kind, n, h = ATT[u]
                if kind == "swa" and n % 2 == 1:
                    sc.wait_ge(pv_done, u + 1)
                    a.copy(o[:, n // 2, 0:512], bank[4 + (n // 2) % 2][:]).then_inc(o_read_a, 1)
                if kind == "sb" and h == SB - 1:
                    sc.wait_ge(pv_done, u + 1)
                    a.copy(o[:, n, 768:1024], bank[4 + n % 2][:, 0:256]).then_inc(o_read_a, 1)

            def head_sqrt(n):
                sc.wait_ge(hss_ready, n + 1)
                a.activation(hss[:, n, :], hss[:, n, :], ACT.Sqrt).then_inc(hstd_ready, 1)

            def mixed(n, half):
                sc.wait_ge(mix_done, 2 * n + half + 1)
                a.copy(o[:, n, half * CW:(half + 1) * CW], mix_bank(n, half)[:]).then_inc(mix_read, 1)

            def late_loads():
                sc.wait_ge(score_done, NU)
                sc.wait_ge(row_stored, 16 * len(ada2_chunk))
                sc.dma_start(mod2[:], mod_dram.broadcast_to([P, 4 * D])).then_inc(late_got, 16)
                sc.dma_start(rw[:], router_w[0].rearrange("(k p) e -> p k e", p=P)).then_inc(late_got, 16)
                sc.dma_start(rb[:], router_b.broadcast_to([P, NE])).then_inc(late_got, 16)
                sc.dma_start(gain2[:], norm2_gain.broadcast_to([P, D])).then_inc(late_got, 16)
                sc.dma_start(resid[:], xv).then_inc(x_again, 16)
                sc.dma_start(bdn[:], b_dn[0]).then_inc(bdn_got, 16)
                for n in range(4):
                    sc.dma_start(bgu[32 * n:32 * n + 32, :], b_gu[0, :, n * CW:(n + 1) * CW]).then_inc(bgu_got, 16)

            for u, (kind, n, h) in enumerate(ATT):
                b, cols = u % AB, (n + 1) * P
                if kind == "swa":
                    first = HD if n == 0 else 0
                    sc.wait_ge(max_ready, u + 1)
                    for t in range(4):
                        a.activation(soft[:, b, t * P + first:(t + 1) * P], score[:, b, t * P + first:(t + 1) * P],
                                     ACT.Exp, bias=mrow[:, u, t:t + 1], accum_out=lrow[:, n, t:t + 1]).then_inc(exp_ready, 1)
                    a.activation(sinkd[:, n, :], sinkd[:, n, :], ACT.Exp).then_inc(exp_ready, 1)
                elif kind == "fox":
                    sc.wait_ge(max_ready, SB0 + u - FOX0 + 1)
                    sc.wait_ge(pt_done, u - AB + 1)
                    a.activation(prob[:, b, 0:cols], score[:, b, 0:cols], ACT.Exp, bias=mrow[:, u, 0:1],
                                 accum_out=lfox[:, n, h:h + 1]).then_inc(tri_ready, 1)
                else:
                    i = u - SB0
                    sc.wait_ge(score_done, u + 1)
                    if i < AB:
                        sc.wait_ge(exp_ready, 5 * SB0)
                        sc.wait_ge(swa_ready, u - AB + 1)
                    else:
                        sc.wait_ge(stick_ready, i - AB + 1)
                    a.activation(soft[:, b, 0:cols], bank[u % 2][:, 0:cols], ACT.Sigmoid, scale=-1.0)
                    a.activation(score[:, b, 0:cols], bank[u % 2][:, 0:cols], ACT.Sigmoid).then_inc(sb_read, 1)
                if u >= 1:
                    transposed(u - 1)
                if u >= 3:
                    outputs(u - 3)
                if u == GATE_JOBS - SWA_JOBS:
                    softplus()
                if u == NU - 2:
                    late_loads()
                if tile_at(u, 3) is not None:
                    head_sqrt(tile_at(u, 3))
                for half in range(2):
                    if tile_at(u, 6 + half) is not None:
                        mixed(tile_at(u, 6 + half), half)
            transposed(NU - 1)
            for u in range(NU - 3, NU):
                outputs(u)
            a.activation(warm[:], ident[:, 0:8], ACT.Sqrt)
            head_sqrt(NT - 1)
            def h2_out(n):
                sc.wait_ge(h2_ready, n + 1)
                sc.dma_start(h2_dram[n * P:(n + 1) * P, :], h2_row[:, n]).then_inc(h2_stored, 16)
                for half in range(2):
                    sc.wait_ge(h2t_done, 2 * n + half + 1)
                    a.copy(h2T[:, 4 * half:4 * half + 4, n * P:(n + 1) * P],
                           bank[4 + 2 * (n % 2) + half][:].rearrange("p (k t) -> p k t", k=4)).then_inc(h2t_read, 1)

            def square_sum(n):
                sc.wait_ge(x2_ready, n + 1)
                if n >= 1:
                    sc.wait_ge(ssq_ready, NT + n)
                a.activation(osq[:], resid[:, n], ACT.Square, accum_out=ssq[:, n:n + 1]).then_inc(ssq_ready, 1)
                sc.wait_ge(var_ready, 2 + n)
                a.activation(rstd[:, n:n + 1], ssq[:, 4 + n:5 + n], ACT.Sqrt).then_inc(std_ready, 1)

            for half in range(2):
                mixed(2, half)
            square_sum(0)
            square_sum(1)
            h2_out(0)
            square_sum(2)
            for half in range(2):
                mixed(3, half)
            h2_out(1)
            square_sum(3)
            h2_out(2)
            h2_out(3)
            sc.wait_ge(gate_z, 1)
            a.activation(gate[:], gate[:], ACT.Exp).then_inc(gate_e, 1)
            a.activation(warm[:], ident[:, 0:8], ACT.Sigmoid)

            def split_high(j):
                ch, q = divmod(j, UPC)
                a.copy(w_hi[:, j % SPLITS], ring[:, slot_of(ch), KQ * q:KQ * q + KQ, :]).then_inc(split_hi[j % USEMS], 1)

            def tokens_high(value):
                sc.wait_ge(xt_done, value)
                a.copy(xT_hi[:, 0:4], bank[6][:].rearrange("p (k t) -> p k t", k=4))
                a.copy(xT_hi[:, 4:8], bank[7][:].rearrange("p (k t) -> p k t", k=4)).then_inc(xt_hi_ready, 1)

            def act_high(ch, p1, p2):
                sc.wait_ge(at_done[ch], p2 if ch >= 2 else p1)
                half = bank[4 + ch % 2][:, 0:256].rearrange("p (k t) -> p k t", k=2)
                a.copy(aT_hi[:, 2 * ch:2 * ch + 2], half).then_inc(at_hi_ready[ch], 1)

            for hf in range(DN_CHUNKS):
                sc.sem_inc(y_ready[hf], 1)
            sc.wait_ge(h2_stored, 16 * NT)
            sc.wait_ge(router_done, 1)
            sc.wait_ge(ring_loaded[slot_of(0)], 16 * load0[0])
            for j in range(UPC):
                split_high(j)
            res_v = res_dram.rearrange("n p d -> p n d")
            sc.wait_ge(resid_ready, GB_FIRST - 2)
            sc.dma_start(res_v[:, 0:NT - 2], resid[:, 0:NT - 2]).then_inc(res_stored, 16)
            tokens_high(1)
            sc.wait_ge(resid_ready, GB_FIRST)
            sc.dma_start(res_v[:, NT - 2], resid[:, NT - 2]).then_inc(res_stored, 16)
            sc.wait_ge(bgu_ready, 1)
            sc.wait_ge(ring_loaded[slot_of(1)], 16 * load0[1])
            for j in range(UPC, LEAD * UPC):
                if j == UPC + 2:
                    sc.wait_ge(gb_done, 2 * NT)
                split_high(j)
            sc.wait_ge(resid_ready, 2 * NT)
            sc.dma_start(res_v[:, NT - 1], resid[:, NT - 1]).then_inc(last_res_stored, 16)
            sc.wait_ge(last_res_stored, 16)
            n_passes = sc.value_load(passes_i[0:1, 0:1], min_val=NE, max_val=MAX_PASSES)
            with sc.Fori(0, n_passes) as p:
                p1, p2 = sc.snap(p + 1), sc.snap(p + 2)
                nth = [sc.snap(p * GU_CHUNKS + (ch + 1)) for ch in range(GU_CHUNKS)]
                turn = turns(sc, p)
                stored = sc.snap(p * 16 + 16)
                loaded = {v: sc.snap(p * 16 + 16 * v) for v in sorted(set(load0[LEAD:]) | {v + 1 for v in load0[:LEAD]})}
                for ch in range(1, CHUNKS + 1):
                    cc = (ch + LEAD - 1) % CHUNKS
                    if ch <= GU_CHUNKS:
                        sc.wait_ge(glu_ready, nth[ch - 1])
                        a.activation(sig[:, (ch - 1) % 2], glu[:, (ch - 1) % 2], ACT.Sigmoid,
                                     scale=ALPHA).then_inc(sig_ready, 1)
                    sc.wait_ge(ring_loaded[slot_of(cc)], loaded[load0[cc] + (ch + LEAD - 1) // CHUNKS])
                    for q in range(UPC):
                        j = (ch + LEAD - 1) * UPC + q
                        sc.wait_ge(unit_used[j % USEMS], turn[j // USEMS])
                        split_high(cc * UPC + q)
                        if ch <= GU_CHUNKS and q == 1:
                            act_high(ch - 1, p1, p2)
                        if ch == GU_CHUNKS + 1 and q == 1:
                            tokens_high(p2)
                    if ch == GU_CHUNKS + 1:
                        sc.wait_ge(y_stored, stored)
                    if ch > GU_CHUNKS:
                        hf = ch - GU_CHUNKS - 1
                        used = ch * UPC - 1
                        sc.wait_ge(unit_used[used % USEMS], turn[used // USEMS + 1])
                        a.copy(y_row[:, hf * CW:(hf + 1) * CW], bank[2 + hf][:]).then_inc(y_ready[hf], 1)

            stored = sc.snap(n_passes * 16 + 16)
            split_past = sc.snap(n_passes * UTURNS + 1)
            for j in range(USEMS):
                sc.wait_ge(split_lo[j], split_past)
            sc.wait_ge(y_stored, stored)
            sc.sem_inc(experts_over, 1)
            sc.dma_start(res_f[:], res_dram.rearrange("n p d -> p n d")).then_inc(fin_got, 16)
            sc.dma_start(gain_f[:], final_gain.rearrange("(a d) -> a d", a=1).broadcast_to([P, D])).then_inc(fin_got, 16)
            for n in range(NT):
                sc.wait_ge(acc_step, TOPK * (n + 1))
                if n >= 1:
                    sc.wait_ge(fin_ss, n)
                a.activation(junk_f[:], acc[:, n], ACT.Square, accum_out=ssq[:, n:n + 1]).then_inc(fin_ss, 1)
                sc.wait_ge(fin_var, n + 1)
                a.activation(rstd[:, n:n + 1], ssq[:, 4 + n:5 + n], ACT.Sqrt).then_inc(fin_std, 1)
                sc.wait_ge(fin_ready, n + 1)
                sc.dma_start(out[0, n * P:(n + 1) * P, :], acc[:, n]).then_inc(out_stored[n % 2], 16)
            for i in range(2):
                sc.wait_ge(out_stored[i], 16 * NT // 2)

        @block.vector
        def _(ve):
            v = nc.vector
            chain = [0]

            def link(ins):
                chain[0] += 1
                ins.then_inc(dve_chain, 1)
                ve.wait_ge(dve_chain, chain[0])

            def wide(ap, n, m):
                return ap.unsqueeze(2).broadcast_to([P, n, m])

            ve.wait_ge(c_sig, 1)
            link(v.tensor_tensor(c_col[:, 2, :], c_col[:, 0, :], c_col[:, 1, :], ALU.mult))

            def ada_first(i):
                acc_i = ada_acc[:, i % 2]
                ve.wait_ge(ring_loaded[slot_at(i)], ring_value[i])
                if i >= 2:
                    ve.wait_ge(ada_summed, i - 1)
                link(v.tensor_scalar(acc_i, ring[:, slot_at(i), 0, :], c_col[:, 2, 0:1], None, ALU.mult))
                for k in range(1, NK):
                    ins = v.scalar_tensor_tensor(acc_i, ring[:, slot_at(i), k, :], c_col[:, 2, k:k + 1], acc_i, ALU.mult, ALU.add)
                    if k < NK - 1:
                        link(ins)
                ins.then_inc(ada_done, 1)

            for i in range(2):
                ada_first(i)
            ve.wait_ge(consts, N_CONST)
            link(v.scalar_tensor_tensor(alibi[:, 3, :], alibi[:, 3, :], -1.0, alibi[:, 3, :], ALU.mult, ALU.max))
            for t in range(4):
                for h in range(2):
                    slope = 2.0 ** (-8.0 * (t + 4 * h + 1) / SWA_Q)
                    link(v.tensor_scalar(alibi[64 * h:64 * h + 64, t, :], alibi[64 * h:64 * h + 64, 3, :], -slope, None, ALU.mult))
            ve.wait_ge(ssq_ready, NT)
            v.tensor_scalar(ssq[:, 4:8], ssq[:, 0:4], 1.0 / D, EPS, ALU.mult, ALU.add).then_inc(var_ready, 1)
            ve.wait_ge(std_ready, 1)
            v.reciprocal(rstd[:, 0:4], rstd[:, 0:4]).then_inc(rstd_ready, 1)
            for i in range(2, 4):
                ada_first(i)
            ve.wait_ge(mod1_got, 32)
            ve.wait_ge(ada_summed, 4)
            link(v.tensor_tensor(mod1[:], bank[0][:, 0:2 * NK], mod1_b[:], ALU.add))
            link(v.scalar_tensor_tensor(mod1[:, NK:2 * NK], mod1[:, NK:2 * NK], 1.0, gain1[:], ALU.add, ALU.mult))
            ve.wait_ge(ht_read, 2 * NT)
            for k in range(NK):
                v.tensor_scalar(hT[:, k, :], hT[:, k, :], mod1[:, NK + k:NK + k + 1], mod1[:, k:k + 1], ALU.mult, ALU.add).then_inc(ht_mod, 1)
            ve.wait_ge(small_got, 48)
            link(v.tensor_scalar(neg_sink[:], neg_sink[:], -1.0, None, ALU.mult))
            link(v.memset(stay_from[:], 1.0))

            def ada_step(m, k):
                g, acc_m = ada2_chunk[m], ada_acc[:, m % 2]
                w = ring[:, slot_at(g), k, :]
                if k == 0:
                    ve.wait_ge(ring_loaded[slot_at(g)], ring_value[g])
                    if m >= 2:
                        ve.wait_ge(sum_done, m - 1)
                    link(v.tensor_scalar(acc_m, w, c_col[:, 2, 0:1], None, ALU.mult))
                else:
                    ins = v.scalar_tensor_tensor(acc_m, w, c_col[:, 2, k:k + 1], acc_m, ALU.mult, ALU.add)
                    if k == NK - 1:
                        ins.then_inc(acc_ready, 1)
                    else:
                        link(ins)

            def ada_row(m):
                ve.wait_ge(sum_done, m + 1)
                ve.wait_ge(bias_got[m % 2], 16 * (m // 2 + 1))
                v.tensor_tensor(mod_row[:, m % 2], bank[3][0:1, :], mod_row[:, m % 2], ALU.add).then_inc(row_ready, 1)

            def project(j):
                i, kind, cols, dst, scale = PROJ[j]
                src = bank[6 + j % 2]
                if kind == "cum_col":
                    for h in range(2):
                        repeat_head(h)
                ve.wait_ge(proj_done, j + 1)
                if kind == "cum_row":
                    v.tensor_copy(dst, src[:]).then_inc(proj_read, 1)
                    if cols + 2 < FOX:
                        repeat_head(cols + 2)
                elif kind == "cum_col":
                    v.tensor_copy(dst, src[:, 0:NT * FOX]).then_inc(proj_read, 1)
                elif kind == "T":
                    v.tensor_scalar(dst, src[:], scale, None, ALU.mult).then_inc(proj_read, 1)
                elif i == 3:
                    link(v.tensor_copy(dst[1], src[:, 256:256 + FOX]))
                    v.tensor_copy(dst[0], src[:, 0:256]).then_inc(proj_read, 1)
                else:
                    w = cols[1] - cols[0]
                    m = len(cols[2])
                    v.tensor_copy(dst, src[:, 0:m * w].rearrange("p (m w) -> p m w", m=m)).then_inc(proj_read, 1)
                if j == GATE_JOBS - 1:
                    ve.wait_ge(proj_read, j + 1)
                    v.tensor_tensor(flog[:], flog[:], fbias[:].unsqueeze(1).broadcast_to([P, NT, FOX]), ALU.add).then_inc(fz_ready, 1)
                if j == GATE_JOBS:
                    ve.wait_ge(fl_ready, 1)
                    v.scalar_tensor_tensor(flog[:], flog[:], 0.0, fwork[:], ALU.min, ALU.subtract).then_inc(lf_ready, 1)
                    ve.wait_ge(lf_ready, 1)
                for m in range(ada_chunks_over(j - 3), ada_chunks_over(j - 2)):
                    ada_row(m)
                for m, k in ADA_STEPS[STEPS_TO[j - 1] if j else 0:STEPS_TO[j]]:
                    ada_step(m, k)

            def repeat_head(h):
                v.tensor_copy(lfb[:, h % 2], wide(flog[:, :, h], NT, P)).then_inc(lfb_ready, 1)

            ve.wait_ge(head_gain_got, 16)
            for j in range(QK_JOBS):
                project(j)

            def swa_normalize(u):
                n, b = ATT[u][1], u % AB
                first = HD if n == 0 else 0
                ve.wait_ge(exp_ready, 5 * (u + 1))
                link(v.tensor_tensor(lrow[:, n, :], lrow[:, n, :], sinkd[:, n, :], ALU.add))
                link(v.reciprocal(lrow[:, n, :], lrow[:, n, :]))
                if u >= AB:
                    ve.wait_ge(pt_done, u - AB + 1)
                v.tensor_tensor(prob[:, b].rearrange("p (t j) -> p t j", t=4)[:, :, first:],
                                soft[:, b].rearrange("p (t j) -> p t j", t=4)[:, :, first:],
                                wide(lrow[:, n, :], 4, P - first), ALU.mult).then_inc(swa_ready, 1)

            def head_norm(n):
                ve.wait_ge(hstd_ready, n + 1)
                link(v.reciprocal(hss[:, n, :], hss[:, n, :]))
                on = o[:, n].rearrange("p (h d) -> p h d", h=HEADS)
                v.tensor_tensor(on, on, wide(hss[:, n, :], HEADS, HD), ALU.mult).then_inc(o_norm, 1)

            def heads_transposed(n):
                for half in range(2):
                    ve.wait_ge(ot_done, 2 * n + half + 1)
                    v.tensor_tensor(oT[:, 4 * half:4 * half + 4, n * P:(n + 1) * P],
                                    heads_bank(n, half)[:].rearrange("p (k t) -> p k t", k=4),
                                    wide(head_gain[:, 4 * half:4 * half + 4], 4, P), ALU.mult).then_inc(ot_read, 1)

            def fox_outputs(u):
                kind, n, h = ATT[u]
                if kind == "fox" and h == FOX - 1:
                    ve.wait_ge(pv_done, u + 1)
                    link(v.reciprocal(lfox[:, n, :], lfox[:, n, :]))
                    v.tensor_tensor(o[:, n, 512:768].rearrange("p (h d) -> p h d", h=FOX),
                                    bank[4 + n % 2][:, 0:256].rearrange("p (h d) -> p h d", h=FOX),
                                    wide(lfox[:, n, :], FOX, HD), ALU.mult).then_inc(o_read_v, 1)
                    ve.wait_ge(o_read_a, NT + n + 1)
                    ve.wait_ge(o_read_v, n + 1)
                    link(v.tensor_tensor(osq[:], o[:, n], o[:, n], ALU.mult))
                    link(v.tensor_reduce(hss[:, n, :], osq[:].rearrange("p (h d) -> p h d", h=HEADS), AX.X, ALU.add))
                    v.tensor_scalar(hss[:, n, :], hss[:, n, :], 1.0 / HD, EPS, ALU.mult, ALU.add).then_inc(hss_ready, 1)

            for u, (kind, n, h) in enumerate(ATT):
                b, cols = u % AB, (n + 1) * P
                diag = slice(n * P, (n + 1) * P)
                if kind == "swa":
                    first = HD if n == 0 else 0
                    s4 = score[:, b].rearrange("p (t j) -> p t j", t=4)[:, :, first:]
                    ve.wait_ge(score_done, u + 1)
                    v.tensor_tensor(s4, bank[u % 2][:].rearrange("p (t j) -> p t j", t=4)[:, :, first:],
                                    alibi[:, :, first:], ALU.add).then_inc(score_read, 1)
                    ve.wait_ge(score_read, u + 1)
                    link(v.tensor_reduce(mtmp[:], s4, AX.X, ALU.max))
                    link(v.scalar_tensor_tensor(mrow[:, u, :], mtmp[:], -1.0, neg_sink[:], ALU.mult, ALU.min))
                    v.tensor_tensor(sinkd[:, n, :], mrow[:, u, :], neg_sink[:], ALU.subtract).then_inc(max_ready, 1)
                elif kind == "fox":
                    ve.wait_ge(score_done, u + 1)
                    if u >= FOX0 + AB:
                        ve.wait_ge(tri_ready, u - AB + 1 - FOX0)
                    else:
                        ve.wait_ge(stick_ready, u - AB + 1 - SB0)
                    v.scalar_tensor_tensor(score[:, b, 0:cols], bank[u % 2][:, 0:cols], cumf_col[:, n, h:h + 1],
                                           cumf_row[:, h, 0:cols], ALU.add, ALU.subtract).then_inc(score_read, 1)
                    ve.wait_ge(score_read, u + 1)
                    link(v.tensor_tensor(score[:, b, diag], score[:, b, diag], causal_add[:], ALU.add))
                    link(v.tensor_reduce(mtmp[:, 0:1], score[:, b, 0:cols], AX.X, ALU.max))
                    v.tensor_scalar(mrow[:, u, 0:1], mtmp[:, 0:1], -1.0, None, ALU.mult).then_inc(max_ready, 1)
                else:
                    ve.wait_ge(sb_read, u - SB0 + 1)
                    v.tensor_tensor(score[:, b, diag], score[:, b, diag], low_strict[:], ALU.mult).then_inc(score_read, 1)
                    link(v.tensor_tensor(soft[:, b, diag], soft[:, b, diag], tri_incl[:, 0:P], ALU.max))
                    link(v.tensor_tensor_scan(stay_from[:, 0:cols][:, ::-1], soft[:, b, 0:cols][:, ::-1],
                                              ones[:, 0:1].broadcast_to([P, cols]), 1.0, ALU.mult, ALU.mult))
                    ve.wait_ge(score_read, u + 1)
                    ve.wait_ge(pt_done, u - AB + 1)
                    v.tensor_tensor(prob[:, b, 0:cols], score[:, b, 0:cols], stay_from[:, 1:cols + 1], ALU.mult).then_inc(stick_ready, 1)
                if kind == "swa":
                    swa_normalize(u)
                for j in JOBS_OF.get(u - 1, ()):
                    project(j)
                if u == FOX0 - 1:
                    ve.wait_ge(proj_read, len(PROJ))
                    ve.wait_ge(row_stored, 16 * len(ada2_chunk))
                if u >= 3:
                    fox_outputs(u - 3)
                if tile_at(u, 4) is not None:
                    head_norm(tile_at(u, 4))
                if tile_at(u, 5) is not None:
                    heads_transposed(tile_at(u, 5))
            heads_transposed(2)
            for u in range(NU - 3, NU):
                fox_outputs(u)
            head_norm(NT - 1)
            heads_transposed(NT - 1)
            ve.wait_ge(late_got, 64)
            gate1, shift2, scale2, gate2 = (mod2[:, i * D:(i + 1) * D] for i in range(4))
            link(v.scalar_tensor_tensor(scale2, scale2, 1.0, gain2[:], ALU.add, ALU.mult))
            ve.wait_ge(x_again, 16)
            for n in range(NT):
                ve.wait_ge(mix_read, 2 * n + 2)
                link(v.tensor_tensor(o[:, n], o[:, n], gate1, ALU.mult))
                v.tensor_tensor(resid[:, n], resid[:, n], o[:, n], ALU.add).then_inc(x2_ready, 1)
                ve.wait_ge(ssq_ready, NT + n + 1)
                v.tensor_scalar(ssq[:, 4 + n:5 + n], ssq[:, n:n + 1], 1.0 / D, EPS, ALU.mult, ALU.add).then_inc(var_ready, 1)
                ve.wait_ge(std_ready, 2 + n)
                link(v.reciprocal(rstd[:, n:n + 1], rstd[:, n:n + 1]))
                link(v.scalar_tensor_tensor(h2_row[:, n], resid[:, n], rstd[:, n:n + 1], scale2, ALU.mult, ALU.mult))
                v.tensor_tensor(h2_row[:, n], h2_row[:, n], shift2, ALU.add).then_inc(h2_ready, 1)
            def make_pick(dest_col):
                v.tensor_tensor(pick[:], pass_slots[:].unsqueeze(1).broadcast_to([P, NT, P]),
                                dest_col.broadcast_to([P, NT, P]), ALU.is_equal).then_inc(pick_ready, 1)

            def token_ids(value):
                ve.wait_ge(ids_done, value)
                v.tensor_copy(ids[:, 0:1], bank[7][:, 0:1]).then_inc(ids_ready, 1)

            ve.wait_ge(bgu_got, 64)
            odd = bgu[:].rearrange("p (f two) -> p f two", two=2)[:, :, 1]
            link(v.tensor_scalar(odd, odd, 1.0, None, ALU.add))
            link(v.tensor_copy(bgu_hi[:], bgu[:]))
            v.tensor_tensor(bgu_lo[:], bgu[:], bgu_hi[:].bitcast(F32), ALU.subtract).then_inc(bgu_ready, 1)
            ve.wait_ge(bdn_got, 16)
            v.tensor_tensor(bdn[:], bdn[:], gate2[0:NE, :], ALU.mult).then_inc(bdn_ready, 1)
            ve.wait_ge(router_done, 1)
            link(v.tensor_tensor(logit[:], bank[0][:, 0:NT * NE].rearrange("p (n e) -> p n e", n=NT),
                                 rb[:].unsqueeze(1).broadcast_to([P, NT, NE]), ALU.add))
            for n in range(NT):
                link(v.max(top[:, n, :], logit[:, n, :]))
                link(v.max_index(topi[:, n, :], top[:, n, :], logit[:, n, :]))
            link(v.tensor_copy(topf[:], topi[:, :, 0:TOPK]))
            v.tensor_tensor(gate[:], top[:, :, 0:TOPK], top[:, :, 0:1].broadcast_to([P, NT, TOPK]), ALU.subtract).then_inc(gate_z, 1)
            ve.wait_ge(consts, N_CONST + 2)
            for n in range(NT):
                link(v.tensor_tensor(hot[:, n], iota_e[:].unsqueeze(1).broadcast_to([P, TOPK, NE]), wide(topf[:, n, :], TOPK, NE), ALU.is_equal))
            v.tensor_reduce(mask[:], hot[:].rearrange("p n k e -> p n e k"), AX.X, ALU.add).then_inc(mask_ready, 1)
            ve.wait_ge(gate_e, 1)
            link(v.tensor_reduce(gsum[:, :, 0], gate[:], AX.X, ALU.add))
            link(v.reciprocal(gsum[:, :, 1], gsum[:, :, 0]))
            link(v.tensor_tensor(gate[:], gate[:], gsum[:, :, 1:2].broadcast_to([P, NT, TOPK]), ALU.mult))
            for n in range(NT):
                link(v.tensor_tensor(hot_w[:, n], hot[:, n], wide(gate[:, n, :], TOPK, NE), ALU.mult))
            v.tensor_reduce(gates_e[:], hot_w[:].rearrange("p n k e -> p n e k"), AX.X, ALU.add).then_inc(gates_ready, 1)
            ve.wait_ge(rank_done, 1)
            link(v.tensor_copy(count[:], bank[2][:, 0:NE]))
            ve.wait_ge(gt_done, 1)
            v.tensor_copy(gT[:].rearrange("e n t -> e (n t)"), bank[3][0:NE, :]).then_inc(gt_read, 1)
            link(v.tensor_scalar(nblk[:, 0, :], count[:], float(P), 1.0, ALU.is_gt, ALU.add))
            link(v.scalar_tensor_tensor(nblk[:, 1, :], count[:], 2.0 * P, nblk[:, 0, :], ALU.is_gt, ALU.add))
            link(v.scalar_tensor_tensor(nblk[:, 0, :], count[:], 3.0 * P, nblk[:, 1, :], ALU.is_gt, ALU.add))
            link(v.tensor_tensor_scan(pend[:], ones[:, 0:NE], nblk[:, 0, :], 0.0, ALU.mult, ALU.add))
            link(v.tensor_tensor_scan(start[:], ones[:, 0:NE], count[:], 0.0, ALU.mult, ALU.add))
            link(v.tensor_tensor(start[:], start[:], count[:], ALU.subtract))
            link(v.tensor_tensor(dest[:], start[:].unsqueeze(1).broadcast_to([P, NT, NE]),
                                 bank[1][:, 0:NT * NE].rearrange("p (n e) -> p n e", n=NT), ALU.add))
            link(v.scalar_tensor_tensor(dest[:], dest[:], 1.0, mask[:], ALU.add, ALU.mult))
            link(v.tensor_scalar(dest[:], dest[:], -1.0, None, ALU.add))
            link(v.tensor_copy(pass_slots[:], slot_iota[:]))
            make_pick(dest[:, :, 0:1])
            link(v.tensor_scalar(over[:, 0, :], pend[:], tok_id[:, 0:1], None, ALU.is_le))
            link(v.scalar_tensor_tensor(from_pass[:], nblk[:, 0, :], -float(P), count[:], ALU.mult, ALU.add))
            link(v.tensor_tensor(over[:, 1, :], over[:, 0, :], from_pass[:], ALU.mult))
            link(v.tensor_reduce(pass_col[:], over[:], AX.X, ALU.add))
            v.tensor_tensor(pass_diag[:], ident[:, 0:NP_TAB].unsqueeze(1).broadcast_to([P, 2, NP_TAB]),
                            wide(pass_col[:], 2, NP_TAB), ALU.mult).then_inc(tab_ready, 1)
            for n in range(NT):
                link(v.tensor_tensor(hot_w[:, n], hot[:, n], dest[:, n, :].unsqueeze(1).broadcast_to([P, TOPK, NE]), ALU.mult))
            token_ids(1)
            link(v.tensor_reduce(my_slot[:], hot_w[:], AX.X, ALU.add))
            link(v.tensor_copy(my_slot_i[:], my_slot[:]))
            ve.wait_ge(tab_done, 1)
            link(v.tensor_scalar(etab[:], bank[6][:, 0:NP_TAB], float(NE - 1), None, ALU.min))
            link(v.tensor_copy(etab_i[:], etab[:]))
            link(v.scalar_tensor_tensor(ybase[:], iota_p[:], float(P), bank[6][:, NP_TAB:2 * NP_TAB], ALU.mult, ALU.add))
            link(v.tensor_copy(ybase_i[:], ybase[:]))
            v.tensor_copy(passes_i[:], pend[:, NE - 1:NE]).then_inc(tables_ready, 1)

            def add_gated_bias(i):
                n, half = divmod(i, 2)
                cs = slice(half * CW, (half + 1) * CW)
                ve.wait_ge(gb_done, i + 1)
                v.tensor_tensor(resid[:, n, cs], resid[:, n, cs], bank[GB_BANKS[i % 6]][:], ALU.add).then_inc(resid_ready, 1)

            def split_low(j):
                ch, q = divmod(j, UPC)
                v.tensor_tensor(w_lo[:, j % SPLITS], ring[:, slot_of(ch), KQ * q:KQ * q + KQ, :],
                                w_hi[:, j % SPLITS].bitcast(F32), ALU.subtract).then_inc(split_lo[j % USEMS], 1)

            def tokens_low(value):
                ve.wait_ge(xt_hi_ready, value)
                for half in range(2):
                    low = v.tensor_tensor(xT_lo[:, 4 * half:4 * half + 4], bank[6 + half][:].rearrange("p (k t) -> p k t", k=4),
                                          xT_hi[:, 4 * half:4 * half + 4].bitcast(F32), ALU.subtract)
                low.then_inc(xt_lo_ready, 1)

            def act_low(ch, p1):
                ve.wait_ge(at_hi_ready[ch], p1)
                half = bank[4 + ch % 2][:, 0:256].rearrange("p (k t) -> p k t", k=2)
                v.tensor_tensor(aT_lo[:, 2 * ch:2 * ch + 2], half, aT_hi[:, 2 * ch:2 * ch + 2].bitcast(F32),
                                ALU.subtract).then_inc(at_lo_ready[ch], 1)

            ve.wait_ge(tables_ready, 1)
            n_passes = ve.value_load(passes_i[0:1, 0:1], min_val=NE, max_val=MAX_PASSES)
            ve.sem_inc(lin_ready[2], 1)
            ve.sem_inc(lin_ready[3], 1)
            ve.sem_inc(act_ready[2], 1)
            ve.sem_inc(act_ready[3], 1)
            for i in range(USEMS):
                ve.sem_inc(unit_used[i], 1)
            for ch in (2, 3):
                ve.sem_inc(at_lo_ready[ch], 1)
            v.tensor_scalar(pick_e[:], expert_of_row[:], 0.0, None, ALU.is_equal).then_inc(pick_e_ready, 1)
            for i in range(GB_FIRST - 1):
                add_gated_bias(i)
            for ch in range(LEAD):
                for q in range(UPC):
                    if q != POOL_Q:
                        ve.wait_ge(split_hi[ch * UPC + q], 1)
                        split_low(ch * UPC + q)
                if ch == 0:
                    add_gated_bias(GB_FIRST - 1)
                    tokens_low(1)
                    for i in range(GB_FIRST, 2 * NT):
                        add_gated_bias(i)
            ve.wait_ge(res_stored, 32)
            with ve.Fori(0, n_passes) as p:
                p1, p2 = ve.snap(p + 1), ve.snap(p + 2)
                turn = turns(ve, p)
                e_next = ve.value_load(etab_i[0:1, bass.ds(p1, 1)], min_val=0, max_val=NE - 1)
                ve.wait_ge(ids_done, p1)
                v.tensor_scalar(pass_slots[:], slot_iota[:], ybase[:, bass.ds(p1, 1)], None, ALU.add).then_inc(pick_step, 1)
                ve.wait_ge(pick_step, p1)
                make_pick(dest[:, :, bass.ds(e_next, 1)])
                for ch in range(1, CHUNKS + 1):
                    cc = (ch + LEAD - 1) % CHUNKS
                    if ch <= GU_CHUNKS:
                        c0, used = ch - 1, ch * UPC - 1
                        gu = bank[c0 % 2][:].rearrange("p (f two) -> p f two", two=2)
                        ve.wait_ge(unit_used[used % USEMS], turn[used // USEMS + 1])
                        ve.wait_ge(act_ready[(c0 + 2) % 4], p1)
                        v.tensor_scalar(glu[:, c0 % 2], gu[:, :, 0], LIMIT, None, ALU.min).then_inc(glu_ready, 1)
                        v.tensor_scalar(lin[:, c0 % 2], gu[:, :, 1], 1.0 - LIMIT, 1.0 + LIMIT, ALU.max, ALU.min).then_inc(lin_ready[c0], 1)
                    for q in range(UPC):
                        j = (ch + LEAD - 1) * UPC + q
                        if q != POOL_Q:
                            ve.wait_ge(split_hi[j % USEMS], turn[j // USEMS])
                            split_low(cc * UPC + q)
                        if ch <= GU_CHUNKS and q == 1:
                            act_low(ch - 1, p1)
                        if ch == GU_CHUNKS + 1 and q == 1:
                            tokens_low(p2)
                    if ch == 1:
                        token_ids(p2)
                    if ch == GU_CHUNKS:
                        v.tensor_scalar(pick_e[:], expert_of_row[:], etab[:, bass.ds(p1, 1)], None, ALU.is_equal).then_inc(pick_e_ready, 1)
            ve.wait_ge(fin_got, 32)

            def final_norm(n):
                ve.wait_ge(fin_ss, n + 1)
                v.tensor_scalar(ssq[:, 4 + n:5 + n], ssq[:, n:n + 1], 1.0 / D, EPS, ALU.mult, ALU.add).then_inc(fin_var, 1)
                ve.wait_ge(fin_std, n + 1)
                link(v.reciprocal(rstd[:, n:n + 1], rstd[:, n:n + 1]))
                v.scalar_tensor_tensor(acc[:, n], acc[:, n], rstd[:, n:n + 1], gain_f[:], ALU.mult, ALU.mult).then_inc(fin_ready, 1)

            for n in range(NT):
                rows = ring[:, n].rearrange("p a b -> p (a b)")
                ve.wait_ge(y_got[n], 16 * TOPK)
                for k in range(TOPK):
                    if k:
                        ve.wait_ge(acc_step, TOPK * n + k)
                    v.scalar_tensor_tensor(acc[:, n], rows[:, k * D:(k + 1) * D], gate[:, n, k:k + 1],
                                           acc[:, n] if k else res_f[:, n], ALU.mult, ALU.add).then_inc(acc_step, 1)
                if n >= 1:
                    final_norm(n - 1)
            final_norm(NT - 1)

        @block.tensor
        def _(pe):
            t = nc.tensor

            def ada_columns(i):
                pe.wait_ge(ada_done, i + 1)
                for q in range(CW // P):
                    col = i * (CW // P) + q
                    mm = t.matmul(bank[0][:, col:col + 1], ada_acc[:, i % 2, q * P:(q + 1) * P], ones[:, 0:1], start=True, stop=True)
                mm.then_inc(ada_summed, 1)

            pe.wait_ge(consts, N_CONST)
            for i in range(2):
                ada_columns(i)
            for n in range(NT):
                pe.wait_ge(xn_ready, n + 1)
                for half in range(2):
                    if n >= 2:
                        pe.wait_ge(ht_read, 2 * (n - 2) + half + 1)
                    for k in range(4):
                        kk = 4 * half + k
                        mm = t.transpose(bank[4 + 2 * (n % 2) + half][:, k * P:(k + 1) * P], x_in[:, n, kk * P:(kk + 1) * P], ident[:])
                    mm.then_inc(ht_done, 1)
            for i in range(2, 4):
                ada_columns(i)
            pe.wait_ge(ht_read, 2 * NT)

            def ada_sum(m):
                pe.wait_ge(acc_ready, m + 1)
                if m >= 1:
                    pe.wait_ge(row_ready, m)
                t.matmul(bank[3][0:1, :], ones[:, 0:1], ada_acc[:, m % 2], start=True, stop=True).then_inc(sum_done, 1)

            def project(j):
                i, kind, cols, dst, scale = PROJ[j]
                if j >= 2:
                    pe.wait_ge(proj_read, j - 1)
                dstb = bank[6 + j % 2]
                if kind == "cum_col":
                    pe.wait_ge(lf_ready, 1)
                    for n in range(NT):
                        for m in range(n + 1):
                            mm = t.matmul(dstb[:, n * FOX:(n + 1) * FOX], ones[:] if m < n else tri_incl[:, 0:P], flog[:, m, :],
                                          start=(m == 0), stop=(m == n))
                elif kind == "cum_row":
                    pe.wait_ge(lfb_ready, cols + 1)
                    for m in range(NT):
                        mm = t.matmul(dstb[:, m * P:SEQ], lfb[:, cols % 2, m, :], tri_incl[:, 0:SEQ - m * P],
                                      start=(m == 0), stop=(m == NT - 1))
                else:
                    g = proj_chunk[i]
                    if j == 0:
                        pe.wait_ge(heads_loaded, 32)
                    else:
                        pe.wait_ge(ring_loaded[slot_at(g)], ring_value[g])
                    w = ring[:, slot_at(g)]
                    if kind == "V":
                        c0, c1, tokens = cols
                        for m, t0 in enumerate(tokens):
                            for k in range(NK):
                                mm = t.matmul(dstb[:, m * (c1 - c0):(m + 1) * (c1 - c0)], hT[:, k, t0:t0 + P], w[:, k, c0:c1],
                                              start=(k == 0), stop=(k == NK - 1))
                    else:
                        for k in range(NK):
                            if j == 0:
                                pe.wait_ge(ht_mod, k + 1)
                            mm = t.matmul(dstb[:], w[:, k, cols:cols + P], hT[:, k, :], start=(k == 0), stop=(k == NK - 1))
                mm.then_inc(proj_done, 1)
                for m in range(ada_chunks_over(j - 2), ada_chunks_over(j - 1)):
                    ada_sum(m)

            for j in range(QK_JOBS):
                project(j)

            def scores(u):
                kind, n, h = ATT[u]
                if u >= 2:
                    if ATT[u - 2][0] == "sb":
                        pe.wait_ge(sb_read, u - 2 - SB0 + 1)
                    else:
                        pe.wait_ge(score_read, u - 2 + 1)
                if u in (0, SB0, FOX0):
                    pe.wait_ge(proj_read, {0: QK_JOBS, SB0: SB_JOBS, FOX0: len(PROJ)}[u])
                dst = bank[u % 2]
                if kind == "swa":
                    k0 = 0 if n == 0 else (n - 1) * HD
                    for tt in range(4):
                        for a in range(2):
                            half = slice(HD * a, HD * a + HD)
                            first = HD if n == 0 else 0
                            mm = t.matmul(dst[half, tt * P + first:(tt + 1) * P], qaT[half, tt, n * HD:(n + 1) * HD],
                                          kaT[half, k0:(n + 1) * HD], start=True, stop=True)
                else:
                    q, kk = (qfT, kfT) if kind == "fox" else (qsT, ksT)
                    half = slice(HD * (h % 2), HD * (h % 2) + HD)
                    mm = t.matmul(dst[:, 0:(n + 1) * P], q[half, h // 2, n * P:(n + 1) * P], kk[half, h // 2, 0:(n + 1) * P],
                                  start=True, stop=True)
                mm.then_inc(score_done, 1)

            def transpose_probs(u):
                kind, n, h = ATT[u]
                if kind == "swa":
                    pe.wait_ge(swa_ready, u + 1)
                elif kind == "fox":
                    pe.wait_ge(tri_ready, u - FOX0 + 1)
                else:
                    pe.wait_ge(stick_ready, u - SB0 + 1)
                if 1 <= u <= PT2:
                    pe.wait_ge(pt_read, u)
                elif u >= 2:
                    pe.wait_ge(pt_read, u - 1)
                if u == PT2:
                    pe.wait_ge(row_ready, len(ada2_chunk))
                dst, b = pt_bank(u), u % AB
                if kind == "swa" and n == 0:
                    for tt in range(4):
                        mm = t.transpose(dst[0:HD, tt * P:(tt + 1) * P], prob[:, b, tt * P + HD:(tt + 1) * P], ident[:])
                else:
                    for m in range(4 if kind == "swa" else n + 1):
                        mm = t.transpose(dst[:, m * P:(m + 1) * P], prob[:, b, m * P:(m + 1) * P], ident[:])
                mm.then_inc(pt_done, 1)

            def times_values(u):
                kind, n, h = ATT[u]
                b = u % AB
                pe.wait_ge(pt_read, u + 1)
                if u == 0:
                    pe.wait_ge(proj_read, SWA_JOBS)
                if kind == "swa":
                    dst = bank[4 + (n // 2) % 2]
                    if n % 2 == 0 and n >= 4:
                        pe.wait_ge(o_read_a, n // 2 - 1)
                    rows = HD if n == 0 else P
                    vals = va[:, n // 2] if n % 2 else (va[0:HD, 0] if n == 0 else va_mid[:, n // 2 - 1])
                    q0 = (n % 2) * HD
                    for tt in range(4):
                        for a in range(2):
                            head = tt + 4 * a
                            mm = t.matmul(dst[q0:q0 + HD, head * HD:(head + 1) * HD],
                                          probT[0:rows, b, tt * P + a * HD:tt * P + (a + 1) * HD],
                                          vals[0:rows, a * HD:(a + 1) * HD], start=True, stop=True)
                else:
                    dst = bank[4 + n % 2]
                    vals = vf if kind == "fox" else vs
                    if h == 0:
                        if kind == "sb":
                            pe.wait_ge(o_read_a, 3 + n if n < 2 else NT + n - 1)
                        elif n < 2:
                            pe.wait_ge(o_read_a, NT + 3 + n)
                        else:
                            pe.wait_ge(o_read_v, n - 1)
                    for m in range(n + 1):
                        mm = t.matmul(dst[:, h * HD:(h + 1) * HD], probT[:, b, m * P:(m + 1) * P], vals[:, m, h * HD:(h + 1) * HD],
                                      start=(m == 0), stop=(m == n))
                mm.then_inc(pv_done, 1)

            def transpose_heads(n):
                pe.wait_ge(o_norm, n + 1)
                if n == NT - 1:
                    pe.wait_ge(score_read, NU)
                elif n >= 1:
                    pe.wait_ge(mix_read, 2 * n)
                for half in range(2):
                    for k in range(4):
                        kk = 4 * half + k
                        mm = t.transpose(heads_bank(n, half)[:, k * P:(k + 1) * P], o[:, n, kk * P:(kk + 1) * P], ident[:])
                    mm.then_inc(ot_done, 1)

            def mix(n, half):
                g = OUT0 + half
                pe.wait_ge(ring_loaded[slot_at(g)], ring_value[g])
                pe.wait_ge(ot_read, 2 * n + 2)
                if n == NT - 1:
                    pe.wait_ge(pt_read, NU)
                for k in range(NK):
                    mm = t.matmul(mix_bank(n, half)[:], oT[:, k, n * P:(n + 1) * P], ring[:, slot_at(g), k, :],
                                  start=(k == 0), stop=(k == NK - 1))
                mm.then_inc(mix_done, 1)

            scores(0)
            scores(1)
            for j in JOBS_OF[-1]:
                project(j)
            for u in range(NU):
                transpose_probs(u)
                if u + 2 < NU:
                    scores(u + 2)
                if u >= 1:
                    times_values(u - 1)
                for j in JOBS_OF.get(u, ()):
                    project(j)
                if tile_at(u, 4) is not None:
                    transpose_heads(tile_at(u, 4))
                for half in range(2):
                    if tile_at(u, 5 + half) is not None:
                        mix(tile_at(u, 5 + half), half)
            times_values(NU - 1)
            def h2_transposed(n):
                pe.wait_ge(h2_ready, n + 1)
                if n == 0:
                    pe.wait_ge(o_read_v, NT)
                if n == 1:
                    pe.wait_ge(mix_read, 6)
                for half in range(2):
                    if n >= 2:
                        pe.wait_ge(h2t_read, 2 * (n - 2) + half + 1)
                    for k in range(4):
                        kk = 4 * half + k
                        mm = t.transpose(bank[4 + 2 * (n % 2) + half][:, k * P:(k + 1) * P], h2_row[:, n, kk * P:(kk + 1) * P], ident[:])
                    mm.then_inc(h2t_done, 1)

            def router(n):
                pe.wait_ge(h2t_read, 2 * n + 2)
                for k in range(NK):
                    mm = t.matmul(bank[0][:, n * NE:(n + 1) * NE], h2T[:, k, n * P:(n + 1) * P], rw[:, k, :],
                                  start=(k == 0), stop=(k == NK - 1))
                if n == NT - 1:
                    mm.then_inc(router_done, 1)

            mix(2, 0)
            transpose_heads(3)
            mix(2, 1)
            mix(3, 0)
            h2_transposed(0)
            router(0)
            mix(3, 1)
            for n in range(1, NT):
                h2_transposed(n)
                router(n)
            pe.wait_ge(mask_ready, 1)
            for n in range(NT):
                for j in range(n + 1):
                    if n == 0:
                        pe.wait_ge(mix_read, 2 * NT)
                    t.matmul(bank[1][:, n * NE:(n + 1) * NE], ones[:] if j < n else tri_strict[:], mask[:, j, :],
                             start=(j == 0), stop=(j == n))
            for n in range(NT):
                mm = t.matmul(bank[2][:, 0:NE], ones[:], mask[:, n, :], start=(n == 0), stop=(n == NT - 1))
            mm.then_inc(rank_done, 1)
            pe.wait_ge(gates_ready, 1)
            for n in range(NT):
                mm = t.transpose(bank[3][0:NE, n * P:(n + 1) * P], gates_e[:, n, :], ident[:])
            mm.then_inc(gt_done, 1)

            def token_numbers():
                for n in range(NT):
                    mm = t.matmul(bank[7][:, 0:1], pick[:, n, :], tok_id[:, n:n + 1], start=(n == 0), stop=(n == NT - 1))
                mm.then_inc(ids_done, 1)

            def transpose_tokens():
                for k in range(NK):
                    mm = t.transpose(bank[6 + k // 4][:, (k % 4) * P:(k % 4 + 1) * P], x_rows[:, k * P:(k + 1) * P], ident[:])
                mm.then_inc(xt_done, 1)

            def unit(dst, hi, lo, j, turn, first):
                pe.wait_ge(split_lo[j % USEMS], turn[j // USEMS])
                ch, q = divmod(j, UPC)
                for kk in range(KQ):
                    k = KQ * q + kk
                    w1, w2 = w_hi[:, j % SPLITS, kk, :], w_lo[:, j % SPLITS, kk, :]
                    t.matmul(dst[:], hi[:, k, :], w1, start=(first and k == 0), stop=False)
                    t.matmul(dst[:], hi[:, k, :], w2, start=False, stop=False)
                    mm = t.matmul(dst[:], lo[:, k, :], w1, start=False, stop=(k == NK - 1))
                mm.then_inc(unit_used[j % USEMS], 1)

            def act_transpose(ch, value):
                pe.wait_ge(act_ready[ch], value)
                pe.wait_ge(at_lo_ready[(ch + 2) % 4], pass_value[0])
                for m in range(2):
                    mm = t.transpose(bank[4 + ch % 2][:, m * P:(m + 1) * P],
                                     act_out[:, ch % 2, m * P:(m + 1) * P], ident[:])
                mm.then_inc(at_done[ch], 1)

            for ch in (2, 3):
                pe.sem_inc(at_done[ch], 1)
            def gated_bias(i):
                n, half = divmod(i, 2)
                if i >= 6:
                    pe.wait_ge(resid_ready, i - 5)
                t.matmul(bank[GB_BANKS[i % 6]][:], gT[:, n, :], bdn[:, half * CW:(half + 1) * CW], start=True, stop=True).then_inc(gb_done, 1)

            pe.wait_ge(gt_read, 1)
            pe.wait_ge(bdn_ready, 1)
            for i in range(3):
                gated_bias(i)
            pe.wait_ge(pick_ready, 1)
            token_numbers()
            pe.wait_ge(tab_ready, 1)
            t.matmul(bank[6][:, 0:2 * NP_TAB], ones[:], pass_diag[:].rearrange("p a b -> p (a b)"),
                     start=True, stop=True).then_inc(tab_done, 1)
            for i in range(3, 5):
                gated_bias(i)
            pe.wait_ge(ids_ready, 1)
            pe.wait_ge(tables_ready, 1)
            pe.wait_ge(x_rows_got, 16)
            transpose_tokens()
            pe.wait_ge(bgu_ready, 1)
            for i in range(5, 2 * NT):
                gated_bias(i)
            pe.wait_ge(resid_ready, GB_FIRST)
            n_passes = pe.value_load(passes_i[0:1, 0:1], min_val=NE, max_val=MAX_PASSES)
            pass_value = [None]
            with pe.Fori(0, n_passes) as p:
                p1, p2 = pe.snap(p + 1), pe.snap(p + 2)
                turn = turns(pe, p)
                pass_value[0] = p1
                rows_got = pe.snap(p * 16 + 32)
                pe.wait_ge(xt_lo_ready, p1)
                pe.wait_ge(pick_e_ready, p1)
                for ch in range(GU_CHUNKS):
                    dst = bank[ch % 2]
                    rows = slice(NE * ch, NE * ch + NE)
                    pe.wait_ge(lin_ready[(ch + 2) % 4], p1)
                    t.matmul(dst[:], pick_e[rows, :], bgu_hi[rows, :], start=True, stop=False)
                    t.matmul(dst[:], pick_e[rows, :], bgu_lo[rows, :], start=False, stop=False)
                    for q in range(UPC):
                        unit(dst, xT_hi, xT_lo, ch * UPC + q, turn, False)
                        if ch >= 1 and q == 1:
                            act_transpose(ch - 1, p2 if ch - 1 >= 2 else p1)
                        if ch == 0 and q == 3:
                            pe.wait_ge(pick_ready, p2)
                            token_numbers()
                for hf in range(DN_CHUNKS):
                    pe.wait_ge(y_ready[hf], p1)
                    for q in range(UPC):
                        if hf == 0:
                            pe.wait_ge(at_lo_ready[q], p2 if q >= 2 else p1)
                        unit(bank[2 + hf], aT_hi, aT_lo, (GU_CHUNKS + hf) * UPC + q, turn, True)
                        if hf == 0 and q == 1:
                            act_transpose(3, p2)
                        if hf == 0 and q == 3:
                            pe.wait_ge(ids_ready, p2)
                            pe.wait_ge(x_rows_got, rows_got)
                            transpose_tokens()


_INS = ['x', 'c', 'norm1_gain', 'norm2_gain', 'ada_w', 'ada_b', 'w_in', 'attn_sinks', 'forget_bias', 'mix_out_gain',
        'w_out', 'router_w', 'router_b', 'expert_w_gate_up', 'expert_b_gate_up', 'expert_w_down', 'expert_b_down',
        'final_gain']


def kernel(**inputs):
    import numpy as _np
    import concourse.bacc as _bacc
    from concourse import mybir as _mybir
    from concourse.bass_utils import run_bass_kernel_spmd as _run

    nc = _bacc.Bacc("TRN2", target_bir_lowering=False, num_devices=1)
    arrays, args = {}, []
    for name in _INS:
        a = _np.ascontiguousarray(inputs[name])
        arrays[f"in_{name}_dram"] = a
        args.append(nc.dram_tensor(f"in_{name}_dram", a.shape, _mybir.dt.from_np(a.dtype), kind="ExternalInput").ap())
    args.append(nc.dram_tensor("out_0_dram", (1, SEQ, D), _mybir.dt.float32, kind="ExternalOutput").ap())
    build_program(nc, *args)
    r = _run(nc, [arrays], core_ids=[0])
    return r.results[0]["out_0_dram"]
```
